# Optimizing a Trainium2 kernel written in Bass

```python
import math
import jax, jax.numpy as jnp
from jax import lax
import numpy as np

D_MODEL = 1024
BATCH = 1
SEQ = 512
DEPTH = 1

N_META = 16
RWKV_HEAD_DIM = 64
RWKV_HEADS = D_MODEL // RWKV_HEAD_DIM
RWKV_WIDTH = RWKV_HEADS * RWKV_HEAD_DIM
DECAY_LORA = 64
AAA_LORA = 64
GATE_LORA = 160
RWKV_LN_EPS = 64e-5
DIFF_HEAD_DIM = 64
DIFF_HEADS = D_MODEL // (2 * DIFF_HEAD_DIM)
DIFF_V_DIM = 2 * DIFF_HEAD_DIM
DIFF_QK_WIDTH = 2 * DIFF_HEADS * DIFF_HEAD_DIM
DIFF_V_WIDTH = DIFF_HEADS * DIFF_V_DIM
ROPE_THETA = 500000.0
ROPE_DIM = DIFF_HEAD_DIM // 4
D_FF = 4 * D_MODEL
N_BRANCH = 2
Q_BLOCK = 128
NORM_EPS = 1e-5
SUBLN_EPS = 1e-5

RWKV_COLS = 3 * RWKV_WIDTH + DECAY_LORA + AAA_LORA + GATE_LORA
DIFF_COLS = 2 * DIFF_QK_WIDTH + DIFF_V_WIDTH
GATE_COLS = N_BRANCH * D_MODEL
N_IN = RWKV_COLS + DIFF_COLS + GATE_COLS


def rms_norm(x, w, eps=NORM_EPS):
    xf = x.astype(jnp.float32)
    y = xf * lax.rsqrt(jnp.mean(xf * xf, axis=-1, keepdims=True) + eps)
    return (y * w.astype(jnp.float32)).astype(x.dtype)

def token_shift(p):
    return jnp.pad(p, ((0, 0), (1, 0), (0, 0)))[:, :-1]

def rwkv7_mix(p, mu, w0, w2, a0, a2, g2, k_k, k_a, r_k, ln_w, ln_b):
    f32 = jnp.float32
    bsz, seqlen, _ = p.shape
    p = p + (token_shift(p) - p) * mu
    c1 = RWKV_WIDTH
    c2 = 2 * RWKV_WIDTH
    c3 = 3 * RWKV_WIDTH
    c4 = c3 + DECAY_LORA
    c5 = c4 + AAA_LORA
    r, k, v, wd, ad, gd = jnp.split(p, [c1, c2, c3, c4, c5], axis=-1)
    w = -jax.nn.softplus(-(w0 + jnp.tanh(wd) @ w2).astype(f32)) - 0.5
    decay = jnp.exp(-jnp.exp(w))
    a = jax.nn.sigmoid((a0 + ad @ a2).astype(f32))
    g = jax.nn.sigmoid(gd) @ g2

    def heads(t):
        return t.astype(f32).reshape(bsz, seqlen, RWKV_HEADS, RWKV_HEAD_DIM)

    kk = heads(k * k_k)
    kk = kk / jnp.maximum(jnp.sqrt(jnp.sum(kk * kk, axis=-1, keepdims=True)), 1e-12)
    k = k.astype(f32) * (1.0 + (a - 1.0) * k_a.astype(f32))
    r_h, k_h, v_h, a_h, w_h = heads(r), heads(k), heads(v), heads(a), heads(decay)

    def tm(t):
        return jnp.moveaxis(t, 1, 0)

    xs = (tm(r_h), tm(w_h), tm(k_h), tm(v_h), tm(-kk), tm(kk * a_h))

    def step(S, inp):
        rt, wt, kt, vt, at, bt = inp
        sa = jnp.einsum('bhvk,bhk->bhv', S, at)
        S = S * wt[:, :, None, :] + sa[..., None] * bt[:, :, None, :] + vt[..., None] * kt[:, :, None, :]
        y = jnp.einsum('bhvk,bhk->bhv', S, rt)
        return S, y

    S0 = jnp.zeros((bsz, RWKV_HEADS, RWKV_HEAD_DIM, RWKV_HEAD_DIM), f32)
    _, ys = lax.scan(step, S0, xs)
    y = jnp.moveaxis(ys, 0, 1)
    mean = jnp.mean(y, axis=-1, keepdims=True)
    var = jnp.mean(jnp.square(y - mean), axis=-1, keepdims=True)
    y = (y - mean) * lax.rsqrt(var + RWKV_LN_EPS)
    y = y.reshape(bsz, seqlen, RWKV_WIDTH) * ln_w.astype(f32) + ln_b.astype(f32)
    bonus = jnp.sum(r_h * k_h * r_k.astype(f32), axis=-1, keepdims=True) * v_h
    y = y + bonus.reshape(bsz, seqlen, RWKV_WIDTH)
    return (y * g.astype(f32)).astype(p.dtype)

def partial_rope(x, pos):
    half = ROPE_DIM // 2
    inv = ROPE_THETA ** (-jnp.arange(0, ROPE_DIM, 2, dtype=jnp.float32) / ROPE_DIM)
    ang = pos.astype(jnp.float32)[:, None] * inv[None, :]
    cos = jnp.cos(ang)[None, :, None, :]
    sin = jnp.sin(ang)[None, :, None, :]
    x1 = x[..., :half].astype(jnp.float32)
    x2 = x[..., half:ROPE_DIM].astype(jnp.float32)
    rot = jnp.concatenate([x1 * cos - x2 * sin, x2 * cos + x1 * sin], axis=-1).astype(x.dtype)
    return jnp.concatenate([rot, x[..., ROPE_DIM:]], axis=-1)

def diff_attention(p, lq1, lk1, lq2, lk2, subln_w, lambda_init):
    f32 = jnp.float32
    bsz, seqlen, _ = p.shape
    q, k, v = jnp.split(p, [DIFF_QK_WIDTH, 2 * DIFF_QK_WIDTH], axis=-1)
    pos = jnp.arange(seqlen)
    q = partial_rope(q.reshape(bsz, seqlen, 2 * DIFF_HEADS, DIFF_HEAD_DIM), pos)
    k = partial_rope(k.reshape(bsz, seqlen, 2 * DIFF_HEADS, DIFF_HEAD_DIM), pos)
    q = jnp.transpose(q, (0, 2, 1, 3)) * (DIFF_HEAD_DIM ** -0.5)
    k = jnp.transpose(k, (0, 2, 1, 3))
    v = jnp.transpose(v.reshape(bsz, seqlen, DIFF_HEADS, DIFF_V_DIM), (0, 2, 1, 3))
    lam = (jnp.exp(jnp.sum(lq1.astype(f32) * lk1.astype(f32)))
           - jnp.exp(jnp.sum(lq2.astype(f32) * lk2.astype(f32))) + lambda_init)
    neg = jnp.finfo(f32).min

    def attend(qb, qpos):
        nq = qb.shape[2]
        s = jnp.einsum('bhqd,bhkd->bhqk', qb, k, preferred_element_type=f32)
        s = jnp.where(pos[None, :] <= qpos[:, None], s, neg)
        pr = jax.nn.softmax(s, axis=-1).reshape(bsz, DIFF_HEADS, 2, nq, seqlen)
        attn_w = pr[:, :, 0] - lam * pr[:, :, 1]
        return jnp.einsum('bhqk,bhkd->bhqd', attn_w.astype(v.dtype), v)

    meta_out = attend(q[:, :, :N_META], pos[:N_META])
    n_blk = (seqlen - N_META) // Q_BLOCK

    def blk(i):
        start = N_META + i * Q_BLOCK
        qb = lax.dynamic_slice_in_dim(q, start, Q_BLOCK, axis=2)
        return attend(qb, start + jnp.arange(Q_BLOCK))

    outs = lax.map(blk, jnp.arange(n_blk))
    outs = jnp.transpose(outs, (1, 2, 0, 3, 4)).reshape(bsz, DIFF_HEADS, n_blk * Q_BLOCK, DIFF_V_DIM)
    o = jnp.concatenate([meta_out, outs], axis=2)
    o = rms_norm(o, subln_w, SUBLN_EPS) * (1.0 - lambda_init)
    return jnp.transpose(o, (0, 2, 1, 3)).reshape(bsz, seqlen, DIFF_V_WIDTH)

def first_inputs(seed: int = 0) -> dict:
    key = jax.random.key(seed)
    ks = jax.random.split(key, 32)
    f32 = jnp.float32

    def nrm(k, shape, scale):
        return jax.random.normal(k, shape, f32) * scale

    L = DEPTH
    return {
        "x": nrm(ks[0], (BATCH, SEQ, D_MODEL), 1.0),
        "meta_tokens": nrm(ks[1], (N_META, D_MODEL), 1.0),
        "norm_mix_w": 1.0 + nrm(ks[2], (L, D_MODEL), 0.02),
        "w_in": nrm(ks[3], (L, D_MODEL, N_IN), D_MODEL ** -0.5),
        "rwkv_mu": jax.random.uniform(ks[4], (L, RWKV_COLS), f32, 0.0, 1.0),
        "rwkv_w0": jax.random.uniform(ks[5], (L, RWKV_WIDTH), f32, -6.5, -1.5),
        "rwkv_w2": nrm(ks[6], (L, DECAY_LORA, RWKV_WIDTH), 0.1 * DECAY_LORA ** -0.5),
        "rwkv_a0": nrm(ks[7], (L, RWKV_WIDTH), 0.01),
        "rwkv_a2": nrm(ks[8], (L, AAA_LORA, RWKV_WIDTH), 0.5 * AAA_LORA ** -0.5),
        "rwkv_g2": nrm(ks[9], (L, GATE_LORA, RWKV_WIDTH), GATE_LORA ** -0.5),
        "rwkv_k_k": 0.85 + nrm(ks[10], (L, RWKV_WIDTH), 0.02),
        "rwkv_k_a": 1.0 + nrm(ks[11], (L, RWKV_WIDTH), 0.02),
        "rwkv_r_k": nrm(ks[12], (L, RWKV_HEADS, RWKV_HEAD_DIM), 0.1),
        "rwkv_ln_w": 1.0 + nrm(ks[13], (L, RWKV_WIDTH), 0.02),
        "rwkv_ln_b": nrm(ks[14], (L, RWKV_WIDTH), 0.01),
        "rwkv_w_o": nrm(ks[15], (L, RWKV_WIDTH, D_MODEL), RWKV_WIDTH ** -0.5),
        "diff_lq1": nrm(ks[16], (L, DIFF_HEAD_DIM), 0.1),
        "diff_lk1": nrm(ks[17], (L, DIFF_HEAD_DIM), 0.1),
        "diff_lq2": nrm(ks[18], (L, DIFF_HEAD_DIM), 0.1),
        "diff_lk2": nrm(ks[19], (L, DIFF_HEAD_DIM), 0.1),
        "diff_subln_w": 1.0 + nrm(ks[20], (L, DIFF_V_DIM), 0.02),
        "diff_w_o": nrm(ks[21], (L, DIFF_V_WIDTH, D_MODEL), DIFF_V_WIDTH ** -0.5),
        "w_out": nrm(ks[22], (L, D_MODEL, D_MODEL), D_MODEL ** -0.5),
        "norm_mlp_w": 1.0 + nrm(ks[23], (L, D_MODEL), 0.02),
        "mlp_w1": nrm(ks[24], (L, D_MODEL, D_FF), D_MODEL ** -0.5),
        "mlp_w2": nrm(ks[25], (L, D_FF, D_MODEL), D_FF ** -0.5),
        "final_norm_w": 1.0 + nrm(ks[26], (D_MODEL,), 0.02),
    }

def first_block(x, meta_tokens, norm_mix_w, w_in, rwkv_mu, rwkv_w0, rwkv_w2, rwkv_a0, rwkv_a2, rwkv_g2,
              rwkv_k_k, rwkv_k_a, rwkv_r_k, rwkv_ln_w, rwkv_ln_b, rwkv_w_o, diff_lq1, diff_lk1, diff_lq2,
              diff_lk2, diff_subln_w, diff_w_o, w_out, norm_mlp_w, mlp_w1, mlp_w2, final_norm_w):
    bsz = x.shape[0]
    meta = jnp.broadcast_to(meta_tokens[None].astype(x.dtype), (bsz, N_META, D_MODEL))
    h_res = jnp.concatenate([meta, x], axis=1)
    seqlen = h_res.shape[1]
    for layer in range(DEPTH):
        lambda_init = 0.8 - 0.6 * math.exp(-0.3 * layer)
        h = rms_norm(h_res, norm_mix_w[layer])
        proj = h @ w_in[layer]
        p_rwkv, p_diff, p_gate = jnp.split(proj, [RWKV_COLS, RWKV_COLS + DIFF_COLS], axis=-1)
        o_rwkv = rwkv7_mix(p_rwkv, rwkv_mu[layer], rwkv_w0[layer], rwkv_w2[layer], rwkv_a0[layer],
                           rwkv_a2[layer], rwkv_g2[layer], rwkv_k_k[layer], rwkv_k_a[layer],
                           rwkv_r_k[layer], rwkv_ln_w[layer], rwkv_ln_b[layer]) @ rwkv_w_o[layer]
        o_diff = diff_attention(p_diff, diff_lq1[layer], diff_lk1[layer], diff_lq2[layer],
                                diff_lk2[layer], diff_subln_w[layer], lambda_init) @ diff_w_o[layer]
        gates = jax.nn.sigmoid(p_gate).reshape(bsz, seqlen, N_BRANCH, D_MODEL)
        merged = gates[:, :, 0] * o_rwkv + gates[:, :, 1] * o_diff
        h_res = h_res + merged @ w_out[layer]
        h = rms_norm(h_res, norm_mlp_w[layer])
        h_res = h_res + jnp.square(jax.nn.relu(h @ mlp_w1[layer])) @ mlp_w2[layer]
    out = rms_norm(h_res, final_norm_w)
    return out[:, N_META:]


_first_inputs = first_inputs


def first_inputs(seed=0):
    import zlib

    import numpy as np

    out = dict(_first_inputs(seed))
    spreads = {}
    factors = {'norm_mix_w': 2.945,
     'rwkv_w2': 37.606,
     'rwkv_a0': 8.0,
     'rwkv_k_k': 64.0,
     'rwkv_k_a': 8.0,
     'rwkv_ln_w': 64.0,
     'rwkv_ln_b': 64.0,
     'diff_subln_w': 56.6,
     'norm_mlp_w': 12.365,
     'final_norm_w': 7.86}
    for name, (base, spread) in spreads.items():
        noise = np.random.default_rng([zlib.crc32(name.encode()), seed]).standard_normal(out[name].shape)
        drawn = base * np.exp(spread * noise) if base else spread * noise
        out[name] = __import__('jax').numpy.asarray(drawn.astype(out[name].dtype))
    for name, factor in factors.items():
        out[name] = (out[name] * factor).astype(out[name].dtype)
    return out


_narrow_inputs = first_inputs


def first_inputs(seed=0):

    out = dict(_narrow_inputs(seed))
    wider = {'rwkv_k_k': 10.01,
     'rwkv_k_a': 3.04,
     'rwkv_ln_w': 4.31,
     'rwkv_ln_b': 9.11,
     'diff_subln_w': 4.1,
     'final_norm_w': 3.15}
    for name, times in wider.items():
        mean = out[name].mean()
        out[name] = (mean + times * (out[name] - mean)).astype(out[name].dtype)
    return out


CHUNK = 64
GDN_HEADS = 4
GDN_DK = 128
GDN_DV = 128
CONV_W = 4
GLA_HEADS = 4
GLA_DK = 64
GLA_DV = 128
GLA_RANK = 16
GLA_NORMALIZER = 16.0
HGRN_HEADS = 4
HGRN_EXPAND = 128
HGRN_DV = 128
LB_FLOOR = 1e-30
N_EXPERTS = 16
N_GROUPS = 4
EXPERTS_PER_GROUP = N_EXPERTS // N_GROUPS
TOP_K = 2
D_FF_2 = 256
ALPHA = (2.0 * DEPTH) ** 0.25
BETA = (8.0 * DEPTH) ** -0.25
LN_EPS = 1e-5
RMS_EPS = 1e-6

GDN_QK = GDN_HEADS * GDN_DK
GDN_V = GDN_HEADS * GDN_DV
GLA_QK = GLA_HEADS * GLA_DK
GLA_V = GLA_HEADS * GLA_DV
HGRN_QK = HGRN_HEADS * HGRN_EXPAND
HGRN_V = HGRN_HEADS * HGRN_DV
SPLIT_SIZES = (GDN_QK, GDN_QK, GDN_V, GDN_HEADS, GDN_HEADS, GDN_V,
               GLA_QK, GLA_QK, GLA_V, GLA_RANK, GLA_V,
               HGRN_QK, HGRN_QK, HGRN_V, HGRN_V,
               D_MODEL, D_MODEL, D_MODEL)
SPLIT_POINTS = tuple(int(v) for v in np.cumsum(SPLIT_SIZES)[:-1])
IN_WIDTH = int(sum(SPLIT_SIZES))


def layer_norm(x, g, b):
    xf = x.astype(jnp.float32)
    mu = xf.mean(-1, keepdims=True)
    var = jnp.square(xf - mu).mean(-1, keepdims=True)
    return ((xf - mu) * lax.rsqrt(var + LN_EPS) * g.astype(jnp.float32) + b.astype(jnp.float32)).astype(x.dtype)

def l2_normalize(x):
    return x * lax.rsqrt(jnp.sum(jnp.square(x), -1, keepdims=True) + RMS_EPS)

def to_chunks(x, n_heads):
    b, s, w = x.shape
    return x.reshape(b, s // CHUNK, CHUNK, n_heads, w // n_heads).transpose(0, 3, 1, 2, 4)

def scalar_to_chunks(x):
    b, s, h = x.shape
    return x.reshape(b, s // CHUNK, CHUNK, h).transpose(0, 3, 1, 2)

def from_chunks(o):
    b, h, n, c, d = o.shape
    return o.transpose(0, 2, 3, 1, 4).reshape(b, n * c, h * d)

def masked_exp(diff, mask):
    return jnp.where(mask, jnp.exp(jnp.where(mask, diff, 0.0)), 0.0)

def gated_rms_heads(o, gate, g, n_heads):
    b, s, w = o.shape
    oh = o.astype(jnp.float32).reshape(b, s, n_heads, w // n_heads)
    oh = oh * lax.rsqrt(jnp.mean(jnp.square(oh), -1, keepdims=True) + RMS_EPS) * g.astype(jnp.float32)
    gh = jax.nn.silu(gate.astype(jnp.float32)).reshape(b, s, n_heads, w // n_heads)
    return (oh * gh).reshape(b, s, w).astype(gate.dtype)

def causal_short_conv(x, w):
    s = x.shape[1]
    xp = jnp.pad(x, ((0, 0), (CONV_W - 1, 0), (0, 0)))
    y = xp[:, 0:s] * w[0]
    for k in range(1, CONV_W):
        y = y + xp[:, k:k + s] * w[k]
    return y

def gated_delta_rule(q, k, v, beta, log_decay):
    c = q.shape[-2]
    incl = jnp.tril(jnp.ones((c, c), bool))
    strict = jnp.tril(jnp.ones((c, c), bool), -1)
    cum = jnp.cumsum(log_decay, axis=-1)
    diff = cum[..., :, None] - cum[..., None, :]
    decay_mat = masked_exp(diff, incl)
    kk = jnp.einsum('bhnid,bhnjd->bhnij', k, k)
    a_strict = jnp.where(strict, beta[..., :, None] * kk * decay_mat, 0.0)
    t_mat = a_strict + jnp.eye(c, dtype=q.dtype)
    rhs = jnp.concatenate([v * beta[..., None], k * (beta * jnp.exp(cum))[..., None]], -1)
    sol = lax.linalg.triangular_solve(t_mat, rhs, left_side=True, lower=True, unit_diagonal=True)
    u, w = sol[..., :v.shape[-1]], sol[..., v.shape[-1]:]
    attn = jnp.einsum('bhnid,bhnjd->bhnij', q, k) * decay_mat
    q_inter = q * jnp.exp(cum)[..., None]
    k_state = k * jnp.exp(cum[..., -1:] - cum)[..., None]
    last = jnp.exp(cum[..., -1])

    def step(s, xs):
        qi_c, u_c, w_c, attn_c, ks_c, last_c = xs
        v_new = u_c - jnp.einsum('bhcd,bhde->bhce', w_c, s)
        o = jnp.einsum('bhcd,bhde->bhce', qi_c, s) + jnp.einsum('bhij,bhje->bhie', attn_c, v_new)
        s = s * last_c[..., None, None] + jnp.einsum('bhcd,bhce->bhde', ks_c, v_new)
        return s, o

    b, h = q.shape[0], q.shape[1]
    s0 = jnp.zeros((b, h, q.shape[-1], v.shape[-1]), q.dtype)
    xs = tuple(jnp.moveaxis(a, 2, 0) for a in (q_inter, u, w, attn, k_state, last))
    _, o = lax.scan(step, s0, xs)
    return jnp.moveaxis(o, 0, 2)

def diag_decay_linear_attention(q, k, v, log_a):
    c = q.shape[-2]
    incl = jnp.tril(jnp.ones((c, c), bool))[:, :, None]
    cum = jnp.cumsum(log_a, axis=-2)
    last = cum[..., -1:, :]
    q_inter = q * jnp.exp(cum)
    k_state = k * jnp.exp(last - cum)
    decay_last = jnp.exp(last[..., 0, :])

    def step(s, xs):
        q_c, k_c, v_c, cum_c, qi_c, ks_c, dl_c = xs
        diff = cum_c[..., :, None, :] - cum_c[..., None, :, :]
        rel = masked_exp(diff, incl)
        attn = jnp.einsum('bhid,bhjd,bhijd->bhij', q_c, k_c, rel)
        o = jnp.einsum('bhij,bhje->bhie', attn, v_c) + jnp.einsum('bhid,bhde->bhie', qi_c, s)
        s = s * dl_c[..., :, None] + jnp.einsum('bhjd,bhje->bhde', ks_c, v_c)
        return s, o

    b, h = q.shape[0], q.shape[1]
    s0 = jnp.zeros((b, h, q.shape[-1], v.shape[-1]), q.dtype)
    xs = tuple(jnp.moveaxis(a, 2, 0) for a in (q, k, v, cum, q_inter, k_state, decay_last))
    _, o = lax.scan(step, s0, xs)
    return jnp.moveaxis(o, 0, 2)

def hybrid_mixer(x, lower_bound, w_in, gdn_conv, gdn_a_log, gdn_dt_bias, gdn_norm, gla_w2, gla_b2,
                 gla_norm, hgrn_norm, w_br_a, w_br_b, w_br_c, w_out):
    f32 = jnp.float32
    proj = x @ w_in
    (a_q, a_k, a_v, a_beta, a_dt, a_g, b_q, b_k, b_v, b_lr, b_g,
     c_q, c_f, c_i, c_g, m_a, m_b, m_c) = jnp.split(proj, SPLIT_POINTS, axis=-1)

    qkv = jax.nn.silu(causal_short_conv(jnp.concatenate([a_q, a_k, a_v], -1), gdn_conv)).astype(f32)
    aq, ak, av = jnp.split(qkv, (GDN_QK, 2 * GDN_QK), axis=-1)
    aq = l2_normalize(to_chunks(aq, GDN_HEADS)) * (GDN_DK ** -0.5)
    ak = l2_normalize(to_chunks(ak, GDN_HEADS))
    av = to_chunks(av, GDN_HEADS)
    beta = scalar_to_chunks(jax.nn.sigmoid(a_beta.astype(f32)))
    g_a = -jnp.exp(gdn_a_log.astype(f32)) * jax.nn.softplus(a_dt.astype(f32) + gdn_dt_bias.astype(f32))
    o_a = from_chunks(gated_delta_rule(aq, ak, av, beta, scalar_to_chunks(g_a)))
    o_a = gated_rms_heads(o_a, a_g, gdn_norm, GDN_HEADS)

    bq = to_chunks(b_q.astype(f32), GLA_HEADS) * (GLA_DK ** -0.5)
    bk = to_chunks(b_k.astype(f32), GLA_HEADS)
    bv = to_chunks(b_v.astype(f32), GLA_HEADS)
    log_alpha = jax.nn.log_sigmoid((b_lr @ gla_w2 + gla_b2).astype(f32)) / GLA_NORMALIZER
    o_b = from_chunks(diag_decay_linear_attention(bq, bk, bv, to_chunks(log_alpha, GLA_HEADS)))
    o_b = gated_rms_heads(o_b, b_g, gla_norm, GLA_HEADS)

    cf = c_f.astype(f32)
    lb = lower_bound.astype(f32)
    log_lb = jnp.log(jnp.maximum(lb, LB_FLOOR))
    log_f = jnp.logaddexp(log_lb, jnp.log1p(-lb) + jax.nn.log_sigmoid(cf))
    k_c = (1.0 - lb) * jax.nn.sigmoid(-cf)
    cq = to_chunks(jax.nn.silu(c_q.astype(f32)), HGRN_HEADS) * (HGRN_EXPAND ** -0.5)
    o_c = from_chunks(diag_decay_linear_attention(cq, to_chunks(k_c, HGRN_HEADS),
                                                  to_chunks(c_i.astype(f32), HGRN_HEADS),
                                                  to_chunks(log_f, HGRN_HEADS)))
    o_c = gated_rms_heads(o_c, c_g, hgrn_norm, HGRN_HEADS)

    y = (jax.nn.sigmoid(m_a) * (o_a @ w_br_a) + jax.nn.sigmoid(m_b) * (o_b @ w_br_b)
         + jax.nn.sigmoid(m_c) * (o_c @ w_br_c))
    return y @ w_out

def grouped_moe(x, w_router, router_bias, w_gate, w_up, w_down):
    b, s, d = x.shape
    t = x.reshape(b * s, d)
    scores = jax.nn.sigmoid((t @ w_router).astype(jnp.float32))
    sel = (scores + router_bias.astype(jnp.float32)).reshape(-1, N_GROUPS, EXPERTS_PER_GROUP)
    group_score = lax.top_k(sel, TOP_K)[0].sum(-1)
    g_idx = jnp.argmax(group_score, axis=-1)
    in_group = jnp.take_along_axis(sel, g_idx[:, None, None], axis=1)[:, 0]
    _, e_local = lax.top_k(in_group, TOP_K)
    e_idx = g_idx[:, None] * EXPERTS_PER_GROUP + e_local
    w_sel = jnp.take_along_axis(scores, e_idx, axis=1)
    w_sel = w_sel / jnp.sum(w_sel, -1, keepdims=True)
    combine = jnp.sum(jax.nn.one_hot(e_idx, N_EXPERTS, dtype=jnp.float32) * w_sel[..., None], 1)
    h = jax.nn.silu(jnp.einsum('td,edf->tef', t, w_gate)) * jnp.einsum('td,edf->tef', t, w_up)
    y = jnp.einsum('tef,efd->td', h * combine[..., None].astype(h.dtype), w_down)
    return y.reshape(b, s, d)

def second_inputs(seed: int = 0) -> dict:
    key = jax.random.key(seed)
    ks = jax.random.split(key, 26)
    f32 = jnp.float32

    def nrm(k, shape, scale):
        return jax.random.normal(k, shape, f32) * scale

    dt = jnp.exp(jax.random.uniform(ks[6], (DEPTH, GDN_HEADS), f32, math.log(1e-3), math.log(1e-1)))
    return {
        "x": nrm(ks[0], (BATCH, SEQ, D_MODEL), 1.0),
        "ln0_g": 1.0 + nrm(ks[1], (D_MODEL,), 0.02),
        "ln0_b": nrm(ks[2], (D_MODEL,), 0.02),
        "w_in": nrm(ks[3], (DEPTH, D_MODEL, IN_WIDTH), D_MODEL ** -0.5),
        "gdn_conv": nrm(ks[4], (DEPTH, CONV_W, 2 * GDN_QK + GDN_V), CONV_W ** -0.5),
        "gdn_a_log": jnp.log(jax.random.uniform(ks[5], (DEPTH, GDN_HEADS), f32, 1.0, 16.0)),
        "gdn_dt_bias": dt + jnp.log(-jnp.expm1(-dt)),
        "gdn_norm": 1.0 + nrm(ks[7], (DEPTH, GDN_DV), 0.02),
        "gla_w2": nrm(ks[8], (DEPTH, GLA_RANK, GLA_QK), GLA_RANK ** -0.5),
        "gla_b2": nrm(ks[9], (DEPTH, GLA_QK), 0.1),
        "gla_norm": 1.0 + nrm(ks[10], (DEPTH, GLA_DV), 0.02),
        "hgrn_lb_logits": nrm(ks[11], (DEPTH, HGRN_QK), 0.5),
        "hgrn_norm": 1.0 + nrm(ks[12], (DEPTH, HGRN_DV), 0.02),
        "w_br_a": nrm(ks[13], (DEPTH, GDN_V, D_MODEL), BETA * GDN_V ** -0.5),
        "w_br_b": nrm(ks[14], (DEPTH, GLA_V, D_MODEL), BETA * GLA_V ** -0.5),
        "w_br_c": nrm(ks[15], (DEPTH, HGRN_V, D_MODEL), BETA * HGRN_V ** -0.5),
        "w_out": nrm(ks[16], (DEPTH, D_MODEL, D_MODEL), BETA * D_MODEL ** -0.5),
        "ln1_g": 1.0 + nrm(ks[17], (DEPTH, D_MODEL), 0.02),
        "ln1_b": nrm(ks[18], (DEPTH, D_MODEL), 0.02),
        "w_router": nrm(ks[19], (D_MODEL, N_EXPERTS), D_MODEL ** -0.5),
        "router_bias": nrm(ks[20], (N_EXPERTS,), 0.01),
        "w_gate": nrm(ks[21], (DEPTH, N_EXPERTS, D_MODEL, D_FF_2), BETA * D_MODEL ** -0.5),
        "w_up": nrm(ks[22], (DEPTH, N_EXPERTS, D_MODEL, D_FF_2), BETA * D_MODEL ** -0.5),
        "w_down": nrm(ks[23], (DEPTH, N_EXPERTS, D_FF_2, D_MODEL), BETA * D_FF_2 ** -0.5),
        "ln2_g": 1.0 + nrm(ks[24], (DEPTH, D_MODEL), 0.02),
        "ln2_b": nrm(ks[25], (DEPTH, D_MODEL), 0.02),
    }

def second_block(x, ln0_g, ln0_b, w_in, gdn_conv, gdn_a_log, gdn_dt_bias, gdn_norm, gla_w2, gla_b2,
              gla_norm, hgrn_lb_logits, hgrn_norm, w_br_a, w_br_b, w_br_c, w_out, ln1_g, ln1_b,
              w_router, router_bias, w_gate, w_up, w_down, ln2_g, ln2_b):
    p = jax.nn.softmax(hgrn_lb_logits.astype(jnp.float32), axis=0)
    lower_bounds = jnp.clip(jnp.cumsum(p, axis=0) - p[0], 0.0, 1.0)
    h = layer_norm(x, ln0_g, ln0_b)
    for l in range(DEPTH):
        mix = hybrid_mixer(h, lower_bounds[l], w_in[l], gdn_conv[l], gdn_a_log[l], gdn_dt_bias[l],
                           gdn_norm[l], gla_w2[l], gla_b2[l], gla_norm[l], hgrn_norm[l],
                           w_br_a[l], w_br_b[l], w_br_c[l], w_out[l])
        h = layer_norm(ALPHA * h + mix, ln1_g[l], ln1_b[l])
        ffn = grouped_moe(h, w_router, router_bias, w_gate[l], w_up[l], w_down[l])
        h = layer_norm(ALPHA * h + ffn, ln2_g[l], ln2_b[l])
    return h


_first_inputs_2 = second_inputs


def second_inputs(seed=0):
    import zlib

    import numpy as np

    out = dict(_first_inputs_2(seed))
    spreads = {}
    factors = {'gdn_a_log': 7.329,
     'gdn_norm': 8.0,
     'gla_w2': 4.849,
     'gla_b2': 8.0,
     'gla_norm': 8.0,
     'hgrn_norm': 8.0,
     'router_bias': 2.971,
     'ln2_g': 2.858,
     'ln2_b': 2.806}
    for name, (base, spread) in spreads.items():
        noise = np.random.default_rng([zlib.crc32(name.encode()), seed]).standard_normal(out[name].shape)
        drawn = base * np.exp(spread * noise) if base else spread * noise
        out[name] = __import__('jax').numpy.asarray(drawn.astype(out[name].dtype))
    for name, factor in factors.items():
        out[name] = (out[name] * factor).astype(out[name].dtype)
    return out


_narrow_inputs_2 = second_inputs


def second_inputs(seed=0):

    out = dict(_narrow_inputs_2(seed))
    wider = {'gdn_norm': 5.08, 'gla_norm': 4.42, 'hgrn_norm': 5.36, 'ln2_g': 3.21, 'ln2_b': 3.22}
    for name, times in wider.items():
        mean = out[name].mean()
        out[name] = (mean + times * (out[name] - mean)).astype(out[name].dtype)
    return out


HEAD_DIM = 64
MIX_WIDTH = D_MODEL
GROUP_WIDTH = MIX_WIDTH // N_GROUPS
HEADS_PER_GROUP = GROUP_WIDTH // HEAD_DIM
FOX_HEADS = HEADS_PER_GROUP
MOBA_HEADS = HEADS_PER_GROUP
SB_HEADS = HEADS_PER_GROUP
SWA_HEADS = HEADS_PER_GROUP
SWA_KV_HEADS = SWA_HEADS // 2
SWA_KV_WIDTH = SWA_KV_HEADS * HEAD_DIM
QUERY_BLOCK = 128
MOBA_BLOCK = 256
MOBA_TOPK = 3
MOBA_QUERY_CHUNK = 32
SWA_WINDOW = 128
NUM_BUCKETS = 32
REL_MAX_DISTANCE = 1024
FORGET_BIAS_INIT = 2.0
NEG_INF = -1e30
ATTN_SCALE = HEAD_DIM ** -0.5
SPLIT_SIZES_3 = (
    GROUP_WIDTH, GROUP_WIDTH, GROUP_WIDTH, FOX_HEADS, GROUP_WIDTH,
    GROUP_WIDTH, GROUP_WIDTH, GROUP_WIDTH, GROUP_WIDTH,
    GROUP_WIDTH, GROUP_WIDTH, GROUP_WIDTH, GROUP_WIDTH,
    GROUP_WIDTH, SWA_KV_WIDTH, SWA_KV_WIDTH, GROUP_WIDTH,
)
IN_WIDTH_3 = sum(SPLIT_SIZES_3)


def rms_norm_3(x, gain):
    xf = x.astype(jnp.float32)
    y = xf * lax.rsqrt(jnp.mean(xf * xf, axis=-1, keepdims=True) + RMS_EPS)
    return (y * gain.astype(jnp.float32)).astype(x.dtype)

def split_columns(proj):
    parts, off = [], 0
    for w in SPLIT_SIZES_3:
        parts.append(proj[..., off:off + w])
        off += w
    return parts

def to_heads(t, n):
    b, s, _ = t.shape
    return t.reshape(b, s, n, HEAD_DIM).transpose(0, 2, 1, 3)

def from_heads(o):
    b, h, s, d = o.shape
    return o.transpose(0, 2, 1, 3).reshape(b, s, h * d)

def unblock(out):
    nb, b, h, qb, d = out.shape
    return out.transpose(1, 2, 0, 3, 4).reshape(b, h, nb * qb, d)

def rel_bucket(dist):
    max_exact = NUM_BUCKETS // 2
    d = jnp.maximum(dist, 0)
    log_ratio = jnp.log(jnp.maximum(d, 1).astype(jnp.float32) / max_exact) / math.log(REL_MAX_DISTANCE / max_exact)
    large = max_exact + (log_ratio * (NUM_BUCKETS - max_exact)).astype(jnp.int32)
    large = jnp.minimum(large, NUM_BUCKETS - 1)
    return jnp.where(d < max_exact, d, large)

def forgetting_attention(q, k, v, log_f):
    b, h, t_len, d = q.shape
    c = jnp.cumsum(log_f, axis=-1)
    pos = jnp.arange(t_len)

    def block(i):
        start = i * QUERY_BLOCK
        q_i = lax.dynamic_slice_in_dim(q, start, QUERY_BLOCK, axis=2)
        c_i = lax.dynamic_slice_in_dim(c, start, QUERY_BLOCK, axis=2)
        t = start + jnp.arange(QUERY_BLOCK)
        s = jnp.einsum('bhqd,bhkd->bhqk', q_i, k).astype(jnp.float32) * ATTN_SCALE
        s = s + c_i[..., :, None] - c[..., None, :]
        s = jnp.where(t[:, None] >= pos[None, :], s, NEG_INF)
        p = jax.nn.softmax(s, axis=-1).astype(v.dtype)
        return jnp.einsum('bhqk,bhkd->bhqd', p, v)

    return unblock(lax.map(block, jnp.arange(t_len // QUERY_BLOCK)))

def moba_attention(q, k, v, rel_bias_h):
    b, h, t_len, d = q.shape
    t_pad = -(-t_len // MOBA_BLOCK) * MOBA_BLOCK
    if t_pad != t_len:
        padw = ((0, 0), (0, 0), (0, t_pad - t_len), (0, 0))
        q, k, v = jnp.pad(q, padw), jnp.pad(k, padw), jnp.pad(v, padw)
    nblk = t_pad // MOBA_BLOCK
    k_eff = min(MOBA_TOPK, nblk)
    k_blocks = k.reshape(b, h, nblk, MOBA_BLOCK, d)
    v_blocks = v.reshape(b, h, nblk, MOBA_BLOCK, d)
    k_mean = jnp.mean(k_blocks.astype(jnp.float32), axis=3)
    gate = jnp.einsum('bhtd,bhnd->bhtn', q.astype(jnp.float32), k_mean)
    q_blk = jnp.arange(t_pad) // MOBA_BLOCK
    past = jnp.arange(nblk)[None, :] < q_blk[:, None]
    gate = jnp.where(past, gate, NEG_INF)
    _, sel = lax.top_k(gate, k_eff)
    n_valid = jnp.minimum(q_blk, k_eff)
    sel_valid = jnp.arange(k_eff)[None, :] < n_valid[:, None]
    b_idx = jnp.arange(b)[:, None, None, None]
    h_idx = jnp.arange(h)[None, :, None, None]
    h_idx5 = h_idx[..., None]
    blk_off = jnp.arange(MOBA_BLOCK)

    def chunk(ci):
        start = ci * MOBA_QUERY_CHUNK
        q_c = lax.dynamic_slice_in_dim(q, start, MOBA_QUERY_CHUNK, axis=2)
        sel_c = lax.dynamic_slice_in_dim(sel, start, MOBA_QUERY_CHUNK, axis=2)
        valid_c = lax.dynamic_slice_in_dim(sel_valid, start, MOBA_QUERY_CHUNK, axis=0)
        t = start + jnp.arange(MOBA_QUERY_CHUNK)
        k_sel = k_blocks[b_idx, h_idx, sel_c]
        v_sel = v_blocks[b_idx, h_idx, sel_c]
        s_sel = jnp.einsum('bhqd,bhqnkd->bhqnk', q_c, k_sel).astype(jnp.float32) * ATTN_SCALE
        key_pos = sel_c[..., None] * MOBA_BLOCK + blk_off
        dist = t[None, None, :, None, None] - key_pos
        s_sel = s_sel + rel_bias_h[h_idx5, rel_bucket(dist)].astype(jnp.float32)
        s_sel = jnp.where(valid_c[None, None, :, :, None], s_sel, NEG_INF)
        own_start = (start // MOBA_BLOCK) * MOBA_BLOCK
        k_own = lax.dynamic_slice_in_dim(k, own_start, MOBA_BLOCK, axis=2)
        v_own = lax.dynamic_slice_in_dim(v, own_start, MOBA_BLOCK, axis=2)
        s_own = jnp.einsum('bhqd,bhkd->bhqk', q_c, k_own).astype(jnp.float32) * ATTN_SCALE
        dist_own = t[:, None] - (own_start + blk_off)[None, :]
        s_own = s_own + rel_bias_h[:, rel_bucket(dist_own)][None].astype(jnp.float32)
        s_own = jnp.where(dist_own >= 0, s_own, NEG_INF)
        n_sel = k_eff * MOBA_BLOCK
        s_all = jnp.concatenate([s_sel.reshape(b, h, MOBA_QUERY_CHUNK, n_sel), s_own], axis=-1)
        p = jax.nn.softmax(s_all, axis=-1).astype(v.dtype)
        p_sel = p[..., :n_sel].reshape(b, h, MOBA_QUERY_CHUNK, k_eff, MOBA_BLOCK)
        p_own = p[..., n_sel:]
        return (jnp.einsum('bhqnk,bhqnkd->bhqd', p_sel, v_sel)
                + jnp.einsum('bhqk,bhkd->bhqd', p_own, v_own))

    out = unblock(lax.map(chunk, jnp.arange(t_pad // MOBA_QUERY_CHUNK)))
    return out[:, :, :t_len]

def stick_breaking_attention(q, k, v):
    b, h, t_len, d = q.shape
    pos = jnp.arange(t_len)

    def block(i):
        start = i * QUERY_BLOCK
        q_i = lax.dynamic_slice_in_dim(q, start, QUERY_BLOCK, axis=2)
        t = start + jnp.arange(QUERY_BLOCK)
        z = jnp.einsum('bhqd,bhkd->bhqk', q_i, k).astype(jnp.float32) * ATTN_SCALE
        strict = pos[None, :] < t[:, None]
        log_keep = jnp.where(strict, jax.nn.log_sigmoid(-z), 0.0)
        suffix = lax.cumsum(log_keep, axis=3, reverse=True) - log_keep
        a = jnp.where(strict, jnp.exp(jax.nn.log_sigmoid(z) + suffix), 0.0)
        return jnp.einsum('bhqk,bhkd->bhqd', a.astype(v.dtype), v)

    return unblock(lax.map(block, jnp.arange(t_len // QUERY_BLOCK)))

def swa_sink_attention(q, k, v, sinks, rel_bias_h):
    b, h, t_len, d = q.shape
    hkv = k.shape[1]
    g = h // hkv
    w = SWA_WINDOW
    nb = t_len // w
    qb = q.reshape(b, hkv, g, nb, w, d)

    def band(a):
        ab = a.reshape(b, hkv, nb, w, d)
        prev = jnp.pad(ab, ((0, 0), (0, 0), (1, 0), (0, 0), (0, 0)))[:, :, :-1]
        return jnp.concatenate([prev, ab], axis=3)

    kb, vb = band(k), band(v)
    s = jnp.einsum('bkgnqd,bknsd->bkgnqs', qb, kb).astype(jnp.float32) * ATTN_SCALE
    qi = jnp.arange(w)
    kj = jnp.arange(2 * w)
    dist = qi[:, None] + w - kj[None, :]
    bias = rel_bias_h[:, rel_bucket(dist)].astype(jnp.float32).reshape(hkv, g, 1, w, 2 * w)
    key_pos = jnp.arange(nb)[:, None] * w - w + kj[None, :]
    allowed = ((dist >= 0) & (dist < w))[None] & (key_pos >= 0)[:, None, :]
    s = jnp.where(allowed, s + bias, NEG_INF)
    sink = jnp.broadcast_to(sinks.astype(jnp.float32).reshape(1, hkv, g, 1, 1, 1), s.shape[:-1] + (1,))
    p = jax.nn.softmax(jnp.concatenate([s, sink], axis=-1), axis=-1)[..., :-1]
    o = jnp.einsum('bkgnqs,bknsd->bkgnqd', p.astype(v.dtype), vb)
    return o.reshape(b, h, t_len, d)

def hybrid_layer(x, norm_gain, w_in, b_forget, fox_qk_gain, moba_qk_gain, swa_qk_gain, sinks, w_out, rel_bias):
    hn = rms_norm_3(x, norm_gain)
    proj = jnp.einsum('btd,de->bte', hn, w_in)
    (fq, fk, fv, ff, fg, mq, mk, mv, mg, sq, sk, sv, sg, wq, wk, wv, wg) = split_columns(proj)
    log_f = jax.nn.log_sigmoid((ff + b_forget).astype(jnp.float32)).transpose(0, 2, 1)
    o_fox = forgetting_attention(rms_norm_3(to_heads(fq, FOX_HEADS), fox_qk_gain[0]),
                                 rms_norm_3(to_heads(fk, FOX_HEADS), fox_qk_gain[1]),
                                 to_heads(fv, FOX_HEADS), log_f)
    o_moba = moba_attention(rms_norm_3(to_heads(mq, MOBA_HEADS), moba_qk_gain[0]),
                            rms_norm_3(to_heads(mk, MOBA_HEADS), moba_qk_gain[1]),
                            to_heads(mv, MOBA_HEADS), rel_bias[:, :MOBA_HEADS].T)
    o_sb = stick_breaking_attention(to_heads(sq, SB_HEADS), to_heads(sk, SB_HEADS), to_heads(sv, SB_HEADS))
    o_swa = swa_sink_attention(rms_norm_3(to_heads(wq, SWA_HEADS), swa_qk_gain[0]),
                               rms_norm_3(to_heads(wk, SWA_KV_HEADS), swa_qk_gain[1]),
                               to_heads(wv, SWA_KV_HEADS), sinks, rel_bias[:, MOBA_HEADS:].T)
    y = jnp.concatenate([from_heads(o_fox) * jax.nn.silu(fg),
                         from_heads(o_moba) * jax.nn.silu(mg),
                         from_heads(o_sb) * jax.nn.silu(sg),
                         from_heads(o_swa) * jax.nn.silu(wg)], axis=-1)
    return x + jnp.einsum('bte,ed->btd', y, w_out)

def third_inputs(seed: int = 0) -> dict:
    key = jax.random.key(seed)
    ks = jax.random.split(key, 10)
    x = jax.random.normal(ks[0], (BATCH, SEQ, D_MODEL), jnp.float32)
    norm_gain = 1.0 + 0.02 * jax.random.normal(ks[1], (DEPTH, D_MODEL), jnp.float32)
    w_in = jax.random.normal(ks[2], (DEPTH, D_MODEL, IN_WIDTH_3), jnp.float32) * D_MODEL ** -0.5
    b_forget = FORGET_BIAS_INIT + 0.1 * jax.random.normal(ks[3], (DEPTH, FOX_HEADS), jnp.float32)
    fox_qk_gain = 1.0 + 0.02 * jax.random.normal(ks[4], (DEPTH, 2, HEAD_DIM), jnp.float32)
    moba_qk_gain = 1.0 + 0.02 * jax.random.normal(ks[5], (DEPTH, 2, HEAD_DIM), jnp.float32)
    swa_qk_gain = 1.0 + 0.02 * jax.random.normal(ks[6], (DEPTH, 2, HEAD_DIM), jnp.float32)
    sinks = 0.5 * jax.random.normal(ks[7], (DEPTH, SWA_HEADS), jnp.float32)
    w_out = jax.random.normal(ks[8], (DEPTH, MIX_WIDTH, D_MODEL), jnp.float32) * MIX_WIDTH ** -0.5
    rel_bias = 0.1 * jax.random.normal(ks[9], (NUM_BUCKETS, MOBA_HEADS + SWA_HEADS), jnp.float32)
    return {'x': x, 'norm_gain': norm_gain, 'w_in': w_in, 'b_forget': b_forget,
            'fox_qk_gain': fox_qk_gain, 'moba_qk_gain': moba_qk_gain, 'swa_qk_gain': swa_qk_gain,
            'sinks': sinks, 'w_out': w_out, 'rel_bias': rel_bias}

def third_block(x, norm_gain, w_in, b_forget, fox_qk_gain, moba_qk_gain, swa_qk_gain, sinks, w_out, rel_bias):
    for layer in range(DEPTH):
        x = hybrid_layer(x, norm_gain[layer], w_in[layer], b_forget[layer], fox_qk_gain[layer],
                         moba_qk_gain[layer], swa_qk_gain[layer], sinks[layer], w_out[layer], rel_bias)
    return x


def setup_inputs(seed=0):
    out = dict(first_inputs(seed))
    for name, value in second_inputs(seed + 1).items():
        if name != "x":
            out[name + "_2"] = value
    for name, value in third_inputs(seed + 2).items():
        if name != "x":
            out[name + "_3"] = value
    return out


def reference(
    x, meta_tokens, norm_mix_w, w_in, rwkv_mu, rwkv_w0, rwkv_w2, rwkv_a0, rwkv_a2, rwkv_g2,
    rwkv_k_k, rwkv_k_a, rwkv_r_k, rwkv_ln_w, rwkv_ln_b, rwkv_w_o, diff_lq1, diff_lk1, diff_lq2,
    diff_lk2, diff_subln_w, diff_w_o, w_out, norm_mlp_w, mlp_w1, mlp_w2, final_norm_w, ln0_g_2,
    ln0_b_2, w_in_2, gdn_conv_2, gdn_a_log_2, gdn_dt_bias_2, gdn_norm_2, gla_w2_2, gla_b2_2,
    gla_norm_2, hgrn_lb_logits_2, hgrn_norm_2, w_br_a_2, w_br_b_2, w_br_c_2, w_out_2, ln1_g_2,
    ln1_b_2, w_router_2, router_bias_2, w_gate_2, w_up_2, w_down_2, ln2_g_2, ln2_b_2,
    norm_gain_3, w_in_3, b_forget_3, fox_qk_gain_3, moba_qk_gain_3, swa_qk_gain_3, sinks_3,
    w_out_3, rel_bias_3,
):
    x = first_block(
        x, meta_tokens, norm_mix_w, w_in, rwkv_mu, rwkv_w0, rwkv_w2, rwkv_a0, rwkv_a2, rwkv_g2,
        rwkv_k_k, rwkv_k_a, rwkv_r_k, rwkv_ln_w, rwkv_ln_b, rwkv_w_o, diff_lq1, diff_lk1,
        diff_lq2, diff_lk2, diff_subln_w, diff_w_o, w_out, norm_mlp_w, mlp_w1, mlp_w2,
        final_norm_w,
    )
    x = second_block(
        x, ln0_g_2, ln0_b_2, w_in_2, gdn_conv_2, gdn_a_log_2, gdn_dt_bias_2, gdn_norm_2,
        gla_w2_2, gla_b2_2, gla_norm_2, hgrn_lb_logits_2, hgrn_norm_2, w_br_a_2, w_br_b_2,
        w_br_c_2, w_out_2, ln1_g_2, ln1_b_2, w_router_2, router_bias_2, w_gate_2, w_up_2,
        w_down_2, ln2_g_2, ln2_b_2,
    )
    return third_block(
        x, norm_gain_3, w_in_3, b_forget_3, fox_qk_gain_3, moba_qk_gain_3, swa_qk_gain_3,
        sinks_3, w_out_3, rel_bias_3,
    )


_drawn_inputs = setup_inputs


def setup_inputs(seed=0):
    import zlib

    import numpy as np

    out = dict(_drawn_inputs(seed))
    spreads = {}
    factors = {'gdn_dt_bias_2': 5.397,
     'norm_gain_3': 8.0,
     'b_forget_3': 8.0,
     'fox_qk_gain_3': 8.0,
     'moba_qk_gain_3': 8.0,
     'swa_qk_gain_3': 8.0,
     'sinks_3': 64.0,
     'rel_bias_3': 8.0}
    for name, (base, spread) in spreads.items():
        noise = np.random.default_rng([zlib.crc32(name.encode()), seed]).standard_normal(out[name].shape)
        drawn = base * np.exp(spread * noise) if base else spread * noise
        out[name] = __import__('jax').numpy.asarray(drawn.astype(out[name].dtype))
    for name, factor in factors.items():
        out[name] = (out[name] * factor).astype(out[name].dtype)
    return out
```

```python
import numpy as np
import concourse.bass as bass
from concourse import mybir

F32 = mybir.dt.float32
ALU = mybir.AluOpType
ACT = mybir.ActivationFunctionType
AXX = mybir.AxisListType.X
MUL, ADD, SUB, MAX, MIN = ALU.mult, ALU.add, ALU.subtract, ALU.max, ALU.min

RING = 7
SLAB = 1024


class Tok:

    def __init__(self, eng):
        self.eng, self.used, self.sem, self.count = eng, False, None, 0


class Prog:

    def __init__(self, nc):
        self.nc = nc
        self.q = {e: [] for e in ("pe", "act", "dve", "pool", "sp")}
        self.last = {}
        self.bank_free = [None] * 8
        self.nbank = 0
        self.held = set()
        self.slabs = []
        self.nsem = 0

    def op(self, eng, fn, *waits):
        t = Tok(eng)
        w = list(flat(waits))
        if eng in ("act", "dve", "pool") and eng in self.last:
            w.append(self.last[eng])
        for x in w:
            if not (x.eng == eng == "pe"):
                x.used = True
        self.q[eng].append((w, fn, t))
        self.last[eng] = t
        return t

    def dma(self, out, in_, *waits, eng="sp"):
        t = Tok("dma")
        t.used = True
        t.sem = self.nc.alloc_semaphore(f"d{self.nsem}")
        t.count = 16
        t.after = len(self.slabs)
        self.nsem += 1
        w = list(flat(waits))
        for x in w:
            x.used = True
        e = self.nc.sync
        self.q[eng].append((w, lambda: e.dma_start(out, in_).then_inc(t.sem, 16), t))
        return t

    def marks(self):
        m = [self.last[e] for e in ("pe", "act", "dve", "pool") if e in self.last]
        for t in m:
            t.used = True
        return m

    def gate(self, marks, engines=("pe", "act", "dve", "pool")):
        for e in engines:
            self.q[e].append(([t for t in marks if t.eng != e], None, None))

    def banks(self, n=1):
        while (n == 2 and self.nbank % 2) or any((self.nbank + i) % 8 in self.held for i in range(n)):
            self.nbank += 1
        b = self.nbank % 8
        self.nbank += n
        return b, [self.bank_free[b + i] for i in range(n) if self.bank_free[b + i]]

    def free(self, b, n, tok):
        for i in range(n):
            self.bank_free[b + i] = tok

    def emit(self, wall, ring, block):
        nc = self.nc
        slot_sem = [nc.alloc_semaphore(f"slab{i}") for i in range(RING)]
        for n, s in enumerate(self.slabs):
            s.tok.sem, s.tok.count = slot_sem[n % RING], 16 * (n // RING + 1)
        sems = {e: nc.alloc_semaphore(f"s_{e}") for e in ("pe", "act", "dve", "pool")}
        for n, s in enumerate(self.slabs):
            if n >= RING:
                self.slabs[n - RING].done.used = True
        for e, lst in self.q.items():
            c = 0
            for w, fn, t in lst:
                if t is not None and t.eng == e and t.used:
                    c += 1
                    t.sem, t.count = sems[e], c

        def run(e, eng):
            seen = {}

            def waits(w):
                for t in w:
                    if t.eng == e == "pe":
                        continue
                    if seen.get(t.sem.num, 0) < t.count:
                        seen[t.sem.num] = t.count
                        eng.wait_ge(t.sem, t.count)

            for w, fn, t in self.q[e]:
                waits(w)
                if fn is None:
                    continue
                i = fn()
                if t.eng == e and t.used:
                    i.then_inc(t.sem, 1)

        @block.sync
        def _(eng):
            head = [x for x in self.q["sp"] if not x[0]]
            tail = [x for x in self.q["sp"] if x[0]]
            for w, fn, t in head:
                fn()
            places = {}
            for x in tail:
                places.setdefault(x[2].after, []).append(x)
            for n, s in enumerate(self.slabs):
                for w, fn, t in places.get(n, ()):
                    for k in w:
                        eng.wait_ge(k.sem, k.count)
                    fn()
                if n >= RING:
                    d = self.slabs[n - RING].done
                    eng.wait_ge(d.sem, d.count)
                eng.dma_start(ring[:, (n % RING) * SLAB:(n % RING) * SLAB + s.n],
                              wall[:, s.off:s.off + s.n]).then_inc(slot_sem[n % RING], 16)
            for w, fn, t in places.get(len(self.slabs), ()):
                for k in w:
                    eng.wait_ge(k.sem, k.count)
                fn()
                eng.wait_ge(t.sem, t.count)

        @block.tensor
        def _(eng):
            run("pe", eng)

        @block.scalar
        def _(eng):
            run("act", eng)

        @block.vector
        def _(eng):
            run("dve", eng)

        @block.gpsimd
        def _(eng):
            run("pool", eng)


def flat(x):
    for y in x:
        if y is None:
            continue
        if isinstance(y, (list, tuple)):
            yield from flat(y)
        else:
            yield y


T1, T2 = 528, 512
CH, NCH = 88, 6
import math
ALPHA = 2.0 ** 0.25
LEVELS = (1, 2, 4, 8, 16, 32, 64)

def constants():
    i = np.arange(128)
    c = {}
    c["ident"] = np.eye(128)
    c["ones"] = np.ones((128, 128))
    c["oblk"] = (i[:, None] // 64 == i[None, :] // 64) * 1.0
    c["triu"] = (i[:, None] <= i[None, :]) * 1.0
    c["sup"] = (i[:, None] < i[None, :]) * 1.0
    c["slo"] = (i[:, None] > i[None, :]) * 1.0
    c["negm"] = np.where(i[:, None] >= i[None, :], 0.0, -1e30)
    for l in LEVELS:
        same = (i[:, None] // (2 * l)) == (i[None, :] // (2 * l))
        up = same & (i[:, None] % (2 * l) < l) & (i[None, :] % (2 * l) >= l)
        c[f"u{l}"] = up * 1.0
    c["l1"] = c["u1"].T.copy()
    pos = np.arange(T1, dtype=np.float32)
    inv = np.float32(500000.0) ** (-np.arange(0, 16, 2, dtype=np.float32) / np.float32(16))
    ang = pos[:, None] * inv.astype(np.float32)[None, :]
    cos, sin = np.ones((128, T1)), np.zeros((128, T1))
    rot = np.zeros((128, 128))
    for h in (0, 64):
        for j in range(8):
            cos[h + j] = cos[h + 8 + j] = np.cos(ang[:, j])
            sin[h + j] = sin[h + 8 + j] = np.sin(ang[:, j])
            rot[h + 8 + j, h + j] = -1.0
            rot[h + j, h + 8 + j] = 1.0
    c["cos"], c["sin"], c["rot"] = cos, sin, rot
    m = np.ones((128, T1)); m[:, ::CH] = 0
    c["rst88"] = m
    m = np.ones((128, T2)); m[:, ::128] = 0
    c["rst128"] = m
    s = np.zeros((128, 16, 128))
    for e in range(16):
        s[e, e] = 1.0
    c["sel16"] = s.reshape(128, 2048)
    d = np.arange(0, 512)
    lr = (np.log(np.maximum(d, 1).astype(np.float32) / np.float32(16)) / np.float32(math.log(1024 / 16))).astype(np.float32)
    large = np.minimum(16 + (lr * np.float32(16)).astype(np.int32), 31)
    bk = np.where(d < 16, d, large)
    oh = np.zeros((128, 512 + 128))
    oh[bk[511 - d], d] = 1.0
    c["oh"] = oh[:, :512]
    return {k: v.astype(np.float32) for k, v in c.items()}


def cols_of(names, sizes):
    off, out = 0, {}
    for n, s in zip(names, sizes):
        out[n] = (off, s)
        off += s
    return out, off


PARAMS = {}


def pack_params(I):
    P = {}

    def vec(name, a):
        a = np.asarray(a, np.float32).reshape(-1)
        P[name] = a.reshape(-1, 128).T

    def rows(name, a):
        a = np.asarray(a, np.float32)
        z = np.zeros((128, a.shape[1]), np.float32)
        z[:a.shape[0]] = a
        P[name] = z

    def rep(name, a):
        P[name] = np.broadcast_to(np.asarray(a, np.float32).reshape(1, -1), (128, np.asarray(a).size))

    vec("nmix", I["norm_mix_w"])
    mu = np.asarray(I["rwkv_mu"], np.float32).reshape(-1)
    vec("mu", mu[:3072])
    vec("muwa", mu[3072:3200])
    vec("mug", np.concatenate([mu[3200:3360], np.zeros(96, np.float32)]))
    for n in ("w0", "a0", "k_k", "k_a", "r_k", "ln_w", "ln_b"):
        vec(n, I["rwkv_" + n])
    P["w2a2"] = np.concatenate([np.asarray(I["rwkv_w2"])[0], np.asarray(I["rwkv_a2"])[0]], 0)
    g2 = np.asarray(I["rwkv_g2"])[0]
    P["g2a"] = g2[:128]
    rows("g2b", g2[128:])
    for n in ("lq1", "lk1", "lq2", "lk2"):
        rep(n, I["diff_" + n])
    vec("subln", I["diff_subln_w"])
    vec("nmlp", I["norm_mlp_w"])
    vec("fin", I["final_norm_w"])
    for n in ("ln0_g", "ln0_b", "ln1_g", "ln1_b", "ln2_g", "ln2_b"):
        vec(n, I[n + "_2"])
    conv = np.asarray(I["gdn_conv_2"])[0]
    P["conv"] = conv.reshape(4, 12, 128).transpose(2, 1, 0).reshape(128, 48)
    rep("alog", I["gdn_a_log_2"])
    rep("dtb", I["gdn_dt_bias_2"])
    for n in ("gdn", "gla", "hgrn"):
        vec(n + "n", I[n + "_norm_2"])
    rows("glaw2", np.asarray(I["gla_w2_2"])[0])
    vec("glab2", I["gla_b2_2"])
    vec("lb", I["hgrn_lb_logits_2"])
    P["wr"] = np.asarray(I["w_router_2"]).reshape(8, 128, 16).transpose(1, 0, 2).reshape(128, 128)
    rep("rb", I["router_bias_2"])
    vec("ng3", I["norm_gain_3"])
    rows("bf", np.asarray(I["b_forget_3"]).reshape(4, 1))
    for n in ("fox", "moba", "swa"):
        g = np.asarray(I[n + "_qk_gain_3"])[0]
        P[n + "g"] = np.concatenate([g, g], 1).T
    rep("sinks", I["sinks_3"])
    rows("relb", I["rel_bias_3"])
    return {k: np.ascontiguousarray(v, np.float32) for k, v in P.items()}


def tiles(w):
    k, n = w.shape
    w = w.reshape(k // 128, 128, n // 128, 128).transpose(2, 1, 0, 3)
    return [t.reshape(128, -1) for t in w]


def pack_weights(I):
    A = lambda n: np.asarray(I[n], np.float32).reshape(np.asarray(I[n]).shape[-2:]) if np.asarray(I[n]).ndim == 3 else np.asarray(I[n], np.float32)
    out = []
    w = A("w_in")
    pad = np.concatenate([w[:, 3072:3360], np.zeros((1024, 96), np.float32)], 1)
    out += tiles(pad)
    r = tiles(w[:, :3072])
    for p in range(8):
        out += [r[p], r[8 + p], r[16 + p]]
    out += tiles(A("rwkv_w_o"))
    q = tiles(w[:, 3360:6432])
    for h in range(8):
        out += [q[h], q[8 + h], q[16 + h]]
    g, o = tiles(w[:, 6432:]), tiles(A("diff_w_o"))
    for t in range(8):
        out += [g[t], g[8 + t], o[t]]
    out += tiles(A("w_out"))
    out += tiles(A("mlp_w1"))
    for t in tiles(A("mlp_w2")):
        out += [t[:, 1024 * j:1024 * j + 1024] for j in range(4)]
    w = A("w_in_2")
    at = {}
    off = 0
    for n, s in zip("aq ak av be dt ag bq bk bv lr bg cq cf ci cg ma mb mc".split(),
                    (512, 512, 512, 4, 4, 512, 256, 256, 512, 16, 512, 512, 512, 512, 512, 1024, 1024, 1024)):
        at[n] = w[:, off:off + s]
        off += s
    small = np.concatenate([at["lr"], at["be"], at["dt"], np.zeros((1024, 104), np.float32)], 1)
    out += tiles(small)
    a = {n: tiles(at[n]) for n in at if n not in ("be", "dt", "lr")}
    for h in range(4):
        out += [a["aq"][h], a["ak"][h], a["av"][h], a["ag"][h]]
    for p in range(2):
        out += [a["bq"][p], a["bk"][p]]
        for h in (2 * p, 2 * p + 1):
            out += [a["bv"][h], a["bg"][h]]
    for h in range(4):
        out += [a["cq"][h], a["cf"][h], a["ci"][h], a["cg"][h]]
    br = [tiles(A("w_br_%s_2" % n)) for n in "abc"]
    for t in range(8):
        for b in range(3):
            out += [a["m" + "abc"[b]][t], br[b][t]]
    out += tiles(A("w_out_2"))
    wg, wu = np.asarray(I["w_gate_2"])[0], np.asarray(I["w_up_2"])[0]
    for e in range(16):
        tg, tu = tiles(wg[e]), tiles(wu[e])
        out += [tg[0], tu[0], tg[1], tu[1]]
    for t in tiles(np.asarray(I["w_down_2"], np.float32).reshape(4096, 1024)):
        out += [t[:, 1024 * j:1024 * j + 1024] for j in range(4)]
    w = A("w_in_3")
    at, off = {}, 0
    for n, s in zip("fq fk fv ff fg mq mk mv mg sq sk sv sg wq wk wv wg".split(),
                    (256, 256, 256, 4, 256, 256, 256, 256, 256, 256, 256, 256, 256, 256, 128, 128, 256)):
        at[n] = w[:, off:off + s]
        off += s
    at["ff"] = np.concatenate([at["ff"], np.zeros((1024, 124), np.float32)], 1)
    a = {n: tiles(v) for n, v in at.items()}
    out += a["ff"]
    for g in "fm":
        for p in range(2):
            out += [a[g + "q"][p], a[g + "k"][p], a[g + "v"][p], a[g + "g"][p]]
    for p in range(2):
        out += [a["sq"][p], a["sk"][p], a["sv"][p], a["sg"][p]]
    out += [a["wv"][0]]
    for p in range(2):
        kp = at["wk"][:, 64 * p:64 * p + 64]
        out += [a["wq"][p], tiles(np.concatenate([kp, kp], 1))[0], a["wg"][p]]
    out += tiles(A("w_out_3"))
    return out


N1 = 3 + 24 + 8 + 24 + 24 + 8 + 32 + 32
N2 = 1 + 16 + 12 + 16 + 48 + 8 + 64 + 32


class Kern:

    def __init__(self, nc, P, ring, psum, arena, cst, par):
        self.nc, self.P, self.ring, self.ps, self.ar = nc, P, ring, psum, arena
        self.c, self.p = cst, par
        self.top = 0
        self.woff = 0

    def sb(self, n):
        a = self.ar[:, self.top:self.top + n]
        self.top += n
        assert self.top <= self.ar.shape[1], (self.top, self.ar.shape)
        return a

    def bank(self, b, n=1):
        return self.ps[:, 512 * b:512 * (b + n)]

    def tt(self, out, a, b, op, *w, eng="dve"):
        e = self.nc.vector if eng == "dve" else self.nc.gpsimd
        return self.P.op(eng, lambda: e.tensor_tensor(out, a, b, op), *w)

    def ts(self, out, a, s1, s2, op0, op1, *w, eng="dve"):
        e = self.nc.vector if eng == "dve" else self.nc.gpsimd
        if op1 is None:
            return self.P.op(eng, lambda: e.tensor_scalar(out, a, s1, None, op0), *w)
        return self.P.op(eng, lambda: e.tensor_scalar(out, a, s1, s2, op0, op1), *w)

    def stt(self, out, a, s, b, op0, op1, *w):
        return self.P.op("dve", lambda: self.nc.vector.scalar_tensor_tensor(out=out, in0=a, scalar=s, in1=b, op0=op0, op1=op1), *w)

    def cp(self, out, a, *w, eng="dve"):
        if eng == "act":
            return self.act(out, a, ACT.Copy, *w)
        e = self.nc.vector if eng == "dve" else self.nc.gpsimd
        return self.P.op(eng, lambda: e.tensor_copy(out, a), *w)

    def ms(self, out, v, *w, eng="dve"):
        e = self.nc.vector if eng == "dve" else self.nc.gpsimd
        return self.P.op(eng, lambda: e.memset(out, v), *w)

    def rec(self, out, a, *w):
        return self.P.op("dve", lambda: self.nc.vector.reciprocal(out, a), *w)

    def red(self, out, a, op, *w, neg=False):
        return self.P.op("dve", lambda: self.nc.vector.tensor_reduce(out, a, AXX, op, negate=neg), *w)

    def scan(self, out, d0, d1, *w):
        return self.P.op("dve", lambda: self.nc.vector.tensor_tensor_scan(out, d0, d1, 0.0, MUL, ADD), *w)

    def cpred(self, out, mask, data, *w):
        return self.P.op("dve", lambda: self.nc.vector.copy_predicated(out, mask, data), *w)

    def act(self, out, a, f, *w, bias=0.0, scale=1.0, accum=None):
        return self.P.op("act", lambda: self.nc.scalar.activation(out, a, f, bias=bias, scale=scale, accum_out=accum), *w)

    def mm(self, out, l, r, start, stop, *w, skip=False):
        return self.P.op("pe", lambda: self.nc.tensor.matmul(out, l, r, start=start, stop=stop, skip_group_check=skip), *w)

    def tr(self, out, a, *w):
        n = a.shape[0]
        return self.P.op("pe", lambda: self.nc.tensor.transpose(out, a, self.c["ident"][0:n, 0:n]), *w)

    def slab(self, n=1024):
        s = Slab(n, self.woff, len(self.P.slabs))
        self.woff += n
        self.P.slabs.append(s)
        s.ap = self.ring[:, (s.i % RING) * SLAB:(s.i % RING) * SLAB + n].rearrange("p (k c) -> p k c", c=128)
        return s

    def lin(self, x, T, nk=8, m=128, x0=0, w=()):
        s = self.slab(nk * 128)
        return self.lin_slab(s, x, T, 0, nk, m, x0, w, True)

    def lin_slab(self, s, x, T, k0, nk, m=128, x0=0, w=(), done=False):
        n = 2 if T > 512 else 1
        b, fr = self.P.banks(n)
        hw = T // n
        first = [s.tok, fr, *w]
        for k in range(nk):
            for j in range(n):
                t = self.mm(self.ps[0:m, 512 * (b + j):512 * (b + j) + hw], s.ap[:, k0 + k, 0:m],
                            x[:, (x0 + k) * T + j * hw:(x0 + k) * T + (j + 1) * hw], k == 0, k == nk - 1, *first)
                first = []
        if done:
            s.done = t
        return b, n, t

    def view(self, b, n, T, m0=0, m1=128):
        if n == 1:
            return self.ps[m0:m1, 512 * b:512 * b + T]
        return self.ps[m0:m1, 512 * b:512 * (b + 2)].rearrange("p (a c) -> p a c", a=2)[:, :, 0:T // 2]

    def like(self, ap, n):
        return ap if n == 1 else ap.rearrange("p (a c) -> p a c", a=2)

    def colsum(self, ones, srcs, T, *w, m=128):
        n = 2 if T > 512 else 1
        b, fr = self.P.banks(n)
        first = [fr, *w]
        hw = T // n
        for k, s in enumerate(srcs):
            for j in range(n):
                t = self.mm(self.ps[0:m, 512 * (b + j):512 * (b + j) + hw], ones, s[:, j * hw:(j + 1) * hw],
                            k == 0, k == len(srcs) - 1, *first)
                first = []
        return b, n, t

    def rstd(self, out, b, n, T, scale, eps, tok):
        t = self.act(self.like(out, n), self.view(b, n, T), ACT.Sqrt, tok, scale=scale, bias=eps)
        self.P.free(b, n, t)
        return self.rec(out, out, t)

    def rms(self, x, wcol, out, T, eps, sq, rs, *w):
        for k in range(8):
            t = self.act(sq[:, k * T:(k + 1) * T], x[:, k * T:(k + 1) * T], ACT.Square, *w)
        b, n, t = self.colsum(self.c["ones"], [sq[:, k * T:(k + 1) * T] for k in range(8)], T, t)
        self.rstd(rs, b, n, T, 1.0 / 1024, eps, t)
        for k in range(8):
            t = self.stt(out[:, k * T:(k + 1) * T], x[:, k * T:(k + 1) * T], wcol[:, k:k + 1], rs, MUL, MUL)
        return t

    def lnorm(self, x, g, b_, out, T, eps, sq, rs, *w):
        b, n, t = self.colsum(self.c["ones"], [x[:, k * T:(k + 1) * T] for k in range(8)], T, *w)
        for k in range(8):
            xs = x[:, k * T:(k + 1) * T]
            t = self.stt(xs, self.view(b, n, T), -1.0 / 1024, xs, MUL, ADD, t)
        self.P.free(b, n, t)
        for k in range(8):
            t2 = self.act(sq[:, k * T:(k + 1) * T], x[:, k * T:(k + 1) * T], ACT.Square, t)
        b, n, t = self.colsum(self.c["ones"], [sq[:, k * T:(k + 1) * T] for k in range(8)], T, t2)
        self.rstd(rs, b, n, T, 1.0 / 1024, eps, t)
        for k in range(8):
            xs = x[:, k * T:(k + 1) * T]
            self.stt(xs, xs, g[:, k:k + 1], rs, MUL, MUL)
            t = self.ts(out[:, k * T:(k + 1) * T], xs, b_[:, k:k + 1], None, ADD, None)
        return t

    def phase(self, top):
        self.P.gate(self.P.marks())
        self.top = top


class Slab:
    def __init__(self, n, off, i):
        self.n, self.off, self.i = n, off, i
        self.tok, self.done = Tok("slab"), None


def block1(K, xT, x_tok=None):
    P, c, p, T = K.P, K.c, K.p, T1
    base = K.top
    oy = K.sb(8 * T)
    h = K.sb(8 * T)
    out = oy[:, 0:4096]
    mark = K.top
    hres = K.sb(8 * T)
    sq = K.sb(8 * T)
    rs = K.sb(T)
    ld = P.dma(hres, xT)
    th = K.rms(hres, p["nmix"], h, T, c["eps5"], sq, rs, ld, x_tok)
    K.phase(mark)

    omka = K.sb(8)
    K.ts(omka, p["k_a"], -1.0, 1.0, MUL, ADD)
    lora = [K.sb(T) for _ in range(3)]
    sh = [K.sb(T + 4) for _ in range(3)]
    dd = [K.sb(T) for _ in range(3)]
    for s in sh:
        tz = K.ms(s[:, 0:1], 0.0)
    dsh = dict((n, K.sb(T)) for n in ("k", "cum", "pm", "e", "a", "at", "bt", "kt"))
    sets = [dict(dsh, r=K.sb(T), v=K.sb(T), rt=K.sb(T), pc=K.sb(8)) for _ in range(2)]
    fin = [K.sb(T) for _ in range(2)]
    toks = dict((n, K.sb(NCH * 128)) for n in ("V", "B", "Kh", "At"))
    unit = [dict((n, K.sb(T)) for n in ("M0", "AT", "Mb", "Ak", "Mk", "X", "XT", "Y")) for _ in range(2)]
    for u in unit:
        u["AV"], u["U0"] = K.sb(NCH * 64), K.sb(NCH * 64)
    WT = unit[0]["M0"]
    St = [K.sb(64) for _ in range(2)]
    tsh = [None] * 3

    def shifted(i, b, n, tok, mu, out, rows=128):
        s = sh[i]
        t = K.act(K.like(s[0:rows, 1:T + 1], n), K.view(b, n, T, 0, rows), ACT.Copy, tok, tz, tsh[i])
        P.free(b, n, t)
        K.tt(dd[i][0:rows], s[0:rows, 0:T], s[0:rows, 1:T + 1], SUB, t)
        tsh[i] = K.stt(out[0:rows], dd[i][0:rows], mu[0:rows], s[0:rows, 1:T + 1], MUL, ADD)
        return tsh[i]

    for i, (mu, rows) in enumerate(((p["muwa"][:, 0:1], 128), (p["mug"][:, 0:1], 128), (p["mug"][:, 1:2], 32))):
        b, n, t = K.lin(h, T, m=rows, w=[th])
        t = shifted(i, b, n, t, mu, lora[i], rows)
        if i == 0:
            tl = K.act(lora[0][0:64], lora[0][0:64], ACT.Tanh, t)
        else:
            tl = K.act(lora[i][0:rows], lora[i][0:rows], ACT.Sigmoid, t)

    up = c["sup"][0:CH, 0:CH].unsqueeze(1).to_broadcast([CH, NCH, CH])
    upi = c["triu"][0:CH, 0:CH].unsqueeze(1).to_broadcast([CH, NCH, CH])
    lo = c["slo"][0:CH, 0:CH].unsqueeze(1).to_broadcast([CH, NCH, CH])
    EH = math.exp(-0.5)

    def bc(ap):
        return ap.unsqueeze(1).to_broadcast([CH, NCH, CH])

    def u3(ap):
        return ap[0:CH, 0:T].rearrange("p (c t) -> p c t", c=NCH)

    def ps4(b):
        return K.ps[0:CH, 512 * b:512 * (b + 2)].rearrange("p (a c) -> p a c", a=2)[:, :, 0:264]

    def blk(b, ci, rows=slice(0, CH), w=CH):
        o = 512 * (b + ci // 3) + (ci % 3) * w
        return K.ps[rows, o:o + w]

    def h2(ap):
        return ap.rearrange("p (a t) -> p a t", a=2)

    def glin(x):
        s = K.slab()
        b, fr = P.banks(2)
        P.held |= {b, b + 1}
        first = [s.tok, fr]
        for k in range(8):
            for j in range(2):
                t = K.mm(K.ps[:, 512 * (b + j):512 * (b + j) + 264], s.ap[:, k, :],
                         x[:, k * T + j * 264:k * T + (j + 1) * 264], k == 0, k == 7, *first)
                first = []
            if k % 2 and k < 7:
                yield
        s.done = t
        P.held -= {b, b + 1}
        return b, 2, t

    def prep(hp, m2):
        d = sets[hp % 2]
        col = slice(hp, hp + 1)
        P.gate(m2, ("act", "dve"))
        for i, nme in enumerate("rkv"):
            b, n, t = yield from glin(h)
            shifted(i, b, n, t, p["mu"][:, 8 * i + hp:8 * i + hp + 1], d[nme])
            if nme == "k":
                K.ts(dd[0], d["k"], p["k_k"][:, col], None, MUL, None)
                tkk = K.tt(dd[1], dd[0], dd[0], MUL)
            yield
            if nme == "k":
                b, n, t = K.colsum(c["oblk"], [dd[1]], T, tkk)
                t = K.act(h2(fin2), K.view(b, n, T), ACT.Sqrt, t)
                P.free(b, n, t)
                K.ts(fin2, fin2, 1e-12, None, MAX, None, t)
                K.rec(fin2, fin2)
                K.tt(dd[0], dd[0], fin2, MUL)
        b, fr = P.banks(2)
        for j in range(2):
            t = K.mm(K.ps[:, 512 * (b + j):512 * (b + j) + 264], p["w2a2"][0:64, 128 * hp:128 * hp + 128],
                     lora[0][0:64, 264 * j:264 * j + 264], True, True, fr, tl)
        t = K.act(h2(d["e"]), K.view(b, 2, T), ACT.Sigmoid, t, bias=p["w0"][:, col])
        P.free(b, 2, t)
        b, fr = P.banks(2)
        for j in range(2):
            t2 = K.mm(K.ps[:, 512 * (b + j):512 * (b + j) + 264], p["w2a2"][64:128, 128 * hp:128 * hp + 128],
                      lora[0][64:128, 264 * j:264 * j + 264], True, True, fr)
        ta = K.act(h2(d["a"]), K.view(b, 2, T), ACT.Sigmoid, t2, bias=p["a0"][:, col])
        P.free(b, 2, ta)
        K.scan(d["cum"], c["rst88"], d["e"], t)
        t1 = K.tt(d["pm"], d["cum"], d["e"], SUB)
        tpm = K.act(d["pm"], d["pm"], ACT.Exp, t1, scale=-EH)
        K.act(d["e"], d["cum"], ACT.Exp, scale=EH)
        tcum = K.act(d["cum"], d["cum"], ACT.Exp, scale=-EH)
        yield
        K.ts(dd[1], d["a"], p["k_a"][:, col], omka[:, col], MUL, ADD, ta)
        K.tt(d["k"], d["k"], dd[1], MUL)
        K.tt(dd[1], dd[0], d["a"], MUL)
        K.stt(d["at"], dd[0], -1.0, d["pm"], MUL, MUL, tpm)
        yield
        K.tt(d["bt"], dd[1], d["e"], MUL, tcum)
        K.tt(d["kt"], d["k"], d["e"], MUL)
        K.tt(d["rt"], d["r"], d["cum"], MUL)
        yield
        K.cp(d["pc"][:, 0:NCH].unsqueeze(2), d["cum"].rearrange("p (c t) -> p c t", c=NCH)[:, :, CH - 1:CH])
        K.stt(d["r"], d["r"], p["r_k"][:, col], d["k"], MUL, MUL)
        pcb = d["pc"][:, 0:NCH].unsqueeze(2).to_broadcast([128, NCH, CH])
        v3 = lambda x: x.rearrange("p (c t) -> p c t", c=NCH)
        K.tt(v3(d["e"]), v3(d["bt"]), pcb, MUL)
        d["tq"] = K.tt(v3(d["pm"]), v3(d["kt"]), pcb, MUL)

    def finish(hp, by, ty, tprev):
        d = sets[hp % 2]
        col = slice(hp, hp + 1)
        y, s1 = fin
        t = K.act(h2(y), K.view(by, 2, T), ACT.Copy, ty, tprev)
        P.free(by, 2, t)
        yield
        b, n, tr2 = K.colsum(c["oblk"], [d["r"]], T)
        b2, n, t = K.colsum(c["oblk"], [y], T, t)
        t = K.stt(h2(y), K.view(b2, n, T), -1.0 / 64, h2(y), MUL, ADD, t)
        P.free(b2, n, t)
        t = K.act(s1, y, ACT.Square, t)
        tv = K.tt(h2(d["v"]), h2(d["v"]), K.view(b, n, T), MUL, tr2)
        P.free(b, n, tv)
        yield
        yield
        b, n, t = K.colsum(c["oblk"], [s1], T, t)
        K.rstd(s1, b, n, T, 1.0 / 64, c["epsgn"], t)
        K.tt(y, y, s1, MUL)
        K.ts(y, y, p["ln_w"][:, col], p["ln_b"][:, col], MUL, ADD)
        K.tt(y, y, d["v"], ADD)
        yield
        yield
        b, fr = P.banks(2)
        for j in range(2):
            o = K.ps[:, 512 * (b + j):512 * (b + j) + 264]
            J = slice(264 * j, 264 * j + 264)
            K.mm(o, p["g2a"][:, 128 * hp:128 * hp + 128], lora[1][:, J], True, False, fr)
            t = K.mm(o, p["g2b"][0:32, 128 * hp:128 * hp + 128], lora[2][0:32, J], False, True)
        d["toy"] = K.tt(h2(oy[:, T * hp:T * hp + T]), h2(y), K.view(b, 2, T), MUL, t)
        P.free(b, 2, d["toy"])

    work = []

    def step():
        while work:
            try:
                next(work[0])
                return
            except StopIteration:
                work.pop(0)

    def drain():
        while work:
            step()

    fin2 = dd[2]
    work.append(prep(0, P.marks()))
    drain()
    mscan = None
    for hp in range(8):
        d = sets[hp % 2]
        pc, tq = d["pc"], d["tq"]
        if mscan:
            P.gate(mscan, ("act", "dve"))
        tt_ = {}
        for nme, src in (("V", d["v"]), ("At", d["at"]), ("B", d["e"]), ("Kh", d["pm"])):
            b, fr = P.banks(2)
            for ci in range(NCH):
                o = 512 * (b + ci // 3) + (ci % 3) * 128
                t = K.tr(K.ps[0:CH, o:o + 128], src[:, CH * ci:CH * ci + CH], fr, tq)
            pv = K.ps[0:CH, 512 * b:512 * (b + 2)].rearrange("p (a c) -> p a c", a=2)[:, :, 0:384]
            tt_[nme] = K.act(h2(toks[nme][0:CH]), pv, ACT.Copy, t)
            P.free(b, 2, tt_[nme])
            step()
        ttok = tt_["Kh"]
        tu = {}
        for hh in range(2):
            u = unit[hh]
            R = slice(64 * hh, 64 * hh + 64)
            for nme, l, r, msk in (("AT", "bt", "at", None), ("X", "at", "bt", "l1"), ("Ak", "kt", "at", "sup"),
                                   ("Mb", "bt", "rt", "triu"), ("Mk", "kt", "rt", "triu")):
                b, fr = P.banks(2)
                for ci in range(NCH):
                    S = slice(CH * ci, CH * ci + CH)
                    t = K.mm(blk(b, ci), d[l][R, S], d[r][R, S], True, True, fr, tq)
                pin = ps4(b)
                if msk is None:
                    t2 = K.act(h2(u[nme][0:CH]), pin, ACT.Copy, t)
                else:
                    mk = c[msk][0:CH, 0:CH].unsqueeze(1).to_broadcast([CH, 3, CH])
                    for a in range(2):
                        t2 = K.tt(u[nme][0:CH, 264 * a:264 * a + 264].rearrange("p (c t) -> p c t", c=3),
                                  pin[:, a].rearrange("p (c t) -> p c t", c=3), mk, MUL, t)
                P.free(b, 2, t2)
                tu[nme] = t2
                step()
            b, fr = P.banks(1)
            for ci in range(NCH):
                t = K.mm(K.ps[0:CH, 512 * b + 64 * ci:512 * b + 64 * ci + 64], u["Ak"][0:CH, CH * ci:CH * ci + CH],
                         toks["V"][0:CH, 128 * ci + 64 * hh:128 * ci + 64 * hh + 64], True, True, fr, tu["Ak"], tt_["V"])
            tav = K.cp(u["AV"][0:CH], K.ps[0:CH, 512 * b:512 * b + 384], t, eng="act")
            P.free(b, 1, tav)
            u["tav"] = tav
            idb = bc(c["ident"][0:CH, 0:CH])
            K.tt(u3(u["X"]), u3(u["X"]), idb, ADD)
            K.tt(u3(u["XT"]), u3(u["AT"]), bc(c["u1"][0:CH, 0:CH]), MUL, tu["AT"])
            K.tt(u3(u["XT"]), u3(u["XT"]), idb, ADD)
            u["tx"] = u["tm"] = K.tt(u3(u["M0"]), u3(u["AT"]), bc(c["u2"][0:CH, 0:CH]), MUL)
        drain()
        if hp < 7:
            work.append(prep(hp + 1, P.marks()))
        for l in (2, 4, 8, 16):
            for hh in range(2):
                u = unit[hh]
                MT = u["M0"] if l in (2, 8) else u["Ak"]
                b, fr = P.banks(2)
                for ci in range(NCH):
                    S = slice(CH * ci, CH * ci + CH)
                    t = K.mm(blk(b, ci), MT[0:CH, S], u["X"][0:CH, S], True, True, fr, u["tm"], u["tx"])
                u["ty"] = K.act(h2(u["Y"][0:CH]), ps4(b), ACT.Copy, t)
                P.free(b, 2, u["ty"])
                if l < 16:
                    MN = u["Ak"] if l in (2, 8) else u["M0"]
                    u["tm"] = K.tt(u3(MN), u3(u["AT"]), bc(c[f"u{2 * l}"][0:CH, 0:CH]), MUL, u["tav"])
            step()
            for hh in range(2):
                u = unit[hh]
                bz, fr = P.banks(2)
                for ci in range(NCH):
                    S = slice(CH * ci, CH * ci + CH)
                    tz_ = K.mm(blk(bz, ci), u["XT"][0:CH, S], u["Y"][0:CH, S], True, True, fr, u["ty"])
                b, fr = P.banks(2)
                for ci in range(NCH):
                    S = slice(CH * ci, CH * ci + CH)
                    t = K.mm(blk(b, ci), u["Y"][0:CH, S], u["XT"][0:CH, S], True, True, fr, u["ty"])
                x = K.tt(h2(u["X"][0:CH]), h2(u["X"][0:CH]), ps4(bz), ADD, tz_, t)
                P.free(bz, 2, x)
                u["tx"] = K.tt(h2(u["XT"][0:CH]), h2(u["XT"][0:CH]), ps4(b), ADD, t)
                P.free(b, 2, u["tx"])
            step()
        for l, w in ((32, 32), (64, CH - 64)):
            L_, H_ = slice(0, l), slice(l, l + w)

            def pw(b, rows, width):
                return K.ps[rows, 512 * b:512 * b + NCH * width].rearrange("p (c t) -> p c t", c=NCH)

            for hh in range(2):
                u = unit[hh]
                b, fr = P.banks(1)
                for ci in range(NCH):
                    t = K.mm(K.ps[H_, 512 * b + l * ci:512 * b + l * ci + l], u["AT"][L_, CH * ci + l:CH * ci + l + w],
                             u["X"][L_, CH * ci:CH * ci + l], True, True, fr, u["tx"])
                u["ty"] = K.act(u3(u["Y"])[H_, :, 0:l], pw(b, H_, l), ACT.Copy, t)
                P.free(b, 1, u["ty"])
            step()
            for hh in range(2):
                u = unit[hh]
                if l < 64:
                    bz, fr = P.banks(1)
                    for ci in range(NCH):
                        tz_ = K.mm(K.ps[H_, 512 * bz + l * ci:512 * bz + l * ci + l], u["XT"][H_, CH * ci + l:CH * ci + l + w],
                                   u["Y"][H_, CH * ci:CH * ci + l], True, True, fr, u["ty"])
                b, fr = P.banks(1)
                for ci in range(NCH):
                    t = K.mm(K.ps[L_, 512 * b + w * ci:512 * b + w * ci + w], u["Y"][H_, CH * ci:CH * ci + l],
                             u["XT"][H_, CH * ci + l:CH * ci + l + w], True, True, fr, u["ty"])
                if l < 64:
                    x = K.tt(u3(u["X"])[H_, :, 0:l], u3(u["X"])[H_, :, 0:l], pw(bz, H_, l), ADD, tz_, t)
                    P.free(bz, 1, x)
                u["tx"] = K.tt(u3(u["XT"])[L_, :, l:l + w], u3(u["XT"])[L_, :, l:l + w], pw(b, L_, w), ADD, t)
                P.free(b, 1, u["tx"])
            step()
        b, fr = P.banks(2)
        for hh in range(2):
            u = unit[hh]
            for ci in range(NCH):
                S = slice(CH * ci, CH * ci + CH)
                t = K.mm(blk(b, ci, slice(64 * hh, 64 * hh + 64)), toks["At"][0:CH, 128 * ci + 64 * hh:128 * ci + 64 * hh + 64],
                         u["XT"][0:CH, S], True, True, fr, u["tx"], ttok)
        tw = K.act(h2(WT), K.view(b, 2, T), ACT.Copy, t)
        P.free(b, 2, tw)
        for hh in range(2):
            u = unit[hh]
            b, fr = P.banks(1)
            for ci in range(NCH):
                t = K.mm(K.ps[0:CH, 512 * b + 64 * ci:512 * b + 64 * ci + 64], u["XT"][0:CH, CH * ci:CH * ci + CH],
                         u["AV"][0:CH, 64 * ci:64 * ci + 64], True, True, fr, u["tx"])
            u["tu"] = K.cp(u["U0"][0:CH], K.ps[0:CH, 512 * b:512 * b + 384], t)
            P.free(b, 1, u["tu"])
        by, fry = P.banks(2)
        P.held |= {by, by + 1}
        tS = None
        for ci in range(NCH):
            S = slice(CH * ci, CH * ci + CH)
            so = St[ci % 2]
            sn = St[(ci + 1) % 2]
            tuu = []
            for hh in range(2):
                u = unit[hh]
                R = slice(64 * hh, 64 * hh + 64)
                if ci:
                    b, fr = P.banks(1)
                    t = K.mm(K.ps[0:CH, 512 * b:512 * b + 64], WT[R, S], so[R, :], True, True, fr, tS, tw)
                    us = u["U0"][0:CH, 64 * ci:64 * ci + 64]
                    t = K.tt(us, us, K.ps[0:CH, 512 * b:512 * b + 64], ADD, t)
                    P.free(b, 1, t)
                    tuu.append(t)
                else:
                    tuu.append(u["tu"])
            step()
            if ci < NCH - 1:
                b, fr = P.banks(1)
                for hh in range(2):
                    u = unit[hh]
                    R = slice(64 * hh, 64 * hh + 64)
                    C = slice(128 * ci + 64 * hh, 128 * ci + 64 * hh + 64)
                    o = K.ps[R, 512 * b:512 * b + 64]
                    K.mm(o, toks["Kh"][0:CH, C], toks["V"][0:CH, C], True, False, fr, ttok)
                    t = K.mm(o, toks["B"][0:CH, C], u["U0"][0:CH, 64 * ci:64 * ci + 64], False, True, tuu[hh])
                o = K.ps[:, 512 * b:512 * b + 64]
                if ci:
                    tSn = K.stt(sn, so, pc[:, ci:ci + 1], o, MUL, ADD, t, ty2)
                else:
                    tSn = K.cp(sn, o, t)
                P.free(b, 1, tSn)
                step()
            for hh in range(2):
                u = unit[hh]
                R = slice(64 * hh, 64 * hh + 64)
                o = blk(by, ci, R)
                C = slice(128 * ci + 64 * hh, 128 * ci + 64 * hh + 64)
                K.mm(o, toks["V"][0:CH, C], u["Mk"][0:CH, S], True, False, fry, tu["Mk"])
                t = K.mm(o, u["U0"][0:CH, 64 * ci:64 * ci + 64], u["Mb"][0:CH, S], False, ci == 0, tuu[hh])
                if ci:
                    t = K.mm(o, so[R, :], d["rt"][R, S], False, True)
            ty2 = t
            tS = tSn
            step()
        drain()
        P.held -= {by, by + 1}
        f = finish(hp, by, ty2, sets[(hp + 1) % 2].get("toy"))
        next(f)
        mscan = P.marks()
        work.append(f)
    drain()
    K.phase(mark)

    orw = K.sb(8 * T)
    od = K.sb(8 * T)
    for k in range(8):
        b, n, t = K.lin(oy, T)
        t = K.act(h2(orw[:, k * T:k * T + T]), K.view(b, n, T), ACT.Copy, t)
        P.free(b, n, t)
    torw = t
    lam = K.sb(8)
    lt = K.sb(64)
    K.tt(lt, p["lq1"], p["lk1"], MUL)
    K.red(lam[:, 0:1], lt, ADD)
    K.tt(lt, p["lq2"], p["lk2"], MUL)
    t = K.red(lam[:, 1:2], lt, ADD)
    t = K.act(lam[:, 2:4], lam[:, 0:2], ACT.Exp, t)
    K.stt(lam[:, 4:5], lam[:, 2:3], -1.0, lam[:, 3:4], MUL, ADD, t)
    K.ts(lam[:, 4:5], lam[:, 4:5], -0.2, None, ADD, None)
    K.ts(lam[:, 5:6], p["subln"], 0.8, None, MUL, None)
    bufs = [dict((n, K.sb(w)) for n, w in (
        ("q", T), ("k", T), ("t1", T), ("t2", T), ("V", 5 * 128), ("P0", T), ("P1", T), ("P2", T), ("P3", T),
        ("aw0", T), ("aw1", T), ("O", T), ("sc", 64))) for _ in range(2)]
    TK = [(0, 16)] + [(16 + 128 * j, 128) for j in range(4)]
    old = [None, None]
    for hd in range(8):
        d = bufs[hd % 2]
        if old[hd % 2]:
            P.gate(old[hd % 2])
        for nme in "qk":
            b, n, t = K.lin(h, T)
            t = K.act(h2(d[nme]), K.view(b, n, T), ACT.Copy, t, scale=0.125 if nme == "q" else 1.0)
            P.free(b, n, t)
            tr_ = K.tt(d["t1"], d[nme], c["cos"], MUL, t)
            b, n, t2 = K.colsum(c["rot"], [d[nme]], T, t)
            t3 = K.tt(h2(d["t2"]), K.view(b, n, T), h2(c["sin"]), MUL, t2)
            P.free(b, n, t3)
            tqk = K.tt(d[nme], d["t1"], d["t2"], ADD)
        s = K.slab()
        b, fr = P.banks(2)
        for j, (t0, tw_) in enumerate(TK):
            o = K.ps[0:tw_, 512 * b + 512 * (j > 0) + 128 * max(j - 1, 0):512 * b + 512 * (j > 0) + 128 * max(j - 1, 0) + 128]
            for k in range(8):
                t = K.mm(o, h[:, k * T + t0:k * T + t0 + tw_], s.ap[:, k, :], k == 0, k == 7, fr, s.tok)
        s.done = t
        K.act(d["V"][0:16, 0:128], K.ps[0:16, 512 * b:512 * b + 128], ACT.Copy, t)
        tV = K.act(d["V"][:, 128:640], K.ps[:, 512 * b + 512:512 * b + 1024], ACT.Copy)
        P.free(b, 2, tV)
        bo, fro = P.banks(2)
        P.held = {bo, bo + 1}
        oO = K.ps[:, 512 * bo + 496:512 * bo + 1024]
        mid = P.marks()
        for i, (q0, qw) in enumerate(TK):
            W = q0 + qw
            pr = []
            for sub in range(2):
                R = slice(64 * sub, 64 * sub + 64)
                b, fr = P.banks(2)
                sm = K.ps[0:qw, 512 * b + 496:512 * b + 512]
                sn = K.ps[0:qw, 512 * b + 512:512 * b + 512 + max(W - 16, 0)]
                K.mm(sm, d["q"][R, q0:q0 + qw], d["k"][R, 0:16], True, i > 0, fr, tqk)
                if i == 0:
                    t = K.mm(sm, c["ident"][0:16, 0:16], c["negm"][0:16, 0:16], False, True)
                else:
                    if i > 1:
                        K.mm(sn[:, 0:W - 144], d["q"][R, q0:q0 + qw], d["k"][R, 16:W - 128], True, True)
                    K.mm(sn[:, W - 144:W - 16], d["q"][R, q0:q0 + qw], d["k"][R, W - 128:W], True, False)
                    t = K.mm(sn[:, W - 144:W - 16], c["ident"], c["negm"], False, True)
                s_ = K.ps[0:qw, 512 * b + 496:512 * b + 496 + W]
                sc = d["sc"][0:qw, 6 * i + 3 * sub:6 * i + 3 * sub + 3]
                Pt = d[f"P{2 * (i % 2) + sub}"][0:qw, 0:W]
                t = K.red(sc[:, 0:1], s_, MAX, t, neg=True)
                t = K.act(Pt, s_, ACT.Exp, t, bias=sc[:, 0:1], accum=sc[:, 1:2])
                P.free(b, 2, t)
                K.rec(sc[:, 2:3], sc[:, 1:2], t)
                pr.append((Pt, sc))
            K.tt(pr[1][1][:, 2:3], pr[1][1][:, 2:3], lam[0:qw, 4:5], MUL)
            K.ts(pr[1][0], pr[1][0], pr[1][1][:, 2:3], None, MUL, None)
            t = K.stt(pr[0][0], pr[0][0], pr[0][1][:, 2:3], pr[1][0], MUL, ADD)
            aw = pr[0][0]
            b, fr = P.banks(2)
            t2 = K.tr(K.ps[0:16, 512 * b:512 * b + qw], aw[:, 0:16], fr, t)
            for j in range(1, i + 1):
                t2 = K.tr(K.ps[:, 512 * b + 512 + 128 * (j - 1):512 * b + 512 + 128 * j], aw[:, TK[j][0]:TK[j][0] + 128])
            a = d[f"aw{i % 2}"]
            t3 = K.act(d["t1"][0:16, 128 * (i % 2):128 * (i % 2) + qw], K.ps[0:16, 512 * b:512 * b + qw], ACT.Copy, t2)
            if i:
                t3 = K.act(a[:, 0:128 * i], K.ps[:, 512 * b + 512:512 * b + 512 + 128 * i], ACT.Copy)
            P.free(b, 2, t3)
            o = oO[:, q0:q0 + qw]
            tO = K.mm(o, d["V"][0:16, 0:128], d["t1"][0:16, 128 * (i % 2):128 * (i % 2) + qw], True, i == 0, fro, t3)
            for j in range(1, i + 1):
                tO = K.mm(o, d["V"][:, 128 * j:128 * j + 128], a[:, 128 * (j - 1):128 * j], False, j == i)
        t = K.act(d["O"], oO, ACT.Copy, tO)
        P.free(bo, 2, t)
        P.held = set()
        t = K.act(d["t2"], d["O"], ACT.Square)
        b, n, t = K.colsum(c["ones"], [d["t2"]], T, t)
        K.rstd(d["t1"], b, n, T, 1.0 / 128, c["eps5"], t)
        tod = K.stt(od[:, hd * T:hd * T + T], d["O"], lam[:, 5:6], d["t1"], MUL, MUL)
        old[hd % 2] = P.marks()
    mg = oy
    sg = [K.sb(T) for _ in range(2)]
    K.P.gate(P.marks())
    for k in range(8):
        b, n, t = K.lin(h, T)
        t0 = K.act(h2(sg[0]), K.view(b, n, T), ACT.Sigmoid, t, P.last["dve"])
        P.free(b, n, t0)
        b, n, t = K.lin(h, T)
        t1 = K.act(h2(sg[1]), K.view(b, n, T), ACT.Sigmoid, t)
        P.free(b, n, t1)
        b, n, t = K.lin(od, T, w=[tod])
        K.tt(sg[0], sg[0], orw[:, k * T:k * T + T], MUL, t0)
        t = K.tt(h2(sg[1]), h2(sg[1]), K.view(b, n, T), MUL, t, t1)
        P.free(b, n, t)
        tm = K.tt(mg[:, k * T:k * T + T], sg[0], sg[1], ADD)
    hres = orw
    ld = P.dma(hres, xT, tm)
    for k in range(8):
        b, n, t = K.lin(mg, T, w=[tm])
        t = K.tt(h2(hres[:, k * T:k * T + T]), h2(hres[:, k * T:k * T + T]), K.view(b, n, T), ADD, t, ld)
        P.free(b, n, t)
    tr_ = t
    K.phase(mark + 8 * T)
    rs = K.sb(T)
    th = K.rms(hres, p["nmlp"], h, T, c["eps5"], oy, rs, tr_)
    rl = [K.sb(T) for _ in range(2)]
    H = K.sb(32 * T)
    tsq = [tr_, tr_]
    for k in range(32):
        b, n, t = K.lin(h, T, w=[th])
        t = K.act(h2(rl[k % 2]), K.view(b, n, T), ACT.Relu, t, tsq[k % 2])
        P.free(b, n, t)
        tr_ = tsq[k % 2] = K.tt(H[:, k * T:k * T + T], rl[k % 2], rl[k % 2], MUL, t)
    for k in range(8):
        b, fr = P.banks(2)
        first = [fr, tr_]
        for g in range(4):
            s = K.slab()
            for kk_ in range(8):
                for j in range(2):
                    kx = 8 * g + kk_
                    t = K.mm(K.ps[:, 512 * (b + j):512 * (b + j) + 264], s.ap[:, kk_, :],
                             H[:, kx * T + 264 * j:kx * T + 264 * j + 264], kx == 0, kx == 31, s.tok, *first)
                    first = []
            s.done = t
        t = K.tt(h2(hres[:, k * T:k * T + T]), h2(hres[:, k * T:k * T + T]), K.view(b, 2, T), ADD, t)
        P.free(b, 2, t)
    th = K.rms(hres, p["fin"], h, T, c["eps5"], oy, rs, t)
    for k in range(8):
        t = K.cp(out[:, k * 512:k * 512 + 512], h[:, k * T + 16:k * T + T], th, eng="pool")
    K.phase(base + 8 * 512)
    return out, t


def block2(K, x, x_tok):
    P, c, p, T = K.P, K.c, K.p, T2
    h = K.sb(8 * T)
    O = K.sb(12 * T)
    rs = K.sb(T)
    th = K.lnorm(x, p["ln0_g"], p["ln0_b"], h, T, c["eps5"], O, rs, x_tok)
    mark = K.top

    def bc4(ap):
        return ap.unsqueeze(1).to_broadcast([128, 4, 128])

    def v4(ap):
        return ap.rearrange("p (j t) -> p j t", j=4)

    def evac(out, b, t, f=ACT.Copy, *w, **kw):
        t = K.act(out, K.bank(b), f, t, *w, **kw)
        P.free(b, 1, t)
        return t

    def v_tile(out):
        s = K.slab()
        b, fr = P.banks(1)
        for j in range(4):
            for k in range(8):
                t = K.mm(K.bank(b)[:, 128 * j:128 * j + 128], h[:, k * T + 128 * j:k * T + 128 * j + 128], s.ap[:, k, :],
                         k == 0, k == 7, fr, s.tok)
        s.done = t
        return evac(out, b, t)

    def gated(bo, tO, ncol, gate, out, o, q, r):
        t = evac(o, bo, tO)
        P.held.discard(bo)
        t = K.act(q, o, ACT.Square)
        b, n, t = K.colsum(c["ones"], [q], T, t)
        K.rstd(r, b, n, T, 1.0 / 128, c["eps6"], t)
        K.stt(o, o, ncol, r, MUL, MUL)
        return K.tt(out, o, gate, MUL)

    s = K.slab()
    LR = K.sb(T)
    b, n, t = K.lin_slab(s, h, T, 0, 8, 16, w=[th])
    tlr = K.act(LR[0:16], K.ps[0:16, 512 * b:512 * b + T], ACT.Copy, t)
    P.free(b, 1, tlr)
    b, fr = P.banks(1)
    for j in range(4):
        for k in range(8):
            t = K.mm(K.bank(b)[:, 8 * j:8 * j + 8], h[:, k * T + 128 * j:k * T + 128 * j + 128], s.ap[:, k, 16:24], k == 0, k == 7, fr)
    s.done = t
    sm = K.bank(b)[:, 0:32].rearrange("p (j e) -> p j e", e=8)
    G = {n: K.sb(16) for n in ("be", "nbe", "v", "sp", "g", "cu", "to", "ec", "el", "eks", "bec", "ea", "s", "s2")}
    g4 = lambda n: G[n].rearrange("p (j e) -> p j e", e=4)
    t = K.act(g4("be"), sm[:, :, 0:4], ACT.Sigmoid, t)
    t = K.tt(g4("v"), sm[:, :, 4:8], p["dtb"].unsqueeze(1).to_broadcast([128, 4, 4]), ADD, t)
    P.free(b, 1, t)
    K.act(G["sp"], G["v"], ACT.Abs, t)
    K.act(G["sp"], G["sp"], ACT.Exp, scale=-1.0)
    t = K.act(G["ea"][:, 0:4], p["alog"], ACT.Exp)
    K.ts(G["s"], G["sp"], 2.0, None, ADD, None, t)
    K.rec(G["s"], G["s"])
    K.tt(G["s"], G["s"], G["sp"], MUL)
    K.tt(G["s2"], G["s"], G["s"], MUL)
    K.ts(G["sp"], G["s2"], 1.0 / 17, None, MUL, None)
    for k in (15, 13, 11, 9, 7, 5, 3):
        K.stt(G["sp"], G["sp"], 1.0 / k, G["s2"], ADD, MUL)
    K.stt(G["sp"], G["sp"], 1.0, G["s"], ADD, MUL)
    K.ts(G["s2"], G["v"], 0.0, None, MAX, None)
    K.stt(G["sp"], G["sp"], 2.0, G["s2"], MUL, ADD)
    t = K.stt(g4("g"), g4("sp"), -1.0, G["ea"][:, 0:4].unsqueeze(1).to_broadcast([128, 4, 4]), MUL, MUL)
    b, fr = P.banks(1)
    K.mm(K.bank(b)[:, 0:16], c["triu"], G["g"], True, True, fr, t)
    t = K.mm(K.bank(b)[:, 16:32], c["ones"], G["g"], True, True)
    K.cp(G["cu"], K.bank(b)[:, 0:16], t)
    t = K.cp(G["to"], K.bank(b)[:, 16:32])
    P.free(b, 1, t)
    K.tt(G["eks"], G["to"], G["cu"], SUB)
    t = K.ts(G["nbe"], G["be"], -1.0, None, MUL, None)
    K.act(G["ec"], G["cu"], ACT.Exp, t)
    K.act(G["el"], G["to"], ACT.Exp)
    t = K.act(G["eks"], G["eks"], ACT.Exp)
    K.tt(G["bec"], G["be"], G["ec"], MUL, t)
    CT = K.sb(128)
    b, fr = P.banks(1)
    t = K.tr(K.bank(b)[0:16, 0:128], G["cu"], fr, P.last["dve"])
    tct = K.cp(CT[0:16], K.bank(b)[0:16, 0:128], t)
    P.free(b, 1, tct)
    s16 = c["sel16"].rearrange("p (e j) -> p e j", e=16)
    keep = K.top

    pad = [K.sb(516) for _ in range(2)]
    for q in pad:
        tz = K.ms(q[:, 0:3], 0.0)
    U = {n: K.sb(T) for n in ("q", "k", "v", "g", "er", "D", "DT", "A", "AT", "X", "XT", "MT", "Y", "M", "VB", "KB", "KS", "qi", "u", "wT",
                              "n0", "n1")}
    St = [K.sb(128) for _ in range(2)]
    for hd in range(4):
        tp = {}
        tcv = [None, None]
        for i, nme in enumerate("qkv"):
            b, n, t = K.lin(h, T, w=[th])
            pp = pad[i % 2]
            t = K.act(pp[:, 3:515], K.bank(b), ACT.Copy, t, tz, tcv[i % 2])
            P.free(b, 1, t)
            w = p["conv"][:, 16 * i + 4 * hd:16 * i + 4 * hd + 4]
            K.ts(U[nme], pp[:, 0:512], w[:, 0:1], None, MUL, None, t)
            for k in range(1, 4):
                t = K.stt(U[nme], pp[:, k:k + 512], w[:, k:k + 1], U[nme], MUL, ADD)
            tcv[i % 2] = t
            tp[nme] = K.act(U[nme], U[nme], ACT.Silu, t)
            if nme != "v":
                sq_, r_ = ("n0", "n1") if nme == "q" else ("u", "wT")
                t = K.act(U[sq_], U[nme], ACT.Square)
                b, n, t = K.colsum(c["ones"], [U[sq_]], T, t)
                K.rstd(U[r_], b, n, T, 1.0, c["eps6"], t)
                tp[nme] = K.stt(U[nme], U[nme], 128.0 ** -0.5 if nme == "q" else 1.0, U[r_], MUL, MUL)
        b, n, t = K.lin(h, T)
        tg = evac(U["g"], b, t, ACT.Silu)
        b, fr = P.banks(1)
        for j in range(4):
            t = K.mm(K.bank(b)[:, 128 * j:128 * j + 128], s16[0:16, 4 * j + hd, :], CT[0:16], True, True, fr, tct)
        ter = K.act(U["er"], K.bank(b), ACT.Exp, t)
        for j in range(4):
            J = slice(128 * j, 128 * j + 128)
            cu = G["cu"][:, 4 * j + hd:4 * j + hd + 1]
            K.ts(U["D"][:, J], K.bank(b)[:, J], cu, 0.0, SUB, MAX, ter)
            t = K.ts(U["DT"][:, J], K.bank(b)[:, J], cu, 0.0, SUB, MIN)
        P.free(b, 1, t)
        K.act(U["D"], U["D"], ACT.Exp, t, scale=-1.0)
        t = K.act(U["DT"], U["DT"], ACT.Exp)
        K.tt(v4(U["D"]), v4(U["D"]), bc4(c["slo"]), MUL, t)
        K.tt(v4(U["DT"]), v4(U["DT"]), bc4(c["triu"]), MUL)
        t = K.tt(U["qi"], U["q"], U["er"], MUL)
        b, fr = P.banks(1)
        for j in range(4):
            J = slice(128 * j, 128 * j + 128)
            t = K.mm(K.bank(b)[:, J], U["k"][:, J], U["k"][:, J], True, True, fr, tp["k"], t)
        for j in range(4):
            J = slice(128 * j, 128 * j + 128)
            ta = K.stt(U["A"][:, J], K.bank(b)[:, J], G["nbe"][:, 4 * j + hd:4 * j + hd + 1], U["D"][:, J], MUL, MUL, t)
        P.free(b, 1, ta)
        b, fr = P.banks(1)
        for j in range(4):
            J = slice(128 * j, 128 * j + 128)
            t = K.mm(K.bank(b)[:, J], U["k"][:, J], U["q"][:, J], True, True, fr)
        tM = K.tt(U["M"], K.bank(b), U["DT"], MUL, t)
        P.free(b, 1, tM)
        for src in "vk":
            b, fr = P.banks(1)
            for j in range(4):
                J = slice(128 * j, 128 * j + 128)
                t = K.tr(K.bank(b)[:, J], U[src][:, J], fr, tp["v"])
            for j in range(4):
                J = slice(128 * j, 128 * j + 128)
                cc = slice(4 * j + hd, 4 * j + hd + 1)
                if src == "v":
                    t = K.ts(U["VB"][:, J], K.bank(b)[:, J], G["be"][:, cc], None, MUL, None, t)
                else:
                    K.ts(U["KB"][:, J], K.bank(b)[:, J], G["bec"][:, cc], None, MUL, None, t)
                    t = K.ts(U["KS"][:, J], K.bank(b)[:, J], G["eks"][:, cc], None, MUL, None)
            P.free(b, 1, t)
        tkb = t
        b, fr = P.banks(1)
        for j in range(4):
            J = slice(128 * j, 128 * j + 128)
            t = K.tr(K.bank(b)[:, J], U["A"][:, J], fr, ta)
        tat = K.cp(U["AT"], K.bank(b), t)
        P.free(b, 1, tat)
        for X, A, m in (("X", "A", "l1"), ("XT", "AT", "u1")):
            K.tt(v4(U[X]), v4(U[A]), bc4(c[m]), MUL)
            tx = K.tt(v4(U[X]), v4(U[X]), bc4(c["ident"]), ADD)

        def four(l, r, *w):
            b, fr = P.banks(1)
            for j in range(4):
                J = slice(128 * j, 128 * j + 128)
                t = K.mm(K.bank(b)[:, J], U[l][:, J], U[r][:, J], True, True, fr, *w)
            return b, t

        t = None
        for l in LEVELS[1:]:
            tm = K.tt(v4(U["MT"]), v4(U["AT"]), bc4(c[f"u{l}"]), MUL, t)
            b, t = four("MT", "X", tm, tx)
            ty = evac(U["Y"], b, t)
            if l < 64:
                bz, tz2 = four("XT", "Y", ty)
            b, t2 = four("Y", "XT", ty)
            if l < 64:
                t3 = K.tt(U["X"], U["X"], K.bank(bz), ADD, tz2, t2)
                P.free(bz, 1, t3)
            tx = K.tt(U["XT"], U["XT"], K.bank(b), ADD, t2)
            P.free(b, 1, tx)
        b, t = four("XT", "VB", tx, tkb)
        tu = K.cp(U["u"], K.bank(b), t)
        P.free(b, 1, tu)
        b, t = four("KB", "XT")
        tw = evac(U["wT"], b, t)
        bo, fro = P.banks(1)
        P.held = {bo}
        tS = None
        tO = None
        for j in range(4):
            J = slice(128 * j, 128 * j + 128)
            so, sn = St[j % 2], St[(j + 1) % 2]
            tv = tu
            if j:
                b, fr = P.banks(1)
                t = K.mm(K.bank(b)[:, 0:128], U["wT"][:, J], so, True, True, fr, tS, tw)
                tv = K.tt(U["u"][:, J], U["u"][:, J], K.bank(b)[:, 0:128], SUB, t)
                P.free(b, 1, tv)
            if j < 3:
                b, fr = P.banks(1)
                t = K.mm(K.bank(b)[:, 0:128], U["KS"][:, J], U["u"][:, J], True, True, fr, tv)
                if j:
                    tn = K.stt(sn, so, G["el"][:, 4 * j + hd:4 * j + hd + 1], K.bank(b)[:, 0:128], MUL, ADD, t, tO)
                else:
                    tn = K.cp(sn, K.bank(b)[:, 0:128], t)
                P.free(b, 1, tn)
            o = K.bank(bo)[:, J]
            tO = K.mm(o, U["u"][:, J], U["M"][:, J], True, j == 0, fro, tv, tM)
            if j:
                tO = K.mm(o, so, U["qi"][:, J], False, True)
            tS = tn
        gated(bo, tO, p["gdnn"], U["g"], O[:, hd * T:hd * T + T], U["n0"], U["n1"], U["D"])
        P.gate(P.marks())
    K.phase(keep)

    W = {n: K.sb(T) for n in ("q", "k", "cum", "E", "Q", "Kz", "ks", "la", "t0", "t1", "n0", "n1", "n2")}
    V = [K.sb(T) for _ in range(2)]
    Gt = [K.sb(T) for _ in range(2)]
    acc = [K.sb(T) for _ in range(2)]
    St = [K.sb(128) for _ in range(2)]
    el = K.sb(8)
    u32 = mybir.dt.uint32

    def decay_attention(heads, rows, tqk, tv, tg, ncol, out0):
        for i in range(heads):
            K.ms(acc[i], 0.0)
        for l in (0,) + LEVELS[::-1]:
            if l:
                nb = T // (2 * l)
                cu, E = (W[n].rearrange("p (b t) -> p b t", t=2 * l) for n in ("cum", "E"))
                ref = cu[:, :, l - 1:l].to_broadcast([128, nb, l])
                K.tt(E[:, :, l:2 * l], cu[:, :, l:2 * l], ref, SUB)
                t = K.tt(E[:, :, 0:l], ref, cu[:, :, 0:l], SUB)
                te = K.act(W["E"], W["E"], ACT.Exp, t)
                K.tt(W["Q"], W["q"], W["E"], MUL, te, tl)
                t = K.tt(W["Kz"], W["k"], W["E"], MUL)
                a, bb = "Kz", "Q"
            else:
                a, bb, t = "k", "q", tqk
            for i in range(heads):
                R = slice(rows * i, rows * i + rows)
                b, fr = P.banks(1)
                for j in range(4):
                    J = slice(128 * j, 128 * j + 128)
                    tl = K.mm(K.bank(b)[:, J], W[a][R, J], W[bb][R, J], True, True, fr, t)
                m = c[f"u{l}"] if l else c["ident"]
                ta = K.cpred(v4(acc[i]), bc4(m.bitcast(u32)), v4(K.bank(b)), tl)
                P.free(b, 1, ta)
        cu = v4(W["cum"])
        t = K.tt(v4(W["E"]), cu[:, :, 127:128].to_broadcast([128, 4, 128]), cu, SUB)
        K.act(W["E"], W["E"], ACT.Exp, t)
        K.act(el[:, 0:4].unsqueeze(2), cu[:, :, 127:128], ACT.Exp)
        t = K.act(W["cum"], W["cum"], ACT.Exp)
        K.tt(W["Kz"], W["k"], W["E"], MUL, t, tl)
        t = K.tt(W["Q"], W["q"], W["cum"], MUL)
        b, fr = P.banks(1)
        for j in range(4):
            J = slice(128 * j, 128 * j + 128)
            t2 = K.tr(K.bank(b)[:, J], W["Kz"][:, J], fr, t)
        tks = evac(W["ks"], b, t2)
        bo = []
        for i in range(heads):
            b, fro = P.banks(1)
            P.held.add(b)
            bo.append((b, fro))
        tS, tn, tO = None, None, None
        for j in range(4):
            J = slice(128 * j, 128 * j + 128)
            so, sn = St[j % 2], St[(j + 1) % 2]
            if j < 3:
                b, fr = P.banks(1)
                for i in range(heads):
                    R = slice(rows * i, rows * i + rows)
                    t = K.mm(K.ps[R, 512 * b:512 * b + 128], W["ks"][:, 128 * j + rows * i:128 * j + rows * i + rows], V[i][:, J],
                             True, True, fr, tks, tv)
                if j:
                    tn = K.stt(sn, so, el[:, j:j + 1], K.bank(b)[:, 0:128], MUL, ADD, t, tO)
                else:
                    tn = K.cp(sn, K.bank(b)[:, 0:128], t)
                P.free(b, 1, tn)
            for i in range(heads):
                R = slice(rows * i, rows * i + rows)
                o = K.bank(bo[i][0])[:, J]
                tO = K.mm(o, V[i][:, J], acc[i][:, J], True, j == 0, bo[i][1], ta, tv)
                if j:
                    tO = K.mm(o, so[R, :], W["Q"][R, J], False, True, tS)
            tS = tn
        for i in range(heads):
            gated(bo[i][0], tO, ncol, Gt[i], O[:, (out0 + i) * T:(out0 + i) * T + T],
                  *((W["n0"], W["n1"], W["n2"]) if i == 0 else (W["la"], W["t0"], W["t1"])))
        P.gate(P.marks())

    for pr in range(2):
        b, n, t = K.lin(h, T)
        evac(W["q"], b, t, ACT.Copy, scale=0.125)
        b, n, t = K.lin(h, T)
        tqk = evac(W["k"], b, t)
        for i in range(2):
            tv = v_tile(V[i])
            b, n, t = K.lin(h, T)
            tg = evac(Gt[i], b, t, ACT.Silu)
        b, fr = P.banks(1)
        t = K.mm(K.bank(b), p["glaw2"][0:16, 128 * pr:128 * pr + 128], LR[0:16], True, True, fr, tlr)
        logsig(K, W["la"], K.bank(b), p["glab2"][:, pr:pr + 1], (W["t0"], W["t1"], None), t, b)
        K.ts(W["la"], W["la"], 1.0 / 16, None, MUL, None)
        K.scan(W["cum"], c["rst128"], W["la"])
        decay_attention(2, 64, tqk, tv, tg, p["glan"], 4 + 2 * pr)

    L = {n: K.sb(4) for n in ("m", "e", "r", "lb", "om", "llb", "l1")}
    K.tt(L["m"], p["lb"], p["lb"], MAX)
    t = K.tt(L["e"], p["lb"], L["m"], SUB)
    t = K.act(L["e"], L["e"], ACT.Exp, t)
    K.rec(L["r"], L["e"], t)
    K.tt(L["e"], L["e"], L["r"], MUL)
    K.tt(L["lb"], L["e"], L["e"], SUB)
    K.ts(L["lb"], L["lb"], 0.0, 1.0, MAX, MIN)
    K.ts(L["om"], L["lb"], -1.0, 1.0, MUL, ADD)
    t = K.ts(L["llb"], L["lb"], 1e-30, None, MAX, None)
    K.act(L["llb"], L["llb"], ACT.Sqrt, t)
    K.act(L["llb"], L["llb"], ACT.Ln)
    t = K.act(L["l1"], L["om"], ACT.Ln)
    K.ts(L["llb"], L["llb"], 2.0, None, MUL, None, t)
    for hd in range(4):
        H1 = slice(hd, hd + 1)
        b, n, t = K.lin(h, T)
        t = evac(W["q"], b, t, ACT.Silu)
        K.ts(W["q"], W["q"], 128.0 ** -0.5, None, MUL, None, t)
        b, n, t = K.lin(h, T)
        K.act(W["k"], K.bank(b), ACT.Sigmoid, t, scale=-1.0)
        t = evac(W["t0"], b, t)
        tqk = K.ts(W["k"], W["k"], L["om"][:, H1], None, MUL, None, t)
        K.act(W["t1"], W["t0"], ACT.Abs)
        K.act(W["t1"], W["t1"], ACT.Exp, scale=-1.0)
        t = K.act(W["t1"], W["t1"], ACT.Ln, bias=c["one"])
        K.stt(W["t0"], W["t0"], 0.0, W["t1"], MIN, SUB, t)
        K.ts(W["t0"], W["t0"], L["l1"][:, H1], None, ADD, None)
        t = K.ts(W["t1"], W["t0"], L["llb"][:, H1], None, SUB, None)
        K.act(W["t1"], W["t1"], ACT.Abs, t)
        K.act(W["t1"], W["t1"], ACT.Exp, scale=-1.0)
        t = K.act(W["t1"], W["t1"], ACT.Ln, bias=c["one"])
        K.stt(W["la"], W["t0"], L["llb"][:, H1], W["t1"], MAX, ADD, t)
        K.scan(W["cum"], c["rst128"], W["la"])
        tv = v_tile(V[0])
        b, n, t = K.lin(h, T)
        tg = evac(Gt[0], b, t, ACT.Silu)
        decay_attention(1, 128, tqk, tv, tg, p["hgrnn"], 8 + hd)
    K.phase(mark)

    y = x
    sg = [K.sb(T) for _ in range(2)]
    tsg = [None, None]
    i = 0
    for k in range(8):
        ys = y[:, k * T:k * T + T]
        for br in range(3):
            b, n, t = K.lin(h, T)
            t = K.act(sg[i % 2], K.bank(b), ACT.Sigmoid, t, tsg[i % 2])
            P.free(b, 1, t)
            b, n, t2 = K.lin(O, T, nk=4, x0=4 * br)
            if br == 0:
                tsg[i % 2] = K.tt(ys, sg[i % 2], K.bank(b), MUL, t, t2)
                P.free(b, 1, tsg[i % 2])
            else:
                t = K.tt(sg[i % 2], sg[i % 2], K.bank(b), MUL, t, t2)
                P.free(b, 1, t)
                tsg[i % 2] = ty = K.tt(ys, ys, sg[i % 2], ADD)
            i += 1
    for k in range(8):
        hs = h[:, k * T:k * T + T]
        b, n, t = K.lin(y, T, w=[ty])
        t = K.stt(hs, hs, ALPHA, K.bank(b), MUL, ADD, t)
        P.free(b, 1, t)
    th = K.lnorm(h, p["ln1_g"], p["ln1_b"], x, T, c["eps5"], O, rs, t)

    R = {n: K.sb(64) for n in ("sc", "sel", "gs", "tmp", "f", "kp", "w", "cnt")}
    e3 = lambda n: R[n].rearrange("p (a e) -> p a e", e=4)
    b, fr = P.banks(1)
    for j in range(4):
        for k in range(8):
            t = K.mm(K.bank(b)[:, 16 * j:16 * j + 16], x[:, k * T + 128 * j:k * T + 128 * j + 128], p["wr"][:, 16 * k:16 * k + 16],
                     k == 0, k == 7, fr, th)
    t = K.act(R["sc"], K.bank(b)[:, 0:64], ACT.Sigmoid, t)
    P.free(b, 1, t)
    K.tt(R["sel"].rearrange("p (j e) -> p j e", e=16), R["sc"].rearrange("p (j e) -> p j e", e=16),
         p["rb"].unsqueeze(1).to_broadcast([128, 4, 16]), ADD, t)
    sel = [e3("sel")[:, :, e] for e in range(4)]
    gs, tmp = R["gs"][:, 0:16], R["tmp"][:, 0:16]
    first = True
    for a in range(4):
        for b_ in range(a + 1, 4):
            K.tt(gs if first else tmp, sel[a], sel[b_], ADD)
            if not first:
                K.tt(gs, gs, tmp, MAX)
            first = False
    gs3 = gs.rearrange("p (j g) -> p j g", g=4)
    K.red(R["tmp"][:, 16:20], gs3, MAX)
    f3 = R["f"][:, 0:16].rearrange("p (j g) -> p j g", g=4)
    K.tt(f3, gs3, R["tmp"][:, 16:20].unsqueeze(2).to_broadcast([128, 4, 4]), ALU.is_ge)
    left = R["tmp"][:, 20:24]
    K.ms(left, 1.0)
    for g in range(4):
        K.tt(f3[:, :, g], f3[:, :, g], left, MUL)
        K.tt(left, left, f3[:, :, g], SUB)
    for e in range(4):
        cnt = R["cnt"][:, 16 * e:16 * e + 16]
        n = 0
        for k in range(4):
            if k != e:
                K.tt(tmp if n else cnt, sel[k], sel[e], ALU.is_ge if k < e else ALU.is_gt)
                if n:
                    K.tt(cnt, cnt, tmp, ADD)
                n += 1
        K.stt(e3("kp")[:, :, e], cnt, 1.5, R["f"][:, 0:16], ALU.is_lt, MUL)
    K.tt(R["w"], R["kp"], R["sc"], MUL)
    w3 = R["w"].rearrange("p (j e) -> p j e", e=16)
    K.red(R["tmp"][:, 24:28], w3, ADD)
    K.rec(R["tmp"][:, 28:32], R["tmp"][:, 24:28])
    t = K.tt(w3, w3, R["tmp"][:, 28:32].unsqueeze(2).to_broadcast([128, 4, 16]), MUL)
    cT = K.sb(T)
    b, fr = P.banks(1)
    for j in range(4):
        t2 = K.tr(K.bank(b)[0:16, 128 * j:128 * j + 128], R["w"][:, 16 * j:16 * j + 16], fr, t)
    tc = K.cp(cT[0:16], K.bank(b)[0:16, :], t2)
    P.free(b, 1, tc)

    H = K.sb(32 * T)
    sg = [K.sb(T) for _ in range(2)]
    tsg = [None, None]
    for e in range(16):
        bc_, fr = P.banks(1)
        tcb = K.mm(K.bank(bc_), s16[0:16, e, :], cT[0:16], True, True, fr, tc)
        P.held = {bc_}
        for f in range(2):
            b, n, t = K.lin(x, T)
            t = K.act(sg[f], K.bank(b), ACT.Silu, t, tsg[f])
            P.free(b, 1, t)
            b, n, t2 = K.lin(x, T)
            t = K.tt(sg[f], sg[f], K.bank(b), MUL, t, t2)
            P.free(b, 1, t)
            tsg[f] = K.tt(H[:, (2 * e + f) * T:(2 * e + f + 1) * T], sg[f], K.bank(bc_), MUL, tcb)
        P.free(bc_, 1, tsg[1])
        P.held = set()
    th = tsg[1]
    for k in range(8):
        b, fr = P.banks(1)
        for g in range(4):
            s = K.slab()
            for kk in range(8):
                kx = 8 * g + kk
                t = K.mm(K.bank(b), s.ap[:, kk, :], H[:, kx * T:kx * T + T], kx == 0, kx == 31, s.tok, fr, th)
            s.done = t
        t = K.stt(h[:, k * T:k * T + T], x[:, k * T:k * T + T], ALPHA, K.bank(b), MUL, ADD, t)
        P.free(b, 1, t)
    t = K.lnorm(h, p["ln2_g"], p["ln2_b"], x, T, c["eps5"], O, rs, t)
    K.phase(mark - 21 * T)
    return x, t


def block3(K, x, x_tok):
    P, c, p, T = K.P, K.c, K.p, T2
    nc = K.nc
    h = K.sb(8 * T)
    y = K.sb(8 * T)
    sq = y
    rs = K.sb(T)
    th = K.rms(x, p["ng3"], h, T, c["eps6"], sq, rs, x_tok)
    small = K.sb(32)
    g8 = {}
    for i, n in enumerate(("foxg", "mobag", "swag")):
        K.ts(small[:, i:i + 1], p[n][:, 0:1], 0.125, None, MUL, None)
        g8[n] = (small[:, i:i + 1], p[n][:, 1:2])

    C4, Cn, Z4 = K.sb(T), K.sb(T), [K.sb(T) for _ in range(3)]
    one4 = K.sb(T)
    K.ms(one4[0:4], 1.0)
    b, n, t = K.lin(h, T, m=4, w=[th])
    logsig(K, C4[0:4], K.ps[0:4, 512 * b:512 * b + T], p["bf"][0:4, 0:1], [z[0:4] for z in Z4], t, b)
    tc = K.scan(Cn[0:4], one4[0:4], C4[0:4])

    vec = [K.sb(640) for _ in range(2)]
    rb = K.sb(128)
    table = [K.sb(512 if i < 4 else 256) for i in range(8)]
    ttab = []
    for i in range(8):
        v = vec[i % 2]
        moba = i < 4
        trb = K.ts(rb[0:32], c["ones"][0:32], p["relb"][0:32, i:i + 1], None, MUL, None, P.last["pe"])
        b, fr = P.banks(1)
        t = K.mm(K.bank(b), rb[0:32, 0:128], c["oh"][0:32], True, True, fr, trb)
        wr = [ttab[-2]] if i >= 2 else []
        if moba:
            K.ms(v[:, 512:640], -1e30, wr)
            t = K.cp(v[:, 0:512], K.bank(b), t)
            W = 640
        else:
            K.ms(v[:, 0:384], -1e30, wr)
            t = K.cp(v[:, 128:256], K.bank(b)[:, 384:512], t)
            W = 384
        P.free(b, 1, t)
        dr = nc.dram_tensor(f"skew{i}", [128 * 640], F32, kind="Internal").ap()
        t = P.dma(dr[0:128 * W].rearrange("(p w) -> p w", w=W), v[:, 0:W], t)
        n = 512 if moba else 256
        rd = dr[127:127 + 128 * (W - 1)].rearrange("(p w) -> p w", w=W - 1)[:, 0:n]
        ttab.append(P.dma(table[i][:, 0:n], rd, t))

    bufs = [dict((n, K.sb(w)) for n, w in (
        ("q", T), ("k", T), ("V", T), ("g", T), ("s0", T), ("s1", T), ("P0", T), ("P1", T), ("t0", T), ("t1", T),
        ("sc", 64))) for _ in range(2)]
    vt = K.sb(T)
    old = [None, None]

    def qk_tile(d, nme, gain):
        b, n, t = K.lin(h, T)
        if gain is None:
            t = K.act(d[nme], K.bank(b), ACT.Copy, t, scale=0.125 if nme == "q" else 1.0)
            P.free(b, 1, t)
            return t
        t = K.act(d[nme], K.bank(b), ACT.Copy, t)
        P.free(b, 1, t)
        s0, s1 = (d["s0"], d["s1"]) if nme == "q" else (d["P0"], d["P1"])
        t = K.act(s0, d[nme], ACT.Square)
        b, n, t = K.colsum(c["oblk"], [s0], T, t)
        K.rstd(s1, b, n, T, 1.0 / 64, c["eps6"], t)
        return K.stt(d[nme], d[nme], gain, s1, MUL, MUL)

    def v_tile(out, fr_tok=None):
        s = K.slab()
        b, fr = P.banks(1)
        for j in range(4):
            for k in range(8):
                t = K.mm(K.bank(b)[:, 128 * j:128 * j + 128], h[:, k * T + 128 * j:k * T + 128 * j + 128], s.ap[:, k, :],
                         k == 0, k == 7, fr, s.tok)
        s.done = t
        t = K.act(out, K.bank(b), ACT.Copy, t, fr_tok)
        P.free(b, 1, t)
        return t

    def gate_tile(d):
        b, n, t = K.lin(h, T)
        t = K.act(d["g"], K.bank(b), ACT.Silu, t)
        P.free(b, 1, t)
        return t

    def softmax_head(d, kind, r, V, vcol, hd, tqk, tv, bo):
        R = slice(64 * r, 64 * r + 64)
        for i in range(4):
            q = d["q"][R, 128 * i:128 * i + 128]
            k0 = max(0, i - 1) if kind == "swa" else 0
            W = 128 * (i + 1 - k0)
            b, fr = P.banks(1)
            s_ = K.bank(b)[:, 0:W]
            K.mm(s_, q, d["k"][R, 128 * k0:128 * (i + 1)], True, False, fr, tqk)
            if kind == "fox":
                K.mm(s_, Cn[0:4, 128 * i:128 * i + 128], s16[0:4, hd, 0:1].to_broadcast([4, W]), False, False, tc, tsel)
                K.mm(s_, seln[0:4, 128 * hd:128 * hd + 128], Cn[0:4, 0:W], False, True)
                K.mm(s_[:, W - 128:W], c["ident"], c["negm"], False, True, skip=True)
            elif kind == "moba":
                K.mm(s_, c["ident"], table[hd][:, 512 - W:512], False, True, ttab[hd])
            else:
                K.mm(s_, c["ident"], table[4 + hd][:, 256 - W:256], False, True, ttab[4 + hd])
            t = P.last["pe"]
            sc = d["sc"][:, 8 * i:8 * i + 8] if r == 0 else d["sc"][:, 32 + 8 * i:40 + 8 * i]
            Pt = d[f"P{i % 2}"][:, 0:W]
            if kind == "swa":
                K.red(sc[:, 3:4], s_, MAX, t)
                t = K.ts(sc[:, 0:1], sc[:, 3:4], p["sinks"][:, hd:hd + 1], -1.0, MAX, MUL)
            else:
                t = K.red(sc[:, 0:1], s_, MAX, t, neg=True)
            t = K.act(Pt, s_, ACT.Exp, t, bias=sc[:, 0:1], accum=sc[:, 1:2])
            P.free(b, 1, t)
            if kind == "swa":
                t = K.act(sc[:, 4:5], p["sinks"][:, hd:hd + 1], ACT.Exp, bias=sc[:, 0:1])
                K.tt(sc[:, 1:2], sc[:, 1:2], sc[:, 4:5], ADD, t)
            K.rec(sc[:, 2:3], sc[:, 1:2], t)
            t = K.ts(Pt, Pt, sc[:, 2:3], None, MUL, None)
            b, fr = P.banks(1)
            nb = W // 128
            for j in range(nb):
                t2 = K.tr(K.bank(b)[:, 128 * j:128 * j + 128], Pt[:, 128 * j:128 * j + 128], fr, t)
            a = d[f"t{i % 2}"]
            t3 = K.cp(a[:, 0:W], K.bank(b)[:, 0:W], t2, eng="act")
            P.free(b, 1, t3)
            for j in range(nb):
                tO = K.mm(K.ps[R, 512 * bo + 128 * i:512 * bo + 128 * i + 128],
                          V[:, 128 * (k0 + j) + vcol:128 * (k0 + j) + vcol + 64], a[:, 128 * j:128 * j + 128],
                          j == 0, j == nb - 1, t3, tv)
        return tO

    seln = K.sb(4 * 128)
    s16 = c["sel16"].rearrange("p (e j) -> p e j", e=16)
    for e in range(4):
        tsel = K.ts(seln[0:4, 128 * e:128 * e + 128], s16[0:4, e, :], -1.0, None, MUL, None)

    def start(i):
        if old[i % 2]:
            P.gate(old[i % 2])
        return bufs[i % 2]

    def finish(i, d, bo, tO, tile, tg):
        t = K.tt(y[:, T * tile:T * tile + T], d["g"], K.bank(bo), MUL, tO, tg)
        P.free(bo, 1, t)
        P.held = set()
        old[i % 2] = P.marks()
        return t

    it = 0
    for gi, kind in enumerate(("fox", "moba")):
        for pr in range(2):
            d = start(it)
            gq, gk = g8[kind + "g"]
            qk_tile(d, "q", gq)
            tqk = qk_tile(d, "k", gk)
            tv = v_tile(d["V"])
            tg = gate_tile(d)
            bo, fro = P.banks(1)
            P.held = {bo}
            P.gate(fro)
            for r in range(2):
                tO = softmax_head(d, kind, r, d["V"], 64 * r, 2 * pr + r, tqk, tv, bo)
            ty = finish(it, d, bo, tO, 2 * gi + pr, tg)
            it += 1
    sb_bufs = [d for d in bufs]
    Lk = [K.sb(T) for _ in range(4)]
    Zk = Z4 + [C4]
    for pr in range(2):
        d = start(it)
        qk_tile(d, "q", None)
        tqk = qk_tile(d, "k", None)
        tv = v_tile(d["V"])
        tg = gate_tile(d)
        bo, fro = P.banks(1)
        P.held = {bo}
        P.gate(fro)
        for r in range(2):
            R = slice(64 * r, 64 * r + 64)
            tl = None
            for j in range(4):
                W = 512 - 128 * j
                b, fr = P.banks(1)
                t = K.mm(K.bank(b)[:, 0:W], d["k"][R, 128 * j:128 * j + 128], d["q"][R, 128 * j:512], True, True, fr, tqk)
                z, lk, s0, s1 = Zk[j][:, 0:W], Lk[j][:, 0:W], d["s0"][:, 0:W], d["s1"][:, 0:W]
                t = K.act(z, K.bank(b)[:, 0:W], ACT.Copy, t, P.last["dve"])
                P.free(b, 1, t)
                K.act(s0, z, ACT.Abs)
                K.act(s0, s0, ACT.Exp, scale=-1.0)
                t = K.act(s0, s0, ACT.Ln, bias=c["one"])
                K.stt(s1, z, 0.0, s0, MAX, ADD, t)
                K.tt(z, z, s1, SUB)
                K.ts(lk, s1, -1.0, None, MUL, None, P.last["pe"])
                tl = K.tt(lk[:, 0:128], lk[:, 0:128], c["sup"], MUL)
            for j in range(4):
                W = 512 - 128 * j
                b, fr = P.banks(1)
                K.mm(K.bank(b)[:, 0:W], c["slo"], Lk[j][:, 0:W], True, True, fr, tl)
                for j2 in range(j + 1, 4):
                    o = 128 * (j2 - j)
                    K.mm(K.bank(b)[:, o:W], c["ones"], Lk[j2][:, 0:W - o], False, True, skip=True)
                t = P.last["pe"]
                a = d[f"P{j % 2}"][:, 0:W]
                t = K.tt(a, Zk[j][:, 0:W], K.bank(b)[:, 0:W], ADD, t)
                P.free(b, 1, t)
                t = K.act(d[f"t{j % 2}"][:, 0:W], a, ACT.Exp, t)
                w0 = d[f"t{j % 2}"]
                t = K.tt(w0[:, 0:128], w0[:, 0:128], c["sup"], MUL, t)
                tO = K.mm(K.ps[R, 512 * bo + 128 * j:512 * bo + 512], d["V"][:, 128 * j + 64 * r:128 * j + 64 * r + 64],
                          w0[:, 0:W], j == 0, True, t, tv, skip=j > 0)
        ty = finish(it, d, bo, tO, 4 + pr, tg)
        it += 1
    tv = v_tile(vt)
    for pr in range(2):
        d = start(it)
        gq, gk = g8["swag"]
        qk_tile(d, "q", gq)
        tqk = qk_tile(d, "k", gk)
        tg = gate_tile(d)
        bo, fro = P.banks(1)
        P.held = {bo}
        P.gate(fro)
        for r in range(2):
            tO = softmax_head(d, "swa", r, vt, 64 * pr, 2 * pr + r, tqk, tv, bo)
        ty = finish(it, d, bo, tO, 6 + pr, tg)
        it += 1
    for k in range(8):
        b, n, t = K.lin(y, T, w=[ty])
        xs = x[:, k * T:k * T + T]
        t = K.tt(xs, xs, K.bank(b), ADD, t)
        P.free(b, 1, t)
    return x, t


def logsig(K, out, src, bias, tmp, tok, b):
    v, a, e = tmp
    n = v.shape[0]
    t = K.act(v, src, ACT.Identity, tok, bias=bias)
    if b is not None:
        K.P.free(b, 1, t)
    K.act(a, v, ACT.Abs)
    K.act(a, a, ACT.Exp, scale=-1.0)
    t = K.act(a, a, ACT.Ln, bias=K.c["one"][0:n])
    return K.stt(out, v, 0.0, a, MIN, SUB, t)


def layout(inputs):
    I = {k: np.asarray(v) for k, v in inputs.items()}
    x = np.concatenate([I["meta_tokens"], I["x"][0]], 0)
    xT = x.T.reshape(8, 128, T1).transpose(1, 0, 2).reshape(128, 8 * T1)
    con = constants()
    par = pack_params(I)
    return xT, con, par, pack_weights(I)


def program(nc, xT, out, con, par, wall, at, blocks=(1, 2, 3)):
    P = Prog(nc)
    ring = nc.alloc_sbuf_tensor("ring", [128, RING * SLAB], F32)
    nfree = (nc.sbuf_bytes_remaining - 64) // 4 // 8 * 8
    arena = nc.alloc_sbuf_tensor("arena", [128, nfree], F32)
    psum = nc.alloc_psum_tensor("psum", [128, 4096], F32)
    c, p = {}, {}
    K = Kern(nc, P, ring, psum, arena, c, p)
    cb, pb = K.sb(at["ncon"]), K.sb(at["npar"])
    loads = [P.dma(cb, con), P.dma(pb, par)]
    for k, (o, n) in at["con"].items():
        c[k] = cb[:, o:o + n]
    for k, (o, n) in at["par"].items():
        p[k] = pb[:, o:o + n]
    eps = K.sb(8)
    for i, (k, v) in enumerate((("eps5", 1e-5), ("eps6", 1e-6), ("epsgn", 64e-5), ("one", 1.0))):
        c[k] = eps[:, i:i + 1]
        K.ms(c[k], v)
    P.gate(P.marks() + loads)
    base = K.top
    x, t = None, None
    if 1 in blocks:
        x, t = block1(K, xT)
    else:
        x = K.sb(4096)
        t = P.dma(x, xT)
    if 2 in blocks:
        x, t = block2(K, x, t)
    if 3 in blocks:
        x, t = block3(K, x, t)
    P.dma(out, x, t)
    with nc.Block() as block:
        P.emit(wall, ring, block)


def offsets(d):
    off, at = 0, {}
    for k, v in d.items():
        at[k] = (off, v.shape[1])
        off += v.shape[1]
    return at, off


def kernel(**inputs):
    import concourse.bacc as bacc
    from concourse.bass_utils import run_bass_kernel_spmd as run

    xT, con, par, w = layout(inputs)
    at = {}
    at["con"], at["ncon"] = offsets(con)
    at["par"], at["npar"] = offsets(par)
    arrays = {
        "in_x": np.ascontiguousarray(xT, np.float32),
        "in_con": np.ascontiguousarray(np.concatenate(list(con.values()), 1)),
        "in_par": np.ascontiguousarray(np.concatenate(list(par.values()), 1)),
        "in_w": np.concatenate(w, 1),
    }
    nc = bacc.Bacc("TRN2", target_bir_lowering=False, num_devices=1)
    d = {k: nc.dram_tensor(k, list(v.shape), F32, kind="ExternalInput").ap() for k, v in arrays.items()}
    out = nc.dram_tensor("out_0", [128, 8 * 512], F32, kind="ExternalOutput").ap()
    program(nc, d["in_x"], out, d["in_con"], d["in_par"], d["in_w"], at)
    r = run(nc, [arrays], core_ids=[0])
    o = np.asarray(r.results[0]["out_0"]).reshape(128, 8, 512).transpose(1, 0, 2).reshape(1024, 512)
    return np.ascontiguousarray(o.T).reshape(1, 512, 1024)
```

```python
import numpy as np
import concourse.bass as bass
from concourse import mybir

F32 = mybir.dt.float32
ALU = mybir.AluOpType
ACT = mybir.ActivationFunctionType
AXX = mybir.AxisListType.X
MUL, ADD, SUB, MAX, MIN = ALU.mult, ALU.add, ALU.subtract, ALU.max, ALU.min

RING = 7
SLAB = 1024


class Tok:

    def __init__(self, eng):
        self.eng, self.used, self.sem, self.count = eng, False, None, 0


class Prog:

    def __init__(self, nc):
        self.nc = nc
        self.q = {e: [] for e in ("pe", "act", "dve", "pool", "sp")}
        self.last = {}
        self.bank_free = [None] * 8
        self.nbank = 0
        self.held = set()
        self.slabs = []
        self.nsem = 0

    def op(self, eng, fn, *waits):
        t = Tok(eng)
        w = list(flat(waits))
        if eng in ("act", "dve", "pool") and eng in self.last:
            w.append(self.last[eng])
        for x in w:
            if not (x.eng == eng == "pe"):
                x.used = True
        self.q[eng].append((w, fn, t))
        self.last[eng] = t
        return t

    def dma(self, out, in_, *waits, eng="sp"):
        t = Tok("dma")
        t.used = True
        t.sem = self.nc.alloc_semaphore(f"d{self.nsem}")
        t.count = 16
        t.after = len(self.slabs)
        self.nsem += 1
        w = list(flat(waits))
        for x in w:
            x.used = True
        e = self.nc.sync
        self.q[eng].append((w, lambda: e.dma_start(out, in_).then_inc(t.sem, 16), t))
        return t

    def marks(self):
        m = [self.last[e] for e in ("pe", "act", "dve", "pool") if e in self.last]
        for t in m:
            t.used = True
        return m

    def gate(self, marks, engines=("pe", "act", "dve", "pool")):
        for e in engines:
            self.q[e].append(([t for t in marks if t.eng != e], None, None))

    def banks(self, n=1):
        while (n == 2 and self.nbank % 2) or any((self.nbank + i) % 8 in self.held for i in range(n)):
            self.nbank += 1
        b = self.nbank % 8
        self.nbank += n
        return b, [self.bank_free[b + i] for i in range(n) if self.bank_free[b + i]]

    def free(self, b, n, tok):
        for i in range(n):
            self.bank_free[b + i] = tok

    def emit(self, wall, ring, block):
        nc = self.nc
        slot_sem = [nc.alloc_semaphore(f"slab{i}") for i in range(RING)]
        for n, s in enumerate(self.slabs):
            s.tok.sem, s.tok.count = slot_sem[n % RING], 16 * (n // RING + 1)
        sems = {e: nc.alloc_semaphore(f"s_{e}") for e in ("pe", "act", "dve", "pool")}
        for n, s in enumerate(self.slabs):
            if n >= RING:
                self.slabs[n - RING].done.used = True
        for e, lst in self.q.items():
            c = 0
            for w, fn, t in lst:
                if t is not None and t.eng == e and t.used:
                    c += 1
                    t.sem, t.count = sems[e], c

        def run(e, eng):
            seen = {}

            def waits(w):
                for t in w:
                    if t.eng == e == "pe":
                        continue
                    if seen.get(t.sem.num, 0) < t.count:
                        seen[t.sem.num] = t.count
                        eng.wait_ge(t.sem, t.count)

            for w, fn, t in self.q[e]:
                waits(w)
                if fn is None:
                    continue
                i = fn()
                if t.eng == e and t.used:
                    i.then_inc(t.sem, 1)

        @block.sync
        def _(eng):
            head = [x for x in self.q["sp"] if not x[0]]
            tail = [x for x in self.q["sp"] if x[0]]
            for w, fn, t in head:
                fn()
            places = {}
            for x in tail:
                places.setdefault(x[2].after, []).append(x)
            for n, s in enumerate(self.slabs):
                for w, fn, t in places.get(n, ()):
                    for k in w:
                        eng.wait_ge(k.sem, k.count)
                    fn()
                if n >= RING:
                    d = self.slabs[n - RING].done
                    eng.wait_ge(d.sem, d.count)
                eng.dma_start(ring[:, (n % RING) * SLAB:(n % RING) * SLAB + s.n],
                              wall[:, s.off:s.off + s.n]).then_inc(slot_sem[n % RING], 16)
            for w, fn, t in places.get(len(self.slabs), ()):
                for k in w:
                    eng.wait_ge(k.sem, k.count)
                fn()
                eng.wait_ge(t.sem, t.count)

        @block.tensor
        def _(eng):
            run("pe", eng)

        @block.scalar
        def _(eng):
            run("act", eng)

        @block.vector
        def _(eng):
            run("dve", eng)

        @block.gpsimd
        def _(eng):
            run("pool", eng)


def flat(x):
    for y in x:
        if y is None:
            continue
        if isinstance(y, (list, tuple)):
            yield from flat(y)
        else:
            yield y


T1, T2 = 528, 512
CH, NCH = 88, 6
import math
ALPHA = 2.0 ** 0.25
LEVELS = (1, 2, 4, 8, 16, 32, 64)

def constants():
    i = np.arange(128)
    c = {}
    c["ident"] = np.eye(128)
    c["ones"] = np.ones((128, 128))
    c["oblk"] = (i[:, None] // 64 == i[None, :] // 64) * 1.0
    c["triu"] = (i[:, None] <= i[None, :]) * 1.0
    c["sup"] = (i[:, None] < i[None, :]) * 1.0
    c["slo"] = (i[:, None] > i[None, :]) * 1.0
    c["negm"] = np.where(i[:, None] >= i[None, :], 0.0, -1e30)
    for l in LEVELS:
        same = (i[:, None] // (2 * l)) == (i[None, :] // (2 * l))
        up = same & (i[:, None] % (2 * l) < l) & (i[None, :] % (2 * l) >= l)
        c[f"u{l}"] = up * 1.0
    c["l1"] = c["u1"].T.copy()
    pos = np.arange(T1, dtype=np.float32)
    inv = np.float32(500000.0) ** (-np.arange(0, 16, 2, dtype=np.float32) / np.float32(16))
    ang = pos[:, None] * inv.astype(np.float32)[None, :]
    cos, sin = np.ones((128, T1)), np.zeros((128, T1))
    rot = np.zeros((128, 128))
    for h in (0, 64):
        for j in range(8):
            cos[h + j] = cos[h + 8 + j] = np.cos(ang[:, j])
            sin[h + j] = sin[h + 8 + j] = np.sin(ang[:, j])
            rot[h + 8 + j, h + j] = -1.0
            rot[h + j, h + 8 + j] = 1.0
    c["cos"], c["sin"], c["rot"] = cos, sin, rot
    m = np.ones((128, T1)); m[:, ::CH] = 0
    c["rst88"] = m
    m = np.ones((128, T2)); m[:, ::128] = 0
    c["rst128"] = m
    s = np.zeros((128, 16, 128))
    for e in range(16):
        s[e, e] = 1.0
    c["sel16"] = s.reshape(128, 2048)
    d = np.arange(0, 512)
    lr = (np.log(np.maximum(d, 1).astype(np.float32) / np.float32(16)) / np.float32(math.log(1024 / 16))).astype(np.float32)
    large = np.minimum(16 + (lr * np.float32(16)).astype(np.int32), 31)
    bk = np.where(d < 16, d, large)
    oh = np.zeros((128, 512 + 128))
    oh[bk[511 - d], d] = 1.0
    c["oh"] = oh[:, :512]
    return {k: v.astype(np.float32) for k, v in c.items()}


def cols_of(names, sizes):
    off, out = 0, {}
    for n, s in zip(names, sizes):
        out[n] = (off, s)
        off += s
    return out, off


PARAMS = {}


def pack_params(I):
    P = {}

    def vec(name, a):
        a = np.asarray(a, np.float32).reshape(-1)
        P[name] = a.reshape(-1, 128).T

    def rows(name, a):
        a = np.asarray(a, np.float32)
        z = np.zeros((128, a.shape[1]), np.float32)
        z[:a.shape[0]] = a
        P[name] = z

    def rep(name, a):
        P[name] = np.broadcast_to(np.asarray(a, np.float32).reshape(1, -1), (128, np.asarray(a).size))

    vec("nmix", I["norm_mix_w"])
    mu = np.asarray(I["rwkv_mu"], np.float32).reshape(-1)
    vec("mu", mu[:3072])
    vec("muwa", mu[3072:3200])
    vec("mug", np.concatenate([mu[3200:3360], np.zeros(96, np.float32)]))
    for n in ("w0", "a0", "k_k", "k_a", "r_k", "ln_w", "ln_b"):
        vec(n, I["rwkv_" + n])
    P["w2a2"] = np.concatenate([np.asarray(I["rwkv_w2"])[0], np.asarray(I["rwkv_a2"])[0]], 0)
    g2 = np.asarray(I["rwkv_g2"])[0]
    P["g2a"] = g2[:128]
    rows("g2b", g2[128:])
    for n in ("lq1", "lk1", "lq2", "lk2"):
        rep(n, I["diff_" + n])
    vec("subln", I["diff_subln_w"])
    vec("nmlp", I["norm_mlp_w"])
    vec("fin", I["final_norm_w"])
    for n in ("ln0_g", "ln0_b", "ln1_g", "ln1_b", "ln2_g", "ln2_b"):
        vec(n, I[n + "_2"])
    conv = np.asarray(I["gdn_conv_2"])[0]
    P["conv"] = conv.reshape(4, 12, 128).transpose(2, 1, 0).reshape(128, 48)
    rep("alog", I["gdn_a_log_2"])
    rep("dtb", I["gdn_dt_bias_2"])
    for n in ("gdn", "gla", "hgrn"):
        vec(n + "n", I[n + "_norm_2"])
    rows("glaw2", np.asarray(I["gla_w2_2"])[0])
    vec("glab2", I["gla_b2_2"])
    vec("lb", I["hgrn_lb_logits_2"])
    P["wr"] = np.asarray(I["w_router_2"]).reshape(8, 128, 16).transpose(1, 0, 2).reshape(128, 128)
    rep("rb", I["router_bias_2"])
    vec("ng3", I["norm_gain_3"])
    rows("bf", np.asarray(I["b_forget_3"]).reshape(4, 1))
    for n in ("fox", "moba", "swa"):
        g = np.asarray(I[n + "_qk_gain_3"])[0]
        P[n + "g"] = np.concatenate([g, g], 1).T
    rep("sinks", I["sinks_3"])
    rows("relb", I["rel_bias_3"])
    return {k: np.ascontiguousarray(v, np.float32) for k, v in P.items()}


def tiles(w):
    k, n = w.shape
    w = w.reshape(k // 128, 128, n // 128, 128).transpose(2, 1, 0, 3)
    return [t.reshape(128, -1) for t in w]


def pack_weights(I):
    A = lambda n: np.asarray(I[n], np.float32).reshape(np.asarray(I[n]).shape[-2:]) if np.asarray(I[n]).ndim == 3 else np.asarray(I[n], np.float32)
    out = []
    w = A("w_in")
    pad = np.concatenate([w[:, 3072:3360], np.zeros((1024, 96), np.float32)], 1)
    out += tiles(pad)
    r = tiles(w[:, :3072])
    for p in range(8):
        out += [r[p], r[8 + p], r[16 + p]]
    out += tiles(A("rwkv_w_o"))
    q = tiles(w[:, 3360:6432])
    for h in range(8):
        out += [q[h], q[8 + h], q[16 + h]]
    g, o = tiles(w[:, 6432:]), tiles(A("diff_w_o"))
    for t in range(8):
        out += [g[t], g[8 + t], o[t]]
    out += tiles(A("w_out"))
    out += tiles(A("mlp_w1"))
    for t in tiles(A("mlp_w2")):
        out += [t[:, 1024 * j:1024 * j + 1024] for j in range(4)]
    w = A("w_in_2")
    at = {}
    off = 0
    for n, s in zip("aq ak av be dt ag bq bk bv lr bg cq cf ci cg ma mb mc".split(),
                    (512, 512, 512, 4, 4, 512, 256, 256, 512, 16, 512, 512, 512, 512, 512, 1024, 1024, 1024)):
        at[n] = w[:, off:off + s]
        off += s
    small = np.concatenate([at["lr"], at["be"], at["dt"], np.zeros((1024, 104), np.float32)], 1)
    out += tiles(small)
    a = {n: tiles(at[n]) for n in at if n not in ("be", "dt", "lr")}
    for h in range(4):
        out += [a["aq"][h], a["ak"][h], a["av"][h], a["ag"][h]]
    for p in range(2):
        out += [a["bq"][p], a["bk"][p]]
        for h in (2 * p, 2 * p + 1):
            out += [a["bv"][h], a["bg"][h]]
    for h in range(4):
        out += [a["cq"][h], a["cf"][h], a["ci"][h], a["cg"][h]]
    br = [tiles(A("w_br_%s_2" % n)) for n in "abc"]
    for t in range(8):
        for b in range(3):
            out += [a["m" + "abc"[b]][t], br[b][t]]
    out += tiles(A("w_out_2"))
    wg, wu = np.asarray(I["w_gate_2"])[0], np.asarray(I["w_up_2"])[0]
    for e in range(16):
        tg, tu = tiles(wg[e]), tiles(wu[e])
        out += [tg[0], tu[0], tg[1], tu[1]]
    for t in tiles(np.asarray(I["w_down_2"], np.float32).reshape(4096, 1024)):
        out += [t[:, 1024 * j:1024 * j + 1024] for j in range(4)]
    w = A("w_in_3")
    at, off = {}, 0
    for n, s in zip("fq fk fv ff fg mq mk mv mg sq sk sv sg wq wk wv wg".split(),
                    (256, 256, 256, 4, 256, 256, 256, 256, 256, 256, 256, 256, 256, 256, 128, 128, 256)):
        at[n] = w[:, off:off + s]
        off += s
    at["ff"] = np.concatenate([at["ff"], np.zeros((1024, 124), np.float32)], 1)
    a = {n: tiles(v) for n, v in at.items()}
    out += a["ff"]
    for g in "fm":
        for p in range(2):
            out += [a[g + "q"][p], a[g + "k"][p], a[g + "v"][p], a[g + "g"][p]]
    for p in range(2):
        out += [a["sq"][p], a["sk"][p], a["sv"][p], a["sg"][p]]
    out += [a["wv"][0]]
    for p in range(2):
        kp = at["wk"][:, 64 * p:64 * p + 64]
        out += [a["wq"][p], tiles(np.concatenate([kp, kp], 1))[0], a["wg"][p]]
    out += tiles(A("w_out_3"))
    return out


N1 = 3 + 24 + 8 + 24 + 24 + 8 + 32 + 32
N2 = 1 + 16 + 12 + 16 + 48 + 8 + 64 + 32


class Kern:

    def __init__(self, nc, P, ring, psum, arena, cst, par):
        self.nc, self.P, self.ring, self.ps, self.ar = nc, P, ring, psum, arena
        self.c, self.p = cst, par
        self.top = 0
        self.woff = 0

    def sb(self, n):
        a = self.ar[:, self.top:self.top + n]
        self.top += n
        assert self.top <= self.ar.shape[1], (self.top, self.ar.shape)
        return a

    def bank(self, b, n=1):
        return self.ps[:, 512 * b:512 * (b + n)]

    def tt(self, out, a, b, op, *w, eng="dve"):
        e = self.nc.vector if eng == "dve" else self.nc.gpsimd
        return self.P.op(eng, lambda: e.tensor_tensor(out, a, b, op), *w)

    def ts(self, out, a, s1, s2, op0, op1, *w, eng="dve"):
        e = self.nc.vector if eng == "dve" else self.nc.gpsimd
        if op1 is None:
            return self.P.op(eng, lambda: e.tensor_scalar(out, a, s1, None, op0), *w)
        return self.P.op(eng, lambda: e.tensor_scalar(out, a, s1, s2, op0, op1), *w)

    def stt(self, out, a, s, b, op0, op1, *w):
        return self.P.op("dve", lambda: self.nc.vector.scalar_tensor_tensor(out=out, in0=a, scalar=s, in1=b, op0=op0, op1=op1), *w)

    def cp(self, out, a, *w, eng="dve"):
        if eng == "act":
            return self.act(out, a, ACT.Copy, *w)
        e = self.nc.vector if eng == "dve" else self.nc.gpsimd
        return self.P.op(eng, lambda: e.tensor_copy(out, a), *w)

    def ms(self, out, v, *w, eng="dve"):
        e = self.nc.vector if eng == "dve" else self.nc.gpsimd
        return self.P.op(eng, lambda: e.memset(out, v), *w)

    def rec(self, out, a, *w):
        return self.P.op("dve", lambda: self.nc.vector.reciprocal(out, a), *w)

    def red(self, out, a, op, *w, neg=False):
        return self.P.op("dve", lambda: self.nc.vector.tensor_reduce(out, a, AXX, op, negate=neg), *w)

    def scan(self, out, d0, d1, *w):
        return self.P.op("dve", lambda: self.nc.vector.tensor_tensor_scan(out, d0, d1, 0.0, MUL, ADD), *w)

    def cpred(self, out, mask, data, *w):
        return self.P.op("dve", lambda: self.nc.vector.copy_predicated(out, mask, data), *w)

    def act(self, out, a, f, *w, bias=0.0, scale=1.0, accum=None):
        return self.P.op("act", lambda: self.nc.scalar.activation(out, a, f, bias=bias, scale=scale, accum_out=accum), *w)

    def mm(self, out, l, r, start, stop, *w, skip=False):
        return self.P.op("pe", lambda: self.nc.tensor.matmul(out, l, r, start=start, stop=stop, skip_group_check=skip), *w)

    def tr(self, out, a, *w):
        n = a.shape[0]
        return self.P.op("pe", lambda: self.nc.tensor.transpose(out, a, self.c["ident"][0:n, 0:n]), *w)

    def slab(self, n=1024, off=None):
        s = Slab(n, self.woff if off is None else off, len(self.P.slabs))
        if off is None:
            self.woff += n
        self.P.slabs.append(s)
        s.ap = self.ring[:, (s.i % RING) * SLAB:(s.i % RING) * SLAB + n].rearrange("p (k c) -> p k c", c=128)
        return s

    def lin(self, x, T, nk=8, m=128, x0=0, w=()):
        s = self.slab(nk * 128)
        return self.lin_slab(s, x, T, 0, nk, m, x0, w, True)

    def lin_slab(self, s, x, T, k0, nk, m=128, x0=0, w=(), done=False):
        n = 2 if T > 512 else 1
        b, fr = self.P.banks(n)
        hw = T // n
        first = [s.tok, fr, *w]
        for k in range(nk):
            for j in range(n):
                t = self.mm(self.ps[0:m, 512 * (b + j):512 * (b + j) + hw], s.ap[:, k0 + k, 0:m],
                            x[:, (x0 + k) * T + j * hw:(x0 + k) * T + (j + 1) * hw], k == 0, k == nk - 1, *first)
                first = []
        if done:
            s.done = t
        return b, n, t

    def view(self, b, n, T, m0=0, m1=128):
        if n == 1:
            return self.ps[m0:m1, 512 * b:512 * b + T]
        return self.ps[m0:m1, 512 * b:512 * (b + 2)].rearrange("p (a c) -> p a c", a=2)[:, :, 0:T // 2]

    def like(self, ap, n):
        return ap if n == 1 else ap.rearrange("p (a c) -> p a c", a=2)

    def colsum(self, ones, srcs, T, *w, m=128):
        n = 2 if T > 512 else 1
        b, fr = self.P.banks(n)
        first = [fr, *w]
        hw = T // n
        for k, s in enumerate(srcs):
            for j in range(n):
                t = self.mm(self.ps[0:m, 512 * (b + j):512 * (b + j) + hw], ones, s[:, j * hw:(j + 1) * hw],
                            k == 0, k == len(srcs) - 1, *first)
                first = []
        return b, n, t

    def rstd(self, out, b, n, T, scale, eps, tok):
        t = self.act(self.like(out, n), self.view(b, n, T), ACT.Sqrt, tok, scale=scale, bias=eps)
        self.P.free(b, n, t)
        return self.rec(out, out, t)

    def rms(self, x, wcol, out, T, eps, sq, rs, *w):
        for k in range(8):
            t = self.act(sq[:, k * T:(k + 1) * T], x[:, k * T:(k + 1) * T], ACT.Square, *w)
        b, n, t = self.colsum(self.c["ones"], [sq[:, k * T:(k + 1) * T] for k in range(8)], T, t)
        self.rstd(rs, b, n, T, 1.0 / 1024, eps, t)
        for k in range(8):
            t = self.stt(out[:, k * T:(k + 1) * T], x[:, k * T:(k + 1) * T], wcol[:, k:k + 1], rs, MUL, MUL)
        return t

    def lnorm(self, x, g, b_, out, T, eps, sq, rs, *w):
        b, n, t = self.colsum(self.c["ones"], [x[:, k * T:(k + 1) * T] for k in range(8)], T, *w)
        for k in range(8):
            xs = x[:, k * T:(k + 1) * T]
            t = self.stt(xs, self.view(b, n, T), -1.0 / 1024, xs, MUL, ADD, t)
        self.P.free(b, n, t)
        for k in range(8):
            t2 = self.act(sq[:, k * T:(k + 1) * T], x[:, k * T:(k + 1) * T], ACT.Square, t)
        b, n, t = self.colsum(self.c["ones"], [sq[:, k * T:(k + 1) * T] for k in range(8)], T, t2)
        self.rstd(rs, b, n, T, 1.0 / 1024, eps, t)
        for k in range(8):
            xs = x[:, k * T:(k + 1) * T]
            self.stt(xs, xs, g[:, k:k + 1], rs, MUL, MUL)
            t = self.ts(out[:, k * T:(k + 1) * T], xs, b_[:, k:k + 1], None, ADD, None)
        return t

    def phase(self, top):
        self.P.gate(self.P.marks())
        self.top = top


class Slab:
    def __init__(self, n, off, i):
        self.n, self.off, self.i = n, off, i
        self.tok, self.done = Tok("slab"), None


def block1(K, xT, x_tok=None):
    P, c, p, T = K.P, K.c, K.p, T1
    base = K.top
    oy = K.sb(8 * T)
    h = K.sb(8 * T)
    out = oy[:, 0:4096]
    mark = K.top
    hres = K.sb(8 * T)
    sq = K.sb(8 * T)
    rs = K.sb(T)
    ld = P.dma(hres, xT)
    th = K.rms(hres, p["nmix"], h, T, c["eps5"], sq, rs, ld, x_tok)
    K.phase(mark)

    omka = K.sb(8)
    K.ts(omka, p["k_a"], -1.0, 1.0, MUL, ADD)
    lora = [K.sb(T) for _ in range(3)]
    sh = [K.sb(T + 4) for _ in range(3)]
    dd = [K.sb(T) for _ in range(3)]
    for s in sh:
        tz = K.ms(s[:, 0:1], 0.0)
    dsh = dict((n, K.sb(T)) for n in ("k", "cum", "pm", "e", "a", "at", "bt", "kt"))
    sets = [dict(dsh, r=K.sb(T), v=K.sb(T), rt=K.sb(T), pc=K.sb(8)) for _ in range(2)]
    fin = [K.sb(T) for _ in range(2)]
    toks = dict((n, K.sb(NCH * 128)) for n in ("V", "B", "Kh", "At"))
    unit = [dict((n, K.sb(T)) for n in ("M0", "AT", "Mb", "Ak", "Mk", "X", "XT", "Y")) for _ in range(2)]
    for u in unit:
        u["AV"], u["U0"] = K.sb(NCH * 64), K.sb(NCH * 64)
    WT = unit[0]["M0"]
    St = [K.sb(64) for _ in range(2)]
    tsh = [None] * 3

    def shifted(i, b, n, tok, mu, out, rows=128):
        s = sh[i]
        t = K.act(K.like(s[0:rows, 1:T + 1], n), K.view(b, n, T, 0, rows), ACT.Copy, tok, tz, tsh[i])
        P.free(b, n, t)
        K.tt(dd[i][0:rows], s[0:rows, 0:T], s[0:rows, 1:T + 1], SUB, t)
        tsh[i] = K.stt(out[0:rows], dd[i][0:rows], mu[0:rows], s[0:rows, 1:T + 1], MUL, ADD)
        return tsh[i]

    for i, (mu, rows) in enumerate(((p["muwa"][:, 0:1], 128), (p["mug"][:, 0:1], 128), (p["mug"][:, 1:2], 32))):
        b, n, t = K.lin(h, T, m=rows, w=[th])
        t = shifted(i, b, n, t, mu, lora[i], rows)
        if i == 0:
            tl = K.act(lora[0][0:64], lora[0][0:64], ACT.Tanh, t)
        else:
            tl = K.act(lora[i][0:rows], lora[i][0:rows], ACT.Sigmoid, t)

    up = c["sup"][0:CH, 0:CH].unsqueeze(1).to_broadcast([CH, NCH, CH])
    upi = c["triu"][0:CH, 0:CH].unsqueeze(1).to_broadcast([CH, NCH, CH])
    lo = c["slo"][0:CH, 0:CH].unsqueeze(1).to_broadcast([CH, NCH, CH])
    EH = math.exp(-0.5)

    def bc(ap):
        return ap.unsqueeze(1).to_broadcast([CH, NCH, CH])

    def u3(ap):
        return ap[0:CH, 0:T].rearrange("p (c t) -> p c t", c=NCH)

    def ps4(b):
        return K.ps[0:CH, 512 * b:512 * (b + 2)].rearrange("p (a c) -> p a c", a=2)[:, :, 0:264]

    def blk(b, ci, rows=slice(0, CH), w=CH):
        o = 512 * (b + ci // 3) + (ci % 3) * w
        return K.ps[rows, o:o + w]

    def h2(ap):
        return ap.rearrange("p (a t) -> p a t", a=2)

    def glin(x, w=()):
        s = K.slab()
        b, fr = P.banks(2)
        P.held |= {b, b + 1}
        first = [s.tok, fr, *w]
        for k in range(8):
            for j in range(2):
                t = K.mm(K.ps[:, 512 * (b + j):512 * (b + j) + 264], s.ap[:, k, :],
                         x[:, k * T + j * 264:k * T + (j + 1) * 264], k == 0, k == 7, *first)
                first = []
            if k % 2 and k < 7:
                yield
        s.done = t
        P.held -= {b, b + 1}
        return b, 2, t

    def prep(hp, m2):
        d = sets[hp % 2]
        col = slice(hp, hp + 1)
        P.gate(m2, ("act", "dve"))
        for i, nme in enumerate("rkv"):
            b, n, t = yield from glin(h)
            shifted(i, b, n, t, p["mu"][:, 8 * i + hp:8 * i + hp + 1], d[nme])
            if nme == "k":
                K.ts(dd[0], d["k"], p["k_k"][:, col], None, MUL, None)
                tkk = K.tt(dd[1], dd[0], dd[0], MUL)
            yield
            if nme == "k":
                b, n, t = K.colsum(c["oblk"], [dd[1]], T, tkk)
                t = K.act(h2(fin2), K.view(b, n, T), ACT.Sqrt, t)
                P.free(b, n, t)
                K.ts(fin2, fin2, 1e-12, None, MAX, None, t)
                K.rec(fin2, fin2)
                K.tt(dd[0], dd[0], fin2, MUL)
        b, fr = P.banks(2)
        for j in range(2):
            t = K.mm(K.ps[:, 512 * (b + j):512 * (b + j) + 264], p["w2a2"][0:64, 128 * hp:128 * hp + 128],
                     lora[0][0:64, 264 * j:264 * j + 264], True, True, fr, tl)
        t = K.act(h2(d["e"]), K.view(b, 2, T), ACT.Sigmoid, t, bias=p["w0"][:, col])
        P.free(b, 2, t)
        b, fr = P.banks(2)
        for j in range(2):
            t2 = K.mm(K.ps[:, 512 * (b + j):512 * (b + j) + 264], p["w2a2"][64:128, 128 * hp:128 * hp + 128],
                      lora[0][64:128, 264 * j:264 * j + 264], True, True, fr)
        ta = K.act(h2(d["a"]), K.view(b, 2, T), ACT.Sigmoid, t2, bias=p["a0"][:, col])
        P.free(b, 2, ta)
        K.scan(d["cum"], c["rst88"], d["e"], t)
        t1 = K.tt(d["pm"], d["cum"], d["e"], SUB)
        tpm = K.act(d["pm"], d["pm"], ACT.Exp, t1, scale=-EH)
        K.act(d["e"], d["cum"], ACT.Exp, scale=EH)
        tcum = K.act(d["cum"], d["cum"], ACT.Exp, scale=-EH)
        yield
        K.ts(dd[1], d["a"], p["k_a"][:, col], omka[:, col], MUL, ADD, ta)
        K.tt(d["k"], d["k"], dd[1], MUL)
        K.tt(dd[1], dd[0], d["a"], MUL)
        K.stt(d["at"], dd[0], -1.0, d["pm"], MUL, MUL, tpm)
        yield
        K.tt(d["bt"], dd[1], d["e"], MUL, tcum)
        K.tt(d["kt"], d["k"], d["e"], MUL)
        K.tt(d["rt"], d["r"], d["cum"], MUL)
        yield
        K.cp(d["pc"][:, 0:NCH].unsqueeze(2), d["cum"].rearrange("p (c t) -> p c t", c=NCH)[:, :, CH - 1:CH])
        K.stt(d["r"], d["r"], p["r_k"][:, col], d["k"], MUL, MUL)
        pcb = d["pc"][:, 0:NCH].unsqueeze(2).to_broadcast([128, NCH, CH])
        v3 = lambda x: x.rearrange("p (c t) -> p c t", c=NCH)
        K.tt(v3(d["e"]), v3(d["bt"]), pcb, MUL)
        d["tq"] = K.tt(v3(d["pm"]), v3(d["kt"]), pcb, MUL)

    def finish(hp, by, ty, tprev):
        d = sets[hp % 2]
        col = slice(hp, hp + 1)
        y, s1 = fin
        t = K.act(h2(y), K.view(by, 2, T), ACT.Copy, ty, tprev)
        P.free(by, 2, t)
        yield
        b, n, tr2 = K.colsum(c["oblk"], [d["r"]], T)
        b2, n, t = K.colsum(c["oblk"], [y], T, t)
        t = K.stt(h2(y), K.view(b2, n, T), -1.0 / 64, h2(y), MUL, ADD, t)
        P.free(b2, n, t)
        t = K.act(s1, y, ACT.Square, t)
        tv = K.tt(h2(d["v"]), h2(d["v"]), K.view(b, n, T), MUL, tr2)
        P.free(b, n, tv)
        yield
        yield
        b, n, t = K.colsum(c["oblk"], [s1], T, t)
        K.rstd(s1, b, n, T, 1.0 / 64, c["epsgn"], t)
        K.tt(y, y, s1, MUL)
        K.ts(y, y, p["ln_w"][:, col], p["ln_b"][:, col], MUL, ADD)
        K.tt(y, y, d["v"], ADD)
        yield
        yield
        b, fr = P.banks(2)
        for j in range(2):
            o = K.ps[:, 512 * (b + j):512 * (b + j) + 264]
            J = slice(264 * j, 264 * j + 264)
            K.mm(o, p["g2a"][:, 128 * hp:128 * hp + 128], lora[1][:, J], True, False, fr)
            t = K.mm(o, p["g2b"][0:32, 128 * hp:128 * hp + 128], lora[2][0:32, J], False, True)
        d["toy"] = K.tt(h2(oy[:, T * hp:T * hp + T]), h2(y), K.view(b, 2, T), MUL, t)
        P.free(b, 2, d["toy"])

    work = []

    def step():
        while work:
            try:
                next(work[0])
                return
            except StopIteration:
                work.pop(0)

    def drain():
        while work:
            step()

    fin2 = dd[2]
    work.append(prep(0, P.marks()))
    drain()
    mscan = None
    for hp in range(8):
        d = sets[hp % 2]
        pc, tq = d["pc"], d["tq"]
        if mscan:
            P.gate(mscan, ("act", "dve"))
        tt_ = {}
        for nme, src in (("V", d["v"]), ("At", d["at"]), ("B", d["e"]), ("Kh", d["pm"])):
            b, fr = P.banks(2)
            for ci in range(NCH):
                o = 512 * (b + ci // 3) + (ci % 3) * 128
                t = K.tr(K.ps[0:CH, o:o + 128], src[:, CH * ci:CH * ci + CH], fr, tq)
            pv = K.ps[0:CH, 512 * b:512 * (b + 2)].rearrange("p (a c) -> p a c", a=2)[:, :, 0:384]
            tt_[nme] = K.act(h2(toks[nme][0:CH]), pv, ACT.Copy, t)
            P.free(b, 2, tt_[nme])
            step()
        ttok = tt_["Kh"]
        tu = {}
        for hh in range(2):
            u = unit[hh]
            R = slice(64 * hh, 64 * hh + 64)
            for nme, l, r, msk in (("AT", "bt", "at", None), ("X", "at", "bt", "l1"), ("Ak", "kt", "at", "sup"),
                                   ("Mb", "bt", "rt", "triu"), ("Mk", "kt", "rt", "triu")):
                b, fr = P.banks(2)
                for ci in range(NCH):
                    S = slice(CH * ci, CH * ci + CH)
                    t = K.mm(blk(b, ci), d[l][R, S], d[r][R, S], True, True, fr, tq)
                pin = ps4(b)
                if msk is None:
                    t2 = K.act(h2(u[nme][0:CH]), pin, ACT.Copy, t)
                else:
                    mk = c[msk][0:CH, 0:CH].unsqueeze(1).to_broadcast([CH, 3, CH])
                    for a in range(2):
                        t2 = K.tt(u[nme][0:CH, 264 * a:264 * a + 264].rearrange("p (c t) -> p c t", c=3),
                                  pin[:, a].rearrange("p (c t) -> p c t", c=3), mk, MUL, t)
                P.free(b, 2, t2)
                tu[nme] = t2
                step()
            b, fr = P.banks(1)
            for ci in range(NCH):
                t = K.mm(K.ps[0:CH, 512 * b + 64 * ci:512 * b + 64 * ci + 64], u["Ak"][0:CH, CH * ci:CH * ci + CH],
                         toks["V"][0:CH, 128 * ci + 64 * hh:128 * ci + 64 * hh + 64], True, True, fr, tu["Ak"], tt_["V"])
            tav = K.cp(u["AV"][0:CH], K.ps[0:CH, 512 * b:512 * b + 384], t, eng="act")
            P.free(b, 1, tav)
            u["tav"] = tav
            idb = bc(c["ident"][0:CH, 0:CH])
            K.tt(u3(u["X"]), u3(u["X"]), idb, ADD)
            K.tt(u3(u["XT"]), u3(u["AT"]), bc(c["u1"][0:CH, 0:CH]), MUL, tu["AT"])
            K.tt(u3(u["XT"]), u3(u["XT"]), idb, ADD)
            u["tx"] = u["tm"] = K.tt(u3(u["M0"]), u3(u["AT"]), bc(c["u2"][0:CH, 0:CH]), MUL)
        drain()
        if hp < 7:
            work.append(prep(hp + 1, P.marks()))
        for l in (2, 4, 8, 16):
            for hh in range(2):
                u = unit[hh]
                MT = u["M0"] if l in (2, 8) else u["Ak"]
                b, fr = P.banks(2)
                for ci in range(NCH):
                    S = slice(CH * ci, CH * ci + CH)
                    t = K.mm(blk(b, ci), MT[0:CH, S], u["X"][0:CH, S], True, True, fr, u["tm"], u["tx"])
                u["ty"] = K.act(h2(u["Y"][0:CH]), ps4(b), ACT.Copy, t)
                P.free(b, 2, u["ty"])
                if l < 16:
                    MN = u["Ak"] if l in (2, 8) else u["M0"]
                    u["tm"] = K.tt(u3(MN), u3(u["AT"]), bc(c[f"u{2 * l}"][0:CH, 0:CH]), MUL, u["tav"])
            step()
            for hh in range(2):
                u = unit[hh]
                bz, fr = P.banks(2)
                for ci in range(NCH):
                    S = slice(CH * ci, CH * ci + CH)
                    tz_ = K.mm(blk(bz, ci), u["XT"][0:CH, S], u["Y"][0:CH, S], True, True, fr, u["ty"])
                b, fr = P.banks(2)
                for ci in range(NCH):
                    S = slice(CH * ci, CH * ci + CH)
                    t = K.mm(blk(b, ci), u["Y"][0:CH, S], u["XT"][0:CH, S], True, True, fr, u["ty"])
                x = K.tt(h2(u["X"][0:CH]), h2(u["X"][0:CH]), ps4(bz), ADD, tz_, t)
                P.free(bz, 2, x)
                u["tx"] = K.tt(h2(u["XT"][0:CH]), h2(u["XT"][0:CH]), ps4(b), ADD, t)
                P.free(b, 2, u["tx"])
            step()
        for l, w in ((32, 32), (64, CH - 64)):
            L_, H_ = slice(0, l), slice(l, l + w)

            def pw(b, rows, width):
                return K.ps[rows, 512 * b:512 * b + NCH * width].rearrange("p (c t) -> p c t", c=NCH)

            for hh in range(2):
                u = unit[hh]
                b, fr = P.banks(1)
                for ci in range(NCH):
                    t = K.mm(K.ps[H_, 512 * b + l * ci:512 * b + l * ci + l], u["AT"][L_, CH * ci + l:CH * ci + l + w],
                             u["X"][L_, CH * ci:CH * ci + l], True, True, fr, u["tx"])
                u["ty"] = K.act(u3(u["Y"])[H_, :, 0:l], pw(b, H_, l), ACT.Copy, t)
                P.free(b, 1, u["ty"])
            step()
            for hh in range(2):
                u = unit[hh]
                if l < 64:
                    bz, fr = P.banks(1)
                    for ci in range(NCH):
                        tz_ = K.mm(K.ps[H_, 512 * bz + l * ci:512 * bz + l * ci + l], u["XT"][H_, CH * ci + l:CH * ci + l + w],
                                   u["Y"][H_, CH * ci:CH * ci + l], True, True, fr, u["ty"])
                b, fr = P.banks(1)
                for ci in range(NCH):
                    t = K.mm(K.ps[L_, 512 * b + w * ci:512 * b + w * ci + w], u["Y"][H_, CH * ci:CH * ci + l],
                             u["XT"][H_, CH * ci + l:CH * ci + l + w], True, True, fr, u["ty"])
                if l < 64:
                    x = K.tt(u3(u["X"])[H_, :, 0:l], u3(u["X"])[H_, :, 0:l], pw(bz, H_, l), ADD, tz_, t)
                    P.free(bz, 1, x)
                u["tx"] = K.tt(u3(u["XT"])[L_, :, l:l + w], u3(u["XT"])[L_, :, l:l + w], pw(b, L_, w), ADD, t)
                P.free(b, 1, u["tx"])
            step()
        b, fr = P.banks(2)
        for hh in range(2):
            u = unit[hh]
            for ci in range(NCH):
                S = slice(CH * ci, CH * ci + CH)
                t = K.mm(blk(b, ci, slice(64 * hh, 64 * hh + 64)), toks["At"][0:CH, 128 * ci + 64 * hh:128 * ci + 64 * hh + 64],
                         u["XT"][0:CH, S], True, True, fr, u["tx"], ttok)
        tw = K.act(h2(WT), K.view(b, 2, T), ACT.Copy, t)
        P.free(b, 2, tw)
        for hh in range(2):
            u = unit[hh]
            b, fr = P.banks(1)
            for ci in range(NCH):
                t = K.mm(K.ps[0:CH, 512 * b + 64 * ci:512 * b + 64 * ci + 64], u["XT"][0:CH, CH * ci:CH * ci + CH],
                         u["AV"][0:CH, 64 * ci:64 * ci + 64], True, True, fr, u["tx"])
            u["tu"] = K.cp(u["U0"][0:CH], K.ps[0:CH, 512 * b:512 * b + 384], t)
            P.free(b, 1, u["tu"])
        by, fry = P.banks(2)
        P.held |= {by, by + 1}
        tS = None
        for ci in range(NCH):
            S = slice(CH * ci, CH * ci + CH)
            so = St[ci % 2]
            sn = St[(ci + 1) % 2]
            tuu = []
            for hh in range(2):
                u = unit[hh]
                R = slice(64 * hh, 64 * hh + 64)
                if ci:
                    b, fr = P.banks(1)
                    t = K.mm(K.ps[0:CH, 512 * b:512 * b + 64], WT[R, S], so[R, :], True, True, fr, tS, tw)
                    us = u["U0"][0:CH, 64 * ci:64 * ci + 64]
                    t = K.tt(us, us, K.ps[0:CH, 512 * b:512 * b + 64], ADD, t)
                    P.free(b, 1, t)
                    tuu.append(t)
                else:
                    tuu.append(u["tu"])
            step()
            if ci < NCH - 1:
                b, fr = P.banks(1)
                for hh in range(2):
                    u = unit[hh]
                    R = slice(64 * hh, 64 * hh + 64)
                    C = slice(128 * ci + 64 * hh, 128 * ci + 64 * hh + 64)
                    o = K.ps[R, 512 * b:512 * b + 64]
                    K.mm(o, toks["Kh"][0:CH, C], toks["V"][0:CH, C], True, False, fr, ttok)
                    t = K.mm(o, toks["B"][0:CH, C], u["U0"][0:CH, 64 * ci:64 * ci + 64], False, True, tuu[hh])
                o = K.ps[:, 512 * b:512 * b + 64]
                if ci:
                    tSn = K.stt(sn, so, pc[:, ci:ci + 1], o, MUL, ADD, t, ty2)
                else:
                    tSn = K.cp(sn, o, t)
                P.free(b, 1, tSn)
                step()
            for hh in range(2):
                u = unit[hh]
                R = slice(64 * hh, 64 * hh + 64)
                o = blk(by, ci, R)
                C = slice(128 * ci + 64 * hh, 128 * ci + 64 * hh + 64)
                K.mm(o, toks["V"][0:CH, C], u["Mk"][0:CH, S], True, False, fry, tu["Mk"])
                t = K.mm(o, u["U0"][0:CH, 64 * ci:64 * ci + 64], u["Mb"][0:CH, S], False, ci == 0, tuu[hh])
                if ci:
                    t = K.mm(o, so[R, :], d["rt"][R, S], False, True)
            ty2 = t
            tS = tSn
            step()
        drain()
        P.held -= {by, by + 1}
        f = finish(hp, by, ty2, sets[(hp + 1) % 2].get("toy"))
        next(f)
        mscan = P.marks()
        work.append(f)
    drain()
    K.phase(mark)

    orw = K.sb(8 * T)
    od = K.sb(8 * T)
    for k in range(8):
        b, n, t = K.lin(oy, T)
        t = K.act(h2(orw[:, k * T:k * T + T]), K.view(b, n, T), ACT.Copy, t)
        P.free(b, n, t)
    torw = t
    lam = K.sb(8)
    lt = K.sb(64)
    K.tt(lt, p["lq1"], p["lk1"], MUL)
    K.red(lam[:, 0:1], lt, ADD)
    K.tt(lt, p["lq2"], p["lk2"], MUL)
    t = K.red(lam[:, 1:2], lt, ADD)
    t = K.act(lam[:, 2:4], lam[:, 0:2], ACT.Exp, t)
    K.stt(lam[:, 4:5], lam[:, 2:3], -1.0, lam[:, 3:4], MUL, ADD, t)
    K.ts(lam[:, 4:5], lam[:, 4:5], -0.2, None, ADD, None)
    K.ts(lam[:, 5:6], p["subln"], 0.8, None, MUL, None)
    bufs = [dict((n, K.sb(w)) for n, w in (
        ("q", T), ("k", T), ("t1", T), ("t2", T), ("V", 5 * 128), ("P0", T), ("P1", T), ("P2", T), ("P3", T),
        ("aw0", 512), ("aw1", 512), ("am", 256), ("O", T), ("sc", 64))) for _ in range(2)]
    TK = [(0, 16)] + [(16 + 128 * j, 128) for j in range(4)]
    old = [None, None]
    tqv = {}

    def project(hd):
        d = bufs[hd % 2]
        if old[hd % 2]:
            P.gate(old[hd % 2], ("act", "dve"))
        for nme in "qk":
            b, n, t = yield from glin(h)
            t = K.act(h2(d[nme]), K.view(b, n, T), ACT.Copy, t, scale=0.125 if nme == "q" else 1.0)
            P.free(b, n, t)
            K.tt(d["t1"], d[nme], c["cos"], MUL, t)
            yield
            b, n, t2 = K.colsum(c["rot"], [d[nme]], T, t)
            t3 = K.tt(h2(d["t2"]), K.view(b, n, T), h2(c["sin"]), MUL, t2)
            P.free(b, n, t3)
            tqk = K.tt(d[nme], d["t1"], d["t2"], ADD)
        s = K.slab()
        b, fr = P.banks(2)
        P.held |= {b, b + 1}
        for j, (t0, tw_) in enumerate(TK):
            o = K.ps[0:tw_, 512 * b + 512 * (j > 0) + 128 * max(j - 1, 0):512 * b + 512 * (j > 0) + 128 * max(j - 1, 0) + 128]
            for k in range(8):
                t = K.mm(o, h[:, k * T + t0:k * T + t0 + tw_], s.ap[:, k, :], k == 0, k == 7, fr, s.tok)
            yield
        s.done = t
        K.act(d["V"][0:16, 0:128], K.ps[0:16, 512 * b:512 * b + 128], ACT.Copy, t)
        tV = K.act(d["V"][:, 128:640], K.ps[:, 512 * b + 512:512 * b + 1024], ACT.Copy)
        P.free(b, 2, tV)
        P.held -= {b, b + 1}
        tqv[hd] = (tqk, tV)

    def scores(hd, i):
        d = bufs[hd % 2]
        q0, qw = TK[i]
        W = q0 + qw
        nb = 2 if W > 512 else 1
        pr = []
        for sub in range(2):
            R = slice(64 * sub, 64 * sub + 64)
            b, fr = P.banks(nb)
            m0 = 512 * b + (496 if nb == 2 else 0)
            sm = K.ps[0:qw, m0:m0 + 16]
            sn = K.ps[0:qw, m0 + 16:m0 + max(W, 17)]
            if nb == 2 or i == 0:
                K.mm(sm, d["q"][R, q0:q0 + qw], d["k"][R, 0:16], True, i > 0, fr, tqv[hd])
                if i == 0:
                    t = K.mm(sm, c["ident"][0:16, 0:16], c["negm"][0:16, 0:16], False, True)
                else:
                    K.mm(sn[:, 0:W - 144], d["q"][R, q0:q0 + qw], d["k"][R, 16:W - 128], True, True)
            else:
                K.mm(K.ps[0:qw, m0:m0 + W - 128], d["q"][R, q0:q0 + qw], d["k"][R, 0:W - 128], True, True, fr, tqv[hd])
            if i:
                K.mm(sn[:, W - 144:W - 16], d["q"][R, q0:q0 + qw], d["k"][R, W - 128:W], True, False)
                t = K.mm(sn[:, W - 144:W - 16], c["ident"], c["negm"], False, True)
            s_ = K.ps[0:qw, m0:m0 + W]
            sc = d["sc"][0:qw, 6 * i + 3 * sub:6 * i + 3 * sub + 3]
            Pt = d[f"P{2 * (i % 2) + sub}"][0:qw, 0:W]
            t = K.red(sc[:, 0:1], s_, MAX, t, neg=True)
            t = K.act(Pt, s_, ACT.Exp, t, bias=sc[:, 0:1], accum=sc[:, 1:2])
            P.free(b, nb, t)
            pr.append((Pt, sc, t))
        K.rec(pr[0][1][:, 2:3], pr[0][1][:, 1:2], pr[0][2])
        K.rec(pr[1][1][:, 2:3], pr[1][1][:, 1:2], t)
        K.tt(pr[1][1][:, 2:3], pr[1][1][:, 2:3], lam[0:qw, 4:5], MUL)
        K.ts(pr[1][0], pr[1][0], pr[1][1][:, 2:3], None, MUL, None)
        return pr[0][0], K.stt(pr[0][0], pr[0][0], pr[0][1][:, 2:3], pr[1][0], MUL, ADD)

    def values(hd, i, aw, t):
        d = bufs[hd % 2]
        q0, qw = TK[i]
        nb = 2 if i == 4 else 1
        b, fr = P.banks(nb)
        m0 = 512 * b if i == 4 else 512 * b + 128 * i
        n0 = 512 * (b + 1) if i == 4 else 512 * b
        t2 = K.tr(K.ps[0:16, m0:m0 + qw], aw[:, 0:16], fr, t)
        for j in range(1, i + 1):
            t2 = K.tr(K.ps[:, n0 + 128 * (j - 1):n0 + 128 * j], aw[:, TK[j][0]:TK[j][0] + 128])
        a = d[f"aw{i % 2}"]
        am = d["am"][0:16, 128 * (i % 2):128 * (i % 2) + qw]
        t3 = K.act(am, K.ps[0:16, m0:m0 + qw], ACT.Copy, t2)
        if i:
            t3 = K.act(a[:, 0:128 * i], K.ps[:, n0:n0 + 128 * i], ACT.Copy)
        P.free(b, nb, t3)
        step()
        bo, fro = d["bo"]
        o = K.ps[:, 512 * bo + 496 + q0:512 * bo + 496 + q0 + qw]
        tO = K.mm(o, d["V"][0:16, 0:128], am, True, i == 0, fro, t3)
        for j in range(1, i + 1):
            tO = K.mm(o, d["V"][:, 128 * j:128 * j + 128], a[:, 128 * (j - 1):128 * j], False, j == i)
        if i < 4:
            return None
        t = K.act(d["O"], K.ps[:, 512 * bo + 496:512 * bo + 1024], ACT.Copy, tO)
        P.free(bo, 2, t)
        P.held -= {bo, bo + 1}
        t = K.act(d["t2"], d["O"], ACT.Square)
        step()
        b, n, t = K.colsum(c["ones"], [d["t2"]], T, t)
        K.rstd(d["t1"], b, n, T, 1.0 / 128, c["eps5"], t)
        tod = K.stt(od[:, hd * T:hd * T + T], d["O"], lam[:, 5:6], d["t1"], MUL, MUL)
        old[hd % 2] = P.marks()
        if hd < 6:
            work.append(project(hd + 2))
        return tod

    work.append(project(0))
    drain()
    work.append(project(1))
    behind = None
    for hd in range(8):
        while hd not in tqv:
            step()
        for i in range(5):
            cur = (hd, i, *scores(hd, i))
            step()
            if behind:
                tod = values(*behind)
            if i == 0:
                bufs[hd % 2]["bo"] = P.banks(2)
                P.held |= {bufs[hd % 2]["bo"][0], bufs[hd % 2]["bo"][0] + 1}
            step()
            behind = cur
    tod = values(*behind)
    drain()
    mg = oy
    sg = [K.sb(T) for _ in range(2)]
    K.P.gate(P.marks())
    for k in range(8):
        b, n, t = K.lin(h, T)
        t0 = K.act(h2(sg[0]), K.view(b, n, T), ACT.Sigmoid, t, P.last["dve"])
        P.free(b, n, t0)
        b, n, t = K.lin(h, T)
        t1 = K.act(h2(sg[1]), K.view(b, n, T), ACT.Sigmoid, t)
        P.free(b, n, t1)
        b, n, t = K.lin(od, T, w=[tod])
        K.tt(sg[0], sg[0], orw[:, k * T:k * T + T], MUL, t0)
        t = K.tt(h2(sg[1]), h2(sg[1]), K.view(b, n, T), MUL, t, t1)
        P.free(b, n, t)
        tm = K.tt(mg[:, k * T:k * T + T], sg[0], sg[1], ADD)
    hres = orw
    ld = P.dma(hres, xT, tm)
    for k in range(8):
        b, n, t = K.lin(mg, T, w=[tm])
        t = K.tt(h2(hres[:, k * T:k * T + T]), h2(hres[:, k * T:k * T + T]), K.view(b, n, T), ADD, t, ld)
        P.free(b, n, t)
    tr_ = t
    K.phase(mark + 8 * T)
    rs = K.sb(T)
    th = K.rms(hres, p["nmlp"], h, T, c["eps5"], oy, rs, tr_)
    rl = [K.sb(T) for _ in range(2)]
    H = K.sb(32 * T)
    tsq = [tr_, tr_]
    for k in range(32):
        b, n, t = K.lin(h, T, w=[th])
        t = K.act(h2(rl[k % 2]), K.view(b, n, T), ACT.Relu, t, tsq[k % 2])
        P.free(b, n, t)
        tr_ = tsq[k % 2] = K.tt(H[:, k * T:k * T + T], rl[k % 2], rl[k % 2], MUL, t)
    for k in range(8):
        b, fr = P.banks(2)
        first = [fr, tr_]
        for g in range(4):
            s = K.slab()
            for kk_ in range(8):
                for j in range(2):
                    kx = 8 * g + kk_
                    t = K.mm(K.ps[:, 512 * (b + j):512 * (b + j) + 264], s.ap[:, kk_, :],
                             H[:, kx * T + 264 * j:kx * T + 264 * j + 264], kx == 0, kx == 31, s.tok, *first)
                    first = []
            s.done = t
        t = K.tt(h2(hres[:, k * T:k * T + T]), h2(hres[:, k * T:k * T + T]), K.view(b, 2, T), ADD, t)
        P.free(b, 2, t)
    th = K.rms(hres, p["fin"], h, T, c["eps5"], oy, rs, t)
    for k in range(8):
        t = K.cp(out[:, k * 512:k * 512 + 512], h[:, k * T + 16:k * T + T], th, eng="pool")
    K.phase(base + 8 * 512)
    return out, t


def block2(K, x, x_tok):
    P, c, p, T = K.P, K.c, K.p, T2
    h = K.sb(8 * T)
    O = K.sb(12 * T)
    rs = K.sb(T)
    th = K.lnorm(x, p["ln0_g"], p["ln0_b"], h, T, c["eps5"], O, rs, x_tok)
    mark = K.top

    def bc4(ap):
        return ap.unsqueeze(1).to_broadcast([128, 4, 128])

    def v4(ap):
        return ap.rearrange("p (j t) -> p j t", j=4)

    def evac(out, b, t, f=ACT.Copy, *w, **kw):
        t = K.act(out, K.bank(b), f, t, *w, **kw)
        P.free(b, 1, t)
        return t

    now = [None]

    def slab_of():
        s = K.slab(off=now[0][1])
        now[0][1] += 1024
        return s

    def glin(w=()):
        s = slab_of()
        b, fr = P.banks(1)
        P.held.add(b)
        for k in range(8):
            t = K.mm(K.bank(b), s.ap[:, k, :], h[:, k * T:k * T + T], k == 0, k == 7, fr, s.tok, *w)
            if k in (2, 5):
                yield
        s.done = t
        P.held.discard(b)
        return b, 1, t

    def v_tile(out):
        s = slab_of()
        b, fr = P.banks(1)
        P.held.add(b)
        for j in range(4):
            for k in range(8):
                t = K.mm(K.bank(b)[:, 128 * j:128 * j + 128], h[:, k * T + 128 * j:k * T + 128 * j + 128], s.ap[:, k, :],
                         k == 0, k == 7, fr, s.tok)
            if j < 3:
                yield
        s.done = t
        P.held.discard(b)
        return evac(out, b, t)

    def gated(bo, tO, ncol, gate, out, o, q, r):
        t = evac(o, bo, tO)
        P.held.discard(bo)
        t = K.act(q, o, ACT.Square)
        yield
        b, n, t = K.colsum(c["ones"], [q], T, t)
        K.rstd(r, b, n, T, 1.0 / 128, c["eps6"], t)
        K.stt(o, o, ncol, r, MUL, MUL)
        return K.tt(out, o, gate, MUL)

    s = K.slab()
    LR = K.sb(T)
    b, n, t = K.lin_slab(s, h, T, 0, 8, 16, w=[th])
    tlr = K.act(LR[0:16], K.ps[0:16, 512 * b:512 * b + T], ACT.Copy, t)
    P.free(b, 1, tlr)
    b, fr = P.banks(1)
    for j in range(4):
        for k in range(8):
            t = K.mm(K.bank(b)[:, 8 * j:8 * j + 8], h[:, k * T + 128 * j:k * T + 128 * j + 128], s.ap[:, k, 16:24], k == 0, k == 7, fr)
    s.done = t
    sm = K.bank(b)[:, 0:32].rearrange("p (j e) -> p j e", e=8)
    G = {n: K.sb(16) for n in ("be", "nbe", "v", "sp", "g", "cu", "to", "ec", "el", "eks", "bec", "ea", "s", "s2")}
    g4 = lambda n: G[n].rearrange("p (j e) -> p j e", e=4)
    t = K.act(g4("be"), sm[:, :, 0:4], ACT.Sigmoid, t)
    t = K.tt(g4("v"), sm[:, :, 4:8], p["dtb"].unsqueeze(1).to_broadcast([128, 4, 4]), ADD, t)
    P.free(b, 1, t)
    K.act(G["sp"], G["v"], ACT.Abs, t)
    K.act(G["sp"], G["sp"], ACT.Exp, scale=-1.0)
    t = K.act(G["ea"][:, 0:4], p["alog"], ACT.Exp)
    K.ts(G["s"], G["sp"], 2.0, None, ADD, None, t)
    K.rec(G["s"], G["s"])
    K.tt(G["s"], G["s"], G["sp"], MUL)
    K.tt(G["s2"], G["s"], G["s"], MUL)
    K.ts(G["sp"], G["s2"], 1.0 / 17, None, MUL, None)
    for k in (15, 13, 11, 9, 7, 5, 3):
        K.stt(G["sp"], G["sp"], 1.0 / k, G["s2"], ADD, MUL)
    K.stt(G["sp"], G["sp"], 1.0, G["s"], ADD, MUL)
    K.ts(G["s2"], G["v"], 0.0, None, MAX, None)
    K.stt(G["sp"], G["sp"], 2.0, G["s2"], MUL, ADD)
    t = K.stt(g4("g"), g4("sp"), -1.0, G["ea"][:, 0:4].unsqueeze(1).to_broadcast([128, 4, 4]), MUL, MUL)
    b, fr = P.banks(1)
    K.mm(K.bank(b)[:, 0:16], c["triu"], G["g"], True, True, fr, t)
    t = K.mm(K.bank(b)[:, 16:32], c["ones"], G["g"], True, True)
    K.cp(G["cu"], K.bank(b)[:, 0:16], t)
    t = K.cp(G["to"], K.bank(b)[:, 16:32])
    P.free(b, 1, t)
    K.tt(G["eks"], G["to"], G["cu"], SUB)
    t = K.ts(G["nbe"], G["be"], -1.0, None, MUL, None)
    K.act(G["ec"], G["cu"], ACT.Exp, t)
    K.act(G["el"], G["to"], ACT.Exp)
    t = K.act(G["eks"], G["eks"], ACT.Exp)
    K.tt(G["bec"], G["be"], G["ec"], MUL, t)
    CT = K.sb(128)
    b, fr = P.banks(1)
    t = K.tr(K.bank(b)[0:16, 0:128], G["cu"], fr, P.last["dve"])
    tct = K.cp(CT[0:16], K.bank(b)[0:16, 0:128], t)
    P.free(b, 1, tct)
    s16 = c["sel16"].rearrange("p (e j) -> p e j", e=16)
    keep = K.top

    pad = [K.sb(516) for _ in range(2)]
    for q in pad:
        tz = K.ms(q[:, 0:3], 0.0)
    U = {n: K.sb(T) for n in ("q", "k", "v", "g", "er", "D", "DT", "A", "AT", "X", "XT", "MT", "Y", "M", "VB", "KB", "KS", "qi", "u", "wT",
                              "n0", "n1")}
    St = [K.sb(128) for _ in range(2)]
    def delta():
        old = None
        for hd in range(4):
            if old:
                P.gate(old, ("act", "dve"))
            tp = {}
            tcv = [None, None]
            for i, nme in enumerate("qkv"):
                b, n, t = yield from glin([th])
                pp = pad[i % 2]
                t = K.act(pp[:, 3:515], K.bank(b), ACT.Copy, t, tz, tcv[i % 2])
                P.free(b, 1, t)
                w = p["conv"][:, 16 * i + 4 * hd:16 * i + 4 * hd + 4]
                K.ts(U[nme], pp[:, 0:512], w[:, 0:1], None, MUL, None, t)
                for k in range(1, 4):
                    t = K.stt(U[nme], pp[:, k:k + 512], w[:, k:k + 1], U[nme], MUL, ADD)
                tcv[i % 2] = t
                tp[nme] = K.act(U[nme], U[nme], ACT.Silu, t)
                if nme != "v":
                    sq_, r_ = ("n0", "n1") if nme == "q" else ("u", "wT")
                    t = K.act(U[sq_], U[nme], ACT.Square)
                    yield
                    b, n, t = K.colsum(c["ones"], [U[sq_]], T, t)
                    K.rstd(U[r_], b, n, T, 1.0, c["eps6"], t)
                    tp[nme] = K.stt(U[nme], U[nme], 128.0 ** -0.5 if nme == "q" else 1.0, U[r_], MUL, MUL)
            b, n, t = yield from glin()
            tg = evac(U["g"], b, t, ACT.Silu)
            yield
            b, fr = P.banks(1)
            for j in range(4):
                t = K.mm(K.bank(b)[:, 128 * j:128 * j + 128], s16[0:16, 4 * j + hd, :], CT[0:16], True, True, fr, tct)
            ter = K.act(U["er"], K.bank(b), ACT.Exp, t)
            for j in range(4):
                J = slice(128 * j, 128 * j + 128)
                cu = G["cu"][:, 4 * j + hd:4 * j + hd + 1]
                K.ts(U["D"][:, J], K.bank(b)[:, J], cu, 0.0, SUB, MAX, ter)
                t = K.ts(U["DT"][:, J], K.bank(b)[:, J], cu, 0.0, SUB, MIN)
            P.free(b, 1, t)
            K.act(U["D"], U["D"], ACT.Exp, t, scale=-1.0)
            t = K.act(U["DT"], U["DT"], ACT.Exp)
            K.tt(v4(U["D"]), v4(U["D"]), bc4(c["slo"]), MUL, t)
            K.tt(v4(U["DT"]), v4(U["DT"]), bc4(c["triu"]), MUL)
            t = K.tt(U["qi"], U["q"], U["er"], MUL)
            yield
            b, fr = P.banks(1)
            for j in range(4):
                J = slice(128 * j, 128 * j + 128)
                t = K.mm(K.bank(b)[:, J], U["k"][:, J], U["k"][:, J], True, True, fr, tp["k"], t)
            for j in range(4):
                J = slice(128 * j, 128 * j + 128)
                ta = K.stt(U["A"][:, J], K.bank(b)[:, J], G["nbe"][:, 4 * j + hd:4 * j + hd + 1], U["D"][:, J], MUL, MUL, t)
            P.free(b, 1, ta)
            b, fr = P.banks(1)
            for j in range(4):
                J = slice(128 * j, 128 * j + 128)
                t = K.mm(K.bank(b)[:, J], U["k"][:, J], U["q"][:, J], True, True, fr)
            tM = K.tt(U["M"], K.bank(b), U["DT"], MUL, t)
            P.free(b, 1, tM)
            for src in "vk":
                b, fr = P.banks(1)
                for j in range(4):
                    J = slice(128 * j, 128 * j + 128)
                    t = K.tr(K.bank(b)[:, J], U[src][:, J], fr, tp["v"])
                for j in range(4):
                    J = slice(128 * j, 128 * j + 128)
                    cc = slice(4 * j + hd, 4 * j + hd + 1)
                    if src == "v":
                        t = K.ts(U["VB"][:, J], K.bank(b)[:, J], G["be"][:, cc], None, MUL, None, t)
                    else:
                        K.ts(U["KB"][:, J], K.bank(b)[:, J], G["bec"][:, cc], None, MUL, None, t)
                        t = K.ts(U["KS"][:, J], K.bank(b)[:, J], G["eks"][:, cc], None, MUL, None)
                P.free(b, 1, t)
            tkb = t
            yield
            b, fr = P.banks(1)
            for j in range(4):
                J = slice(128 * j, 128 * j + 128)
                t = K.tr(K.bank(b)[:, J], U["A"][:, J], fr, ta)
            tat = K.cp(U["AT"], K.bank(b), t)
            P.free(b, 1, tat)
            for X, A, m in (("X", "A", "l1"), ("XT", "AT", "u1")):
                K.tt(v4(U[X]), v4(U[A]), bc4(c[m]), MUL)
                tx = K.tt(v4(U[X]), v4(U[X]), bc4(c["ident"]), ADD)

            def four(l, r, *w):
                b, fr = P.banks(1)
                for j in range(4):
                    J = slice(128 * j, 128 * j + 128)
                    t = K.mm(K.bank(b)[:, J], U[l][:, J], U[r][:, J], True, True, fr, *w)
                return b, t

            yield
            tm = K.tt(v4(U["MT"]), v4(U["AT"]), bc4(c["u2"]), MUL)
            ms_ = ("MT", "D")
            tl2 = None
            for i, l in enumerate(LEVELS[1:-1]):
                b, t = four(ms_[i % 2], "X", tm, tx)
                ty = evac(U["Y"], b, t)
                if l < 32:
                    tm = K.tt(v4(U[ms_[(i + 1) % 2]]), v4(U["AT"]), bc4(c[f"u{2 * l}"]), MUL, tl2, tat, tx, eng="pool")
                tl2 = t
                yield
                bz, tz2 = four("XT", "Y", ty)
                t3 = K.tt(U["X"], U["X"], K.bank(bz), ADD, tz2, tz2)
                P.free(bz, 1, t3)
                b, t2 = four("Y", "XT", ty)
                tx = K.tt(U["XT"], U["XT"], K.bank(b), ADD, t2)
                P.free(b, 1, tx)
                yield
            b, fr = P.banks(1)
            for j in range(4):
                t = K.mm(K.ps[64:128, 512 * b + 64 * j:512 * b + 64 * j + 64], U["AT"][0:64, 128 * j + 64:128 * j + 128],
                         U["X"][0:64, 128 * j:128 * j + 64], True, True, fr, tx)
            ty = K.act(v4(U["Y"])[64:128, :, 0:64], K.ps[64:128, 512 * b:512 * b + 256].rearrange("p (j t) -> p j t", j=4),
                       ACT.Copy, t)
            P.free(b, 1, ty)
            yield
            b, fr = P.banks(1)
            for j in range(4):
                t = K.mm(K.ps[0:64, 512 * b + 64 * j:512 * b + 64 * j + 64], U["Y"][64:128, 128 * j:128 * j + 64],
                         U["XT"][64:128, 128 * j + 64:128 * j + 128], True, True, fr, ty)
            tx = K.tt(v4(U["XT"])[0:64, :, 64:128], v4(U["XT"])[0:64, :, 64:128],
                      K.ps[0:64, 512 * b:512 * b + 256].rearrange("p (j t) -> p j t", j=4), ADD, t)
            P.free(b, 1, tx)
            yield
            b, t = four("XT", "VB", tx, tkb)
            tu = K.cp(U["u"], K.bank(b), t)
            P.free(b, 1, tu)
            b, t = four("KB", "XT")
            tw = evac(U["wT"], b, t)
            bo, fro = P.banks(1)
            P.held.add(bo)
            yield
            tS = None
            tO = None
            for j in range(4):
                J = slice(128 * j, 128 * j + 128)
                so, sn = St[j % 2], St[(j + 1) % 2]
                tv = tu
                if j:
                    b, fr = P.banks(1)
                    t = K.mm(K.bank(b)[:, 0:128], U["wT"][:, J], so, True, True, fr, tS, tw)
                    tv = K.tt(U["u"][:, J], U["u"][:, J], K.bank(b)[:, 0:128], SUB, t)
                    P.free(b, 1, tv)
                yield
                if j < 3:
                    b, fr = P.banks(1)
                    t = K.mm(K.bank(b)[:, 0:128], U["KS"][:, J], U["u"][:, J], True, True, fr, tv)
                    if j:
                        tn = K.stt(sn, so, G["el"][:, 4 * j + hd:4 * j + hd + 1], K.bank(b)[:, 0:128], MUL, ADD, t, tO)
                    else:
                        tn = K.cp(sn, K.bank(b)[:, 0:128], t)
                    P.free(b, 1, tn)
                    yield
                o = K.bank(bo)[:, J]
                tO = K.mm(o, U["u"][:, J], U["M"][:, J], True, j == 0, fro, tv, tM)
                if j:
                    tO = K.mm(o, so, U["qi"][:, J], False, True)
                tS = tn
            yield from gated(bo, tO, p["gdnn"], U["g"], O[:, hd * T:hd * T + T], U["n0"], U["n1"], U["D"])
            old = P.marks()

    W = {n: x[:, i * T:i * T + T] for i, n in enumerate(("q", "k", "cum", "E", "Q", "Kz", "ks", "la"))}
    W.update((n, K.sb(T)) for n in ("t0", "t1", "n0", "n1", "n2"))
    V = [K.sb(T) for _ in range(2)]
    Gt = [K.sb(T) for _ in range(2)]
    acc = [K.sb(T) for _ in range(2)]
    Sg = [K.sb(128) for _ in range(2)]
    el = K.sb(8)
    u32 = mybir.dt.uint32

    oldg = []

    def decay_attention(heads, rows, tqk, tv, tg, ncol, out0):
        for i in range(heads):
            K.ms(acc[i], 0.0)
        def decays(n, l):
            nb = T // (2 * l)
            cu, E = (W[x].rearrange("p (b t) -> p b t", t=2 * l) for x in ("cum", "E"))
            ref = cu[:, :, l - 1:l].to_broadcast([128, nb, l])
            K.tt(E[:, :, l:2 * l], cu[:, :, l:2 * l], ref, SUB, tE[0])
            t = K.tt(E[:, :, 0:l], ref, cu[:, :, 0:l], SUB)
            te = K.act(W["E"], W["E"], ACT.Exp, t)
            qn, kn = (("Q", "Kz"), ("n0", "n1"))[n % 2]
            K.tt(W[qn], W["q"], W["E"], MUL, te, tmm[n % 2])
            tE[0] = K.tt(W[kn], W["k"], W["E"], MUL, te, tqk, tmm[n % 2], eng="pool")
            return kn, qn, [tE[0], P.last["dve"]]

        tmm, tE = [None, None], [None]
        lv = (0,) + LEVELS[::-1]
        nxt = ("k", "q", tqk)
        for n, l in enumerate(lv):
            a, bb, t = nxt
            got = []
            for i in range(heads):
                R = slice(rows * i, rows * i + rows)
                b, fr = P.banks(1)
                for j in range(4):
                    J = slice(128 * j, 128 * j + 128)
                    tl = K.mm(K.bank(b)[:, J], W[a][R, J], W[bb][R, J], True, True, fr, t)
                got.append((b, tl))
            if n:
                tmm[n % 2] = tl
            if n + 1 < len(lv):
                nxt = decays(n + 1, lv[n + 1])
            m = c[f"u{l}"] if l else c["ident"]
            for i, (b, tl) in enumerate(got):
                ta = K.cpred(v4(acc[i]), bc4(m.bitcast(u32)), v4(K.bank(b)), tl)
                P.free(b, 1, ta)
            yield
        cu = v4(W["cum"])
        t = K.tt(v4(W["E"]), cu[:, :, 127:128].to_broadcast([128, 4, 128]), cu, SUB, tE[0])
        K.act(W["E"], W["E"], ACT.Exp, t)
        K.act(el[:, 0:4].unsqueeze(2), cu[:, :, 127:128], ACT.Exp)
        t = K.act(W["cum"], W["cum"], ACT.Exp)
        K.tt(W["Kz"], W["k"], W["E"], MUL, t, tl)
        t = K.tt(W["Q"], W["q"], W["cum"], MUL)
        yield
        b, fr = P.banks(1)
        for j in range(4):
            J = slice(128 * j, 128 * j + 128)
            t2 = K.tr(K.bank(b)[:, J], W["Kz"][:, J], fr, t)
        tks = evac(W["ks"], b, t2)
        bo = []
        for i in range(heads):
            b, fro = P.banks(1)
            P.held.add(b)
            bo.append((b, fro))
        yield
        tS, tn, tO = None, None, None
        for j in range(4):
            J = slice(128 * j, 128 * j + 128)
            so, sn = Sg[j % 2], Sg[(j + 1) % 2]
            if j < 3:
                b, fr = P.banks(1)
                for i in range(heads):
                    R = slice(rows * i, rows * i + rows)
                    t = K.mm(K.ps[R, 512 * b:512 * b + 128], W["ks"][:, 128 * j + rows * i:128 * j + rows * i + rows], V[i][:, J],
                             True, True, fr, tks, tv)
                if j:
                    tn = K.stt(sn, so, el[:, j:j + 1], K.bank(b)[:, 0:128], MUL, ADD, t, tO)
                else:
                    tn = K.cp(sn, K.bank(b)[:, 0:128], t)
                P.free(b, 1, tn)
                yield
            for i in range(heads):
                R = slice(rows * i, rows * i + rows)
                o = K.bank(bo[i][0])[:, J]
                tO = K.mm(o, V[i][:, J], acc[i][:, J], True, j == 0, bo[i][1], ta, tv)
                if j:
                    tO = K.mm(o, so[R, :], W["Q"][R, J], False, True, tS)
            tS = tn
        for i in range(heads):
            yield from gated(bo[i][0], tO, ncol, Gt[i], O[:, (out0 + i) * T:(out0 + i) * T + T],
                  *((W["n0"], W["n1"], W["n2"]) if i == 0 else (W["la"], W["t0"], W["t1"])))
        oldg.append(P.marks())

    def linear():
        for pr in range(2):
            if oldg:
                P.gate(oldg[-1], ("act", "dve"))
            b, n, t = yield from glin()
            evac(W["q"], b, t, ACT.Copy, scale=0.125)
            b, n, t = yield from glin()
            tqk = evac(W["k"], b, t)
            for i in range(2):
                tv = yield from v_tile(V[i])
                b, n, t = yield from glin()
                tg = evac(Gt[i], b, t, ACT.Silu)
            b, fr = P.banks(1)
            t = K.mm(K.bank(b), p["glaw2"][0:16, 128 * pr:128 * pr + 128], LR[0:16], True, True, fr, tlr)
            logsig(K, W["la"], K.bank(b), p["glab2"][:, pr:pr + 1], (W["t0"], W["t1"], None), t, b)
            K.ts(W["la"], W["la"], 1.0 / 16, None, MUL, None)
            K.scan(W["cum"], c["rst128"], W["la"])
            yield
            yield from decay_attention(2, 64, tqk, tv, tg, p["glan"], 4 + 2 * pr)

        L = {n: K.sb(4) for n in ("m", "e", "r", "lb", "om", "llb", "l1")}
        K.tt(L["m"], p["lb"], p["lb"], MAX)
        t = K.tt(L["e"], p["lb"], L["m"], SUB)
        t = K.act(L["e"], L["e"], ACT.Exp, t)
        K.rec(L["r"], L["e"], t)
        K.tt(L["e"], L["e"], L["r"], MUL)
        K.tt(L["lb"], L["e"], L["e"], SUB)
        K.ts(L["lb"], L["lb"], 0.0, 1.0, MAX, MIN)
        K.ts(L["om"], L["lb"], -1.0, 1.0, MUL, ADD)
        t = K.ts(L["llb"], L["lb"], 1e-30, None, MAX, None)
        K.act(L["llb"], L["llb"], ACT.Sqrt, t)
        K.act(L["llb"], L["llb"], ACT.Ln)
        t = K.act(L["l1"], L["om"], ACT.Ln)
        K.ts(L["llb"], L["llb"], 2.0, None, MUL, None, t)
        for hd in range(4):
            H1 = slice(hd, hd + 1)
            P.gate(oldg[-1], ("act", "dve"))
            b, n, t = yield from glin()
            t = evac(W["q"], b, t, ACT.Silu)
            K.ts(W["q"], W["q"], 128.0 ** -0.5, None, MUL, None, t)
            b, n, t = yield from glin()
            K.act(W["k"], K.bank(b), ACT.Sigmoid, t, scale=-1.0)
            t = evac(W["t0"], b, t)
            tqk = K.ts(W["k"], W["k"], L["om"][:, H1], None, MUL, None, t)
            K.act(W["t1"], W["t0"], ACT.Abs)
            K.act(W["t1"], W["t1"], ACT.Exp, scale=-1.0)
            t = K.act(W["t1"], W["t1"], ACT.Ln, bias=c["one"])
            K.stt(W["t0"], W["t0"], 0.0, W["t1"], MIN, SUB, t)
            K.ts(W["t0"], W["t0"], L["l1"][:, H1], None, ADD, None)
            t = K.ts(W["t1"], W["t0"], L["llb"][:, H1], None, SUB, None)
            K.act(W["t1"], W["t1"], ACT.Abs, t)
            K.act(W["t1"], W["t1"], ACT.Exp, scale=-1.0)
            t = K.act(W["t1"], W["t1"], ACT.Ln, bias=c["one"])
            K.stt(W["la"], W["t0"], L["llb"][:, H1], W["t1"], MAX, ADD, t)
            K.scan(W["cum"], c["rst128"], W["la"])
            tv = yield from v_tile(V[0])
            b, n, t = yield from glin()
            tg = evac(Gt[0], b, t, ACT.Silu)
            yield
            yield from decay_attention(1, 128, tqk, tv, tg, p["hgrnn"], 8 + hd)

    runs = [[delta(), K.woff], [linear(), K.woff + 16 * 1024]]
    while runs:
        for r in list(runs):
            now[0] = r
            try:
                next(r[0])
            except StopIteration:
                runs.remove(r)
    K.woff += 44 * 1024
    K.phase(mark)

    y = x
    sg = [K.sb(T) for _ in range(2)]
    tsg = [None, None]
    i = 0
    for k in range(8):
        ys = y[:, k * T:k * T + T]
        for br in range(3):
            b, n, t = K.lin(h, T)
            t = K.act(sg[i % 2], K.bank(b), ACT.Sigmoid, t, tsg[i % 2])
            P.free(b, 1, t)
            b, n, t2 = K.lin(O, T, nk=4, x0=4 * br)
            if br == 0:
                tsg[i % 2] = K.tt(ys, sg[i % 2], K.bank(b), MUL, t, t2)
                P.free(b, 1, tsg[i % 2])
            else:
                t = K.tt(sg[i % 2], sg[i % 2], K.bank(b), MUL, t, t2)
                P.free(b, 1, t)
                tsg[i % 2] = ty = K.tt(ys, ys, sg[i % 2], ADD)
            i += 1
    for k in range(8):
        hs = h[:, k * T:k * T + T]
        b, n, t = K.lin(y, T, w=[ty])
        t = K.stt(hs, hs, ALPHA, K.bank(b), MUL, ADD, t)
        P.free(b, 1, t)
    th = K.lnorm(h, p["ln1_g"], p["ln1_b"], x, T, c["eps5"], O, rs, t)

    R = {n: K.sb(64) for n in ("sc", "sel", "gs", "tmp", "f", "kp", "w", "cnt")}
    e3 = lambda n: R[n].rearrange("p (a e) -> p a e", e=4)
    b, fr = P.banks(1)
    for j in range(4):
        for k in range(8):
            t = K.mm(K.bank(b)[:, 16 * j:16 * j + 16], x[:, k * T + 128 * j:k * T + 128 * j + 128], p["wr"][:, 16 * k:16 * k + 16],
                     k == 0, k == 7, fr, th)
    t = K.act(R["sc"], K.bank(b)[:, 0:64], ACT.Sigmoid, t)
    P.free(b, 1, t)
    K.tt(R["sel"].rearrange("p (j e) -> p j e", e=16), R["sc"].rearrange("p (j e) -> p j e", e=16),
         p["rb"].unsqueeze(1).to_broadcast([128, 4, 16]), ADD, t)
    sel = [e3("sel")[:, :, e] for e in range(4)]
    gs, tmp = R["gs"][:, 0:16], R["tmp"][:, 0:16]
    first = True
    for a in range(4):
        for b_ in range(a + 1, 4):
            K.tt(gs if first else tmp, sel[a], sel[b_], ADD)
            if not first:
                K.tt(gs, gs, tmp, MAX)
            first = False
    gs3 = gs.rearrange("p (j g) -> p j g", g=4)
    K.red(R["tmp"][:, 16:20], gs3, MAX)
    f3 = R["f"][:, 0:16].rearrange("p (j g) -> p j g", g=4)
    K.tt(f3, gs3, R["tmp"][:, 16:20].unsqueeze(2).to_broadcast([128, 4, 4]), ALU.is_ge)
    left = R["tmp"][:, 20:24]
    K.ms(left, 1.0)
    for g in range(4):
        K.tt(f3[:, :, g], f3[:, :, g], left, MUL)
        K.tt(left, left, f3[:, :, g], SUB)
    for e in range(4):
        cnt = R["cnt"][:, 16 * e:16 * e + 16]
        n = 0
        for k in range(4):
            if k != e:
                K.tt(tmp if n else cnt, sel[k], sel[e], ALU.is_ge if k < e else ALU.is_gt)
                if n:
                    K.tt(cnt, cnt, tmp, ADD)
                n += 1
        K.stt(e3("kp")[:, :, e], cnt, 1.5, R["f"][:, 0:16], ALU.is_lt, MUL)
    K.tt(R["w"], R["kp"], R["sc"], MUL)
    w3 = R["w"].rearrange("p (j e) -> p j e", e=16)
    K.red(R["tmp"][:, 24:28], w3, ADD)
    K.rec(R["tmp"][:, 28:32], R["tmp"][:, 24:28])
    t = K.tt(w3, w3, R["tmp"][:, 28:32].unsqueeze(2).to_broadcast([128, 4, 16]), MUL)
    cT = K.sb(T)
    b, fr = P.banks(1)
    for j in range(4):
        t2 = K.tr(K.bank(b)[0:16, 128 * j:128 * j + 128], R["w"][:, 16 * j:16 * j + 16], fr, t)
    tc = K.cp(cT[0:16], K.bank(b)[0:16, :], t2)
    P.free(b, 1, tc)

    H = K.sb(32 * T)
    sg = [K.sb(T) for _ in range(2)]
    tsg = [None, None]
    for e in range(16):
        bc_, fr = P.banks(1)
        tcb = K.mm(K.bank(bc_), s16[0:16, e, :], cT[0:16], True, True, fr, tc)
        P.held = {bc_}
        for f in range(2):
            b, n, t = K.lin(x, T)
            t = K.act(sg[f], K.bank(b), ACT.Silu, t, tsg[f])
            P.free(b, 1, t)
            b, n, t2 = K.lin(x, T)
            t = K.tt(sg[f], sg[f], K.bank(b), MUL, t, t2)
            P.free(b, 1, t)
            tsg[f] = K.tt(H[:, (2 * e + f) * T:(2 * e + f + 1) * T], sg[f], K.bank(bc_), MUL, tcb)
        P.free(bc_, 1, tsg[1])
        P.held = set()
    th = tsg[1]
    for k in range(8):
        b, fr = P.banks(1)
        for g in range(4):
            s = K.slab()
            for kk in range(8):
                kx = 8 * g + kk
                t = K.mm(K.bank(b), s.ap[:, kk, :], H[:, kx * T:kx * T + T], kx == 0, kx == 31, s.tok, fr, th)
            s.done = t
        t = K.stt(h[:, k * T:k * T + T], x[:, k * T:k * T + T], ALPHA, K.bank(b), MUL, ADD, t)
        P.free(b, 1, t)
    t = K.lnorm(h, p["ln2_g"], p["ln2_b"], x, T, c["eps5"], O, rs, t)
    K.phase(mark - 21 * T)
    return x, t


def block3(K, x, x_tok):
    P, c, p, T = K.P, K.c, K.p, T2
    nc = K.nc
    h = K.sb(8 * T)
    y = K.sb(8 * T)
    sq = y
    rs = K.sb(T)
    th = K.rms(x, p["ng3"], h, T, c["eps6"], sq, rs, x_tok)
    small = K.sb(32)
    g8 = {}
    for i, n in enumerate(("foxg", "mobag", "swag")):
        K.ts(small[:, i:i + 1], p[n][:, 0:1], 0.125, None, MUL, None)
        g8[n] = (small[:, i:i + 1], p[n][:, 1:2])

    C4, Cn, Z4 = K.sb(T), K.sb(T), [K.sb(T) for _ in range(3)]
    one4 = K.sb(T)
    K.ms(one4[0:4], 1.0)
    b, n, t = K.lin(h, T, m=4, w=[th])
    logsig(K, C4[0:4], K.ps[0:4, 512 * b:512 * b + T], p["bf"][0:4, 0:1], [z[0:4] for z in Z4], t, b)
    tc = K.scan(Cn[0:4], one4[0:4], C4[0:4])

    vec = [K.sb(640) for _ in range(2)]
    rb = K.sb(128)
    table = [K.sb(512 if i < 4 else 256) for i in range(8)]
    ttab = []
    for i in range(8):
        v = vec[i % 2]
        moba = i < 4
        trb = K.ts(rb[0:32], c["ones"][0:32], p["relb"][0:32, i:i + 1], None, MUL, None, P.last["pe"])
        b, fr = P.banks(1)
        t = K.mm(K.bank(b), rb[0:32, 0:128], c["oh"][0:32], True, True, fr, trb)
        wr = [ttab[-2]] if i >= 2 else []
        if moba:
            K.ms(v[:, 512:640], -1e30, wr)
            t = K.cp(v[:, 0:512], K.bank(b), t)
            W = 640
        else:
            K.ms(v[:, 0:384], -1e30, wr)
            t = K.cp(v[:, 128:256], K.bank(b)[:, 384:512], t)
            W = 384
        P.free(b, 1, t)
        dr = nc.dram_tensor(f"skew{i}", [128 * 640], F32, kind="Internal").ap()
        t = P.dma(dr[0:128 * W].rearrange("(p w) -> p w", w=W), v[:, 0:W], t)
        n = 512 if moba else 256
        rd = dr[127:127 + 128 * (W - 1)].rearrange("(p w) -> p w", w=W - 1)[:, 0:n]
        ttab.append(P.dma(table[i][:, 0:n], rd, t))

    bufs = [dict((n, K.sb(w)) for n, w in (
        ("q", T), ("k", T), ("V", T), ("g", T), ("s0", T), ("s1", T), ("P0", T), ("P1", T), ("t0", T), ("t1", T),
        ("sc", 64))) for _ in range(2)]
    vt = K.sb(T)
    old = [None, None]

    now = [None]

    def slab_of():
        s = K.slab(off=now[0][1])
        now[0][1] += 1024
        return s

    def glin():
        s = slab_of()
        b, fr = P.banks(1)
        P.held.add(b)
        for k in range(8):
            t = K.mm(K.bank(b), s.ap[:, k, :], h[:, k * T:k * T + T], k == 0, k == 7, fr, s.tok)
            if k in (1, 3, 5):
                yield
        s.done = t
        P.held.discard(b)
        return b, t

    def qk_tile(d, nme, gain):
        b, t = yield from glin()
        if gain is None:
            t = K.act(d[nme], K.bank(b), ACT.Copy, t, scale=0.125 if nme == "q" else 1.0)
            P.free(b, 1, t)
            return t
        t = K.act(d[nme], K.bank(b), ACT.Copy, t)
        P.free(b, 1, t)
        s0, s1 = (d["s0"], d["s1"]) if nme == "q" else (d["P0"], d["P1"])
        t = K.act(s0, d[nme], ACT.Square)
        yield
        b, n, t = K.colsum(c["oblk"], [s0], T, t)
        K.rstd(s1, b, n, T, 1.0 / 64, c["eps6"], t)
        return K.stt(d[nme], d[nme], gain, s1, MUL, MUL)

    def v_tile(out, fr_tok=None):
        s = slab_of()
        b, fr = P.banks(1)
        P.held.add(b)
        for j in range(4):
            for k in range(8):
                t = K.mm(K.bank(b)[:, 128 * j:128 * j + 128], h[:, k * T + 128 * j:k * T + 128 * j + 128], s.ap[:, k, :],
                         k == 0, k == 7, fr, s.tok)
            if j < 3:
                yield
        s.done = t
        P.held.discard(b)
        t = K.act(out, K.bank(b), ACT.Copy, t, fr_tok)
        P.free(b, 1, t)
        return t

    def gate_tile(d):
        b, t = yield from glin()
        t = K.act(d["g"], K.bank(b), ACT.Silu, t)
        P.free(b, 1, t)
        return t

    def scores(d, kind, r, i, hd, tqk):
        R = slice(64 * r, 64 * r + 64)
        q = d["q"][R, 128 * i:128 * i + 128]
        k0 = max(0, i - 1) if kind == "swa" else 0
        W = 128 * (i + 1 - k0)
        b, fr = P.banks(1)
        s_ = K.bank(b)[:, 0:W]
        t = K.mm(s_, q, d["k"][R, 128 * k0:128 * (i + 1)], True, False, fr, tqk)
        if kind == "fox":
            K.mm(s_, Cn[0:4, 128 * i:128 * i + 128], s16[0:4, hd, 0:1].to_broadcast([4, W]), False, False, tc, tsel)
            K.mm(s_, seln[0:4, 128 * hd:128 * hd + 128], Cn[0:4, 0:W], False, True)
            t = K.mm(s_[:, W - 128:W], c["ident"], c["negm"], False, True, skip=True)
        elif kind == "moba":
            t = K.mm(s_, c["ident"], table[hd][:, 512 - W:512], False, True, ttab[hd])
        else:
            t = K.mm(s_, c["ident"], table[4 + hd][:, 256 - W:256], False, True, ttab[4 + hd])
        sc = d["sc"][:, 32 * r + 8 * i:32 * r + 8 * i + 8]
        Pt = d[f"P{i % 2}"][:, 0:W]
        if kind == "swa":
            K.red(sc[:, 3:4], s_, MAX, t)
            t = K.ts(sc[:, 0:1], sc[:, 3:4], p["sinks"][:, hd:hd + 1], -1.0, MAX, MUL)
        else:
            t = K.red(sc[:, 0:1], s_, MAX, t, neg=True)
        t = K.act(Pt, s_, ACT.Exp, t, bias=sc[:, 0:1], accum=sc[:, 1:2])
        P.free(b, 1, t)
        if kind == "swa":
            t = K.act(sc[:, 4:5], p["sinks"][:, hd:hd + 1], ACT.Exp, bias=sc[:, 0:1])
            K.tt(sc[:, 1:2], sc[:, 1:2], sc[:, 4:5], ADD, t)
        K.rec(sc[:, 2:3], sc[:, 1:2], t)
        return r, i, k0, W, Pt, K.ts(Pt, Pt, sc[:, 2:3], None, MUL, None)

    def values(d, V, vcol, bo, fro, tv, r, i, k0, W, Pt, t):
        b, fr = P.banks(1)
        nb = W // 128
        for j in range(nb):
            t2 = K.tr(K.bank(b)[:, 128 * j:128 * j + 128], Pt[:, 128 * j:128 * j + 128], fr, t)
        a = d[f"t{i % 2}"]
        t3 = K.cp(a[:, 0:W], K.bank(b)[:, 0:W], t2, eng="act")
        P.free(b, 1, t3)
        yield
        for j in range(nb):
            tO = K.mm(K.ps[64 * r:64 * r + 64, 512 * bo + 128 * i:512 * bo + 128 * i + 128],
                      V[:, 128 * (k0 + j) + vcol[r]:128 * (k0 + j) + vcol[r] + 64], a[:, 128 * j:128 * j + 128],
                      j == 0, j == nb - 1, t3, tv, fro)
        return tO

    def softmax_pair(d, kind, V, vcol, hd, tqk, tv, bo, fro):
        behind = None
        for r in range(2):
            for i in range(4):
                cur = scores(d, kind, r, i, hd + r, tqk)
                yield
                if behind:
                    yield from values(d, V, vcol, bo, fro, tv, *behind)
                behind = cur
        return (yield from values(d, V, vcol, bo, fro, tv, *behind))

    seln = K.sb(4 * 128)
    s16 = c["sel16"].rearrange("p (e j) -> p e j", e=16)
    for e in range(4):
        tsel = K.ts(seln[0:4, 128 * e:128 * e + 128], s16[0:4, e, :], -1.0, None, MUL, None)

    def start(i):
        if old[i]:
            P.gate(old[i], ("act", "dve"))
        return bufs[i]

    def out_bank():
        bo, fro = P.banks(1)
        P.held.add(bo)
        return bo, fro

    def finish(i, d, bo, tO, tile, tg):
        t = K.tt(y[:, T * tile:T * tile + T], d["g"], K.bank(bo), MUL, tO, tg)
        P.free(bo, 1, t)
        P.held.discard(bo)
        old[i] = P.marks()
        return t

    def dense():
        for gi, kind in enumerate(("fox", "moba")):
            for pr in range(2):
                d = start(0)
                gq, gk = g8[kind + "g"]
                yield from qk_tile(d, "q", gq)
                yield
                tqk = yield from qk_tile(d, "k", gk)
                yield
                tv = yield from v_tile(d["V"])
                tg = yield from gate_tile(d)
                yield
                bo, fro = out_bank()
                tO = yield from softmax_pair(d, kind, d["V"], (0, 64), 2 * pr, tqk, tv, bo, fro)
                finish(0, d, bo, tO, 2 * gi + pr, tg)

    Lk = [K.sb(T) for _ in range(4)]
    Zk = Z4 + [C4]

    def sticks(pr):
        d = start(1)
        yield from qk_tile(d, "q", None)
        tqk = yield from qk_tile(d, "k", None)
        tv = yield from v_tile(d["V"])
        tg = yield from gate_tile(d)
        yield
        bo, fro = out_bank()
        tdv, tpe = tc, None
        for r in range(2):
            R = slice(64 * r, 64 * r + 64)
            for j in range(4):
                W = 512 - 128 * j
                b, fr = P.banks(1)
                t = K.mm(K.bank(b)[:, 0:W], d["k"][R, 128 * j:128 * j + 128], d["q"][R, 128 * j:512], True, True, fr, tqk)
                z, lk = Zk[j][:, 0:W], Lk[j][:, 0:W]
                s0, s1 = (d["s0"], d["s1"]) if j % 2 == 0 else (d["P0"], d["P1"])
                s0, s1 = s0[:, 0:W], s1[:, 0:W]
                t = K.act(z, K.bank(b)[:, 0:W], ACT.Copy, t, tdv)
                P.free(b, 1, t)
                K.act(s0, z, ACT.Abs, tpe)
                K.act(s0, s0, ACT.Exp, scale=-1.0)
                t = K.act(s0, s0, ACT.Ln, bias=c["one"])
                K.stt(s1, z, 0.0, s0, MAX, ADD, t)
                K.tt(z, z, s1, SUB)
                K.ts(lk, s1, -1.0, None, MUL, None, tpe)
                tl = K.tt(lk[:, 0:128], lk[:, 0:128], c["sup"], MUL)
                if j:
                    tdv = tlast
                tlast = tl
                yield
            for j in range(4):
                W = 512 - 128 * j
                b, fr = P.banks(1)
                t = K.mm(K.bank(b)[:, 0:W], c["slo"], Lk[j][:, 0:W], True, True, fr, tl)
                for j2 in range(j + 1, 4):
                    o = 128 * (j2 - j)
                    t = K.mm(K.bank(b)[:, o:W], c["ones"], Lk[j2][:, 0:W - o], False, True, skip=True)
                a = d[f"P{j % 2}"][:, 0:W]
                t = K.tt(a, Zk[j][:, 0:W], K.bank(b)[:, 0:W], ADD, t)
                P.free(b, 1, t)
                t = K.act(d[f"t{j % 2}"][:, 0:W], a, ACT.Exp, t)
                w0 = d[f"t{j % 2}"]
                t = tdv = K.tt(w0[:, 0:128], w0[:, 0:128], c["sup"], MUL, t)
                yield
                tO = tpe = K.mm(K.ps[R, 512 * bo + 128 * j:512 * bo + 512], d["V"][:, 128 * j + 64 * r:128 * j + 64 * r + 64],
                                w0[:, 0:W], j == 0, True, t, tv, fro, skip=j > 0)
        finish(1, d, bo, tO, 4 + pr, tg)

    def local():
        for pr in range(2):
            yield from sticks(pr)
        tv = yield from v_tile(vt)
        for pr in range(2):
            d = start(1)
            gq, gk = g8["swag"]
            yield from qk_tile(d, "q", gq)
            yield
            tqk = yield from qk_tile(d, "k", gk)
            yield
            tg = yield from gate_tile(d)
            yield
            bo, fro = out_bank()
            tO = yield from softmax_pair(d, "swa", vt, (64 * pr, 64 * pr), 2 * pr, tqk, tv, bo, fro)
            finish(1, d, bo, tO, 6 + pr, tg)

    runs = [[dense(), K.woff], [local(), K.woff + 16 * 1024]]
    while runs:
        for r in list(runs):
            now[0] = r
            try:
                next(r[0])
            except StopIteration:
                runs.remove(r)
    K.woff += 31 * 1024
    ty = P.last["dve"]
    for k in range(8):
        b, n, t = K.lin(y, T, w=[ty])
        xs = x[:, k * T:k * T + T]
        t = K.tt(xs, xs, K.bank(b), ADD, t)
        P.free(b, 1, t)
    return x, t


def logsig(K, out, src, bias, tmp, tok, b):
    v, a, e = tmp
    n = v.shape[0]
    t = K.act(v, src, ACT.Identity, tok, bias=bias)
    if b is not None:
        K.P.free(b, 1, t)
    K.act(a, v, ACT.Abs)
    K.act(a, a, ACT.Exp, scale=-1.0)
    t = K.act(a, a, ACT.Ln, bias=K.c["one"][0:n])
    return K.stt(out, v, 0.0, a, MIN, SUB, t)


def layout(inputs):
    I = {k: np.asarray(v) for k, v in inputs.items()}
    x = np.concatenate([I["meta_tokens"], I["x"][0]], 0)
    xT = x.T.reshape(8, 128, T1).transpose(1, 0, 2).reshape(128, 8 * T1)
    con = constants()
    par = pack_params(I)
    return xT, con, par, pack_weights(I)


def program(nc, xT, out, con, par, wall, at, blocks=(1, 2, 3)):
    P = Prog(nc)
    ring = nc.alloc_sbuf_tensor("ring", [128, RING * SLAB], F32)
    nfree = (nc.sbuf_bytes_remaining - 64) // 4 // 8 * 8
    arena = nc.alloc_sbuf_tensor("arena", [128, nfree], F32)
    psum = nc.alloc_psum_tensor("psum", [128, 4096], F32)
    c, p = {}, {}
    K = Kern(nc, P, ring, psum, arena, c, p)
    cb, pb = K.sb(at["ncon"]), K.sb(at["npar"])
    loads = [P.dma(cb, con), P.dma(pb, par)]
    for k, (o, n) in at["con"].items():
        c[k] = cb[:, o:o + n]
    for k, (o, n) in at["par"].items():
        p[k] = pb[:, o:o + n]
    eps = K.sb(8)
    for i, (k, v) in enumerate((("eps5", 1e-5), ("eps6", 1e-6), ("epsgn", 64e-5), ("one", 1.0))):
        c[k] = eps[:, i:i + 1]
        K.ms(c[k], v)
    P.gate(P.marks() + loads)
    base = K.top
    x, t = None, None
    if 1 in blocks:
        x, t = block1(K, xT)
    else:
        x = K.sb(4096)
        t = P.dma(x, xT)
    if 2 in blocks:
        x, t = block2(K, x, t)
    if 3 in blocks:
        x, t = block3(K, x, t)
    P.dma(out, x, t)
    with nc.Block() as block:
        P.emit(wall, ring, block)


def offsets(d):
    off, at = 0, {}
    for k, v in d.items():
        at[k] = (off, v.shape[1])
        off += v.shape[1]
    return at, off


def kernel(**inputs):
    import concourse.bacc as bacc
    from concourse.bass_utils import run_bass_kernel_spmd as run

    xT, con, par, w = layout(inputs)
    at = {}
    at["con"], at["ncon"] = offsets(con)
    at["par"], at["npar"] = offsets(par)
    arrays = {
        "in_x": np.ascontiguousarray(xT, np.float32),
        "in_con": np.ascontiguousarray(np.concatenate(list(con.values()), 1)),
        "in_par": np.ascontiguousarray(np.concatenate(list(par.values()), 1)),
        "in_w": np.concatenate(w, 1),
    }
    nc = bacc.Bacc("TRN2", target_bir_lowering=False, num_devices=1)
    d = {k: nc.dram_tensor(k, list(v.shape), F32, kind="ExternalInput").ap() for k, v in arrays.items()}
    out = nc.dram_tensor("out_0", [128, 8 * 512], F32, kind="ExternalOutput").ap()
    program(nc, d["in_x"], out, d["in_con"], d["in_par"], d["in_w"], at)
    r = run(nc, [arrays], core_ids=[0])
    o = np.asarray(r.results[0]["out_0"]).reshape(128, 8, 512).transpose(1, 0, 2).reshape(1024, 512)
    return np.ascontiguousarray(o.T).reshape(1, 512, 1024)
```

```python
import numpy as np
import concourse.bass as bass
from concourse import mybir

F32 = mybir.dt.float32
F32R = mybir.dt.float32r
ALU = mybir.AluOpType
ACT = mybir.ActivationFunctionType
AXX = mybir.AxisListType.X
MUL, ADD, SUB, MAX, MIN = ALU.mult, ALU.add, ALU.subtract, ALU.max, ALU.min

RING = 7
SLAB = 1024


class Tok:

    def __init__(self, eng):
        self.eng, self.used, self.sem, self.count = eng, False, None, 0


class Prog:

    def __init__(self, nc):
        self.nc = nc
        self.q = {e: [] for e in ("pe", "act", "dve", "pool", "sp")}
        self.last = {}
        self.bank_free = [None] * 8
        self.nbank = 0
        self.held = set()
        self.slabs = []
        self.nsem = 0

    def op(self, eng, fn, *waits):
        t = Tok(eng)
        w = list(flat(waits))
        if eng in ("act", "dve", "pool") and eng in self.last:
            w.append(self.last[eng])
        for x in w:
            if not (x.eng == eng == "pe"):
                x.used = True
        self.q[eng].append((w, fn, t))
        self.last[eng] = t
        return t

    def dma(self, out, in_, *waits, eng="sp"):
        t = Tok("dma")
        t.used = True
        t.sem = self.nc.alloc_semaphore(f"d{self.nsem}")
        t.count = 16
        t.after = len(self.slabs)
        self.nsem += 1
        w = list(flat(waits))
        for x in w:
            x.used = True
        e = self.nc.gpsimd if eng == "pool" else self.nc.sync
        self.q[eng].append((w, lambda: e.dma_start(out, in_).then_inc(t.sem, 16), t))
        return t

    def marks(self):
        m = [self.last[e] for e in ("pe", "act", "dve", "pool") if e in self.last]
        for t in m:
            t.used = True
        return m

    def gate(self, marks, engines=("pe", "act", "dve", "pool")):
        for e in engines:
            self.q[e].append(([t for t in marks if t.eng != e], None, None))

    def banks(self, n=1):
        while (n == 2 and self.nbank % 2) or any((self.nbank + i) % 8 in self.held for i in range(n)):
            self.nbank += 1
        b = self.nbank % 8
        self.nbank += n
        return b, [self.bank_free[b + i] for i in range(n) if self.bank_free[b + i]]

    def free(self, b, n, tok):
        for i in range(n):
            self.bank_free[b + i] = tok

    def emit(self, wall, ring, block):
        nc = self.nc
        slot_sem = [nc.alloc_semaphore(f"slab{i}") for i in range(RING)]
        for n, s in enumerate(self.slabs):
            s.tok.sem, s.tok.count = slot_sem[n % RING], 16 * (n // RING + 1)
        sems = {e: nc.alloc_semaphore(f"s_{e}") for e in ("pe", "act", "dve", "pool")}
        for n, s in enumerate(self.slabs):
            if n >= RING:
                self.slabs[n - RING].done.used = True
        for e, lst in self.q.items():
            c = 0
            for w, fn, t in lst:
                if t is not None and t.eng == e and t.used:
                    c += 1
                    t.sem, t.count = sems[e], c

        def run(e, eng):
            seen = {}

            def waits(w):
                for t in w:
                    if t.eng == e == "pe":
                        continue
                    if seen.get(t.sem.num, 0) < t.count:
                        seen[t.sem.num] = t.count
                        eng.wait_ge(t.sem, t.count)

            for w, fn, t in self.q[e]:
                waits(w)
                if fn is None:
                    continue
                i = fn()
                if t.eng == e and t.used:
                    i.then_inc(t.sem, 1)

        @block.sync
        def _(eng):
            head = [x for x in self.q["sp"] if not x[0]]
            tail = [x for x in self.q["sp"] if x[0]]
            for w, fn, t in head:
                fn()
            places = {}
            for x in tail:
                places.setdefault(x[2].after, []).append(x)
            for n, s in enumerate(self.slabs):
                for w, fn, t in places.get(n, ()):
                    for k in w:
                        eng.wait_ge(k.sem, k.count)
                    fn()
                if n >= RING:
                    d = self.slabs[n - RING].done
                    eng.wait_ge(d.sem, d.count)
                eng.dma_start(ring[:, (n % RING) * SLAB:(n % RING) * SLAB + s.n],
                              wall[:, s.off:s.off + s.n]).then_inc(slot_sem[n % RING], 16)
            for w, fn, t in places.get(len(self.slabs), ()):
                for k in w:
                    eng.wait_ge(k.sem, k.count)
                fn()
                eng.wait_ge(t.sem, t.count)

        @block.tensor
        def _(eng):
            run("pe", eng)

        @block.scalar
        def _(eng):
            run("act", eng)

        @block.vector
        def _(eng):
            run("dve", eng)

        @block.gpsimd
        def _(eng):
            run("pool", eng)


def flat(x):
    for y in x:
        if y is None:
            continue
        if isinstance(y, (list, tuple)):
            yield from flat(y)
        else:
            yield y


T1, T2 = 528, 512
CH, NCH = 88, 6
import math
ALPHA = 2.0 ** 0.25
LEVELS = (1, 2, 4, 8, 16, 32, 64)

def constants():
    i = np.arange(128)
    c = {}
    c["ident"] = np.eye(128)
    c["ones"] = np.ones((128, 128))
    c["oblk"] = (i[:, None] // 64 == i[None, :] // 64) * 1.0
    c["triu"] = (i[:, None] <= i[None, :]) * 1.0
    c["sup"] = (i[:, None] < i[None, :]) * 1.0
    c["slo"] = (i[:, None] > i[None, :]) * 1.0
    c["negm"] = np.where(i[:, None] >= i[None, :], 0.0, -1e30)
    for l in LEVELS:
        same = (i[:, None] // (2 * l)) == (i[None, :] // (2 * l))
        up = same & (i[:, None] % (2 * l) < l) & (i[None, :] % (2 * l) >= l)
        c[f"u{l}"] = up * 1.0
    c["l1"] = c["u1"].T.copy()
    for n in ("l1", "u1", "u2", "u4", "u8", "u16", "id"):
        full = np.eye(128, dtype=np.float32) if n == "id" else c[n]
        pk = np.concatenate([full[32 * b:32 * b + 32, 32 * b:32 * b + 32] for b in range(4)], 0)
        c["p" + n] = pk
        c["q" + n] = pk.copy()
        c["q" + n][64:, 24:] = 0
    pos = np.arange(T1, dtype=np.float32)
    inv = np.float32(500000.0) ** (-np.arange(0, 16, 2, dtype=np.float32) / np.float32(16))
    ang = pos[:, None] * inv.astype(np.float32)[None, :]
    cos, sin = np.ones((128, T1)), np.zeros((128, T1))
    rot = np.zeros((128, 128))
    for h in (0, 64):
        for j in range(8):
            cos[h + j] = cos[h + 8 + j] = np.cos(ang[:, j])
            sin[h + j] = sin[h + 8 + j] = np.sin(ang[:, j])
            rot[h + 8 + j, h + j] = -1.0
            rot[h + j, h + 8 + j] = 1.0
    c["cos"], c["sin"], c["rot"] = cos, sin, rot
    m = np.ones((128, T1)); m[:, ::CH] = 0
    c["rst88"] = m
    m = np.ones((128, T2)); m[:, ::128] = 0
    c["rst128"] = m
    s = np.zeros((128, 16, 128))
    for e in range(16):
        s[e, e] = 1.0
    c["sel16"] = s.reshape(128, 2048)
    d = np.arange(0, 512)
    lr = (np.log(np.maximum(d, 1).astype(np.float32) / np.float32(16)) / np.float32(math.log(1024 / 16))).astype(np.float32)
    large = np.minimum(16 + (lr * np.float32(16)).astype(np.int32), 31)
    bk = np.where(d < 16, d, large)
    oh = np.zeros((128, 512 + 128))
    oh[bk[511 - d], d] = 1.0
    c["oh"] = oh[:, :512]
    return {k: v.astype(np.float32) for k, v in c.items()}


def cols_of(names, sizes):
    off, out = 0, {}
    for n, s in zip(names, sizes):
        out[n] = (off, s)
        off += s
    return out, off


PARAMS = {}


def pack_params(I):
    P = {}

    def vec(name, a):
        a = np.asarray(a, np.float32).reshape(-1)
        P[name] = a.reshape(-1, 128).T

    def rows(name, a):
        a = np.asarray(a, np.float32)
        z = np.zeros((128, a.shape[1]), np.float32)
        z[:a.shape[0]] = a
        P[name] = z

    def rep(name, a):
        P[name] = np.broadcast_to(np.asarray(a, np.float32).reshape(1, -1), (128, np.asarray(a).size))

    vec("nmix", I["norm_mix_w"])
    mu = np.asarray(I["rwkv_mu"], np.float32).reshape(-1)
    vec("mu", mu[:3072])
    vec("muwa", mu[3072:3200])
    vec("mug", np.concatenate([mu[3200:3360], np.zeros(96, np.float32)]))
    for n in ("w0", "a0", "k_k", "k_a", "r_k", "ln_w", "ln_b"):
        vec(n, I["rwkv_" + n])
    P["w2a2"] = np.concatenate([np.asarray(I["rwkv_w2"])[0], np.asarray(I["rwkv_a2"])[0]], 0)
    g2 = np.asarray(I["rwkv_g2"])[0]
    P["g2a"] = g2[:128]
    rows("g2b", g2[128:])
    for n in ("lq1", "lk1", "lq2", "lk2"):
        rep(n, I["diff_" + n])
    vec("subln", I["diff_subln_w"])
    vec("nmlp", I["norm_mlp_w"])
    vec("fin", I["final_norm_w"])
    for n in ("ln0_g", "ln0_b", "ln1_g", "ln1_b", "ln2_g", "ln2_b"):
        vec(n, I[n + "_2"])
    conv = np.asarray(I["gdn_conv_2"])[0]
    P["conv"] = conv.reshape(4, 12, 128).transpose(2, 1, 0).reshape(128, 48)
    rep("alog", I["gdn_a_log_2"])
    rep("dtb", I["gdn_dt_bias_2"])
    for n in ("gdn", "gla", "hgrn"):
        vec(n + "n", I[n + "_norm_2"])
    rows("glaw2", np.asarray(I["gla_w2_2"])[0])
    vec("glab2", I["gla_b2_2"])
    vec("lb", I["hgrn_lb_logits_2"])
    P["wr"] = np.asarray(I["w_router_2"]).reshape(8, 128, 16).transpose(1, 0, 2).reshape(128, 128)
    rep("rb", I["router_bias_2"])
    vec("ng3", I["norm_gain_3"])
    rows("bf", np.asarray(I["b_forget_3"]).reshape(4, 1))
    for n in ("fox", "moba", "swa"):
        g = np.asarray(I[n + "_qk_gain_3"])[0]
        P[n + "g"] = np.concatenate([g, g], 1).T
    rep("sinks", I["sinks_3"])
    rows("relb", I["rel_bias_3"])
    return {k: np.ascontiguousarray(v, np.float32) for k, v in P.items()}


def tiles(w):
    k, n = w.shape
    w = w.reshape(k // 128, 128, n // 128, 128).transpose(2, 1, 0, 3)
    return [t.reshape(128, -1) for t in w]


def pack_weights(I):
    A = lambda n: np.asarray(I[n], np.float32).reshape(np.asarray(I[n]).shape[-2:]) if np.asarray(I[n]).ndim == 3 else np.asarray(I[n], np.float32)
    out = []
    w = A("w_in")
    pad = np.concatenate([w[:, 3072:3360], np.zeros((1024, 96), np.float32)], 1)
    out += tiles(pad)
    r = tiles(w[:, :3072])
    for p in range(8):
        out += [r[p], r[8 + p], r[16 + p]]
    out += tiles(A("rwkv_w_o"))
    q = tiles(w[:, 3360:6432])
    for h in range(8):
        out += [q[h], q[8 + h], q[16 + h]]
    g, o = tiles(w[:, 6432:]), tiles(A("diff_w_o"))
    for t in range(8):
        out += [g[t], g[8 + t], o[t]]
    out += tiles(A("w_out"))
    out += tiles(A("mlp_w1"))
    for t in tiles(A("mlp_w2")):
        out += [t[:, 1024 * j:1024 * j + 1024] for j in range(4)]
    w = A("w_in_2")
    at = {}
    off = 0
    for n, s in zip("aq ak av be dt ag bq bk bv lr bg cq cf ci cg ma mb mc".split(),
                    (512, 512, 512, 4, 4, 512, 256, 256, 512, 16, 512, 512, 512, 512, 512, 1024, 1024, 1024)):
        at[n] = w[:, off:off + s]
        off += s
    small = np.concatenate([at["lr"], at["be"], at["dt"], np.zeros((1024, 104), np.float32)], 1)
    out += tiles(small)
    a = {n: tiles(at[n]) for n in at if n not in ("be", "dt", "lr")}
    for h in range(4):
        out += [a["aq"][h], a["ak"][h], a["av"][h], a["ag"][h]]
    for p in range(2):
        out += [a["bq"][p], a["bk"][p]]
        for h in (2 * p, 2 * p + 1):
            out += [a["bv"][h], a["bg"][h]]
    for h in range(4):
        out += [a["cq"][h], a["cf"][h], a["ci"][h], a["cg"][h]]
    br = [tiles(A("w_br_%s_2" % n)) for n in "abc"]
    for t in range(8):
        for b in range(3):
            out += [a["m" + "abc"[b]][t], br[b][t]]
    out += tiles(A("w_out_2"))
    wg, wu = np.asarray(I["w_gate_2"])[0], np.asarray(I["w_up_2"])[0]
    for e in range(16):
        tg, tu = tiles(wg[e]), tiles(wu[e])
        out += [tg[0], tu[0], tg[1], tu[1]]
    for t in tiles(np.asarray(I["w_down_2"], np.float32).reshape(4096, 1024)):
        out += [t[:, 1024 * j:1024 * j + 1024] for j in range(4)]
    w = A("w_in_3")
    at, off = {}, 0
    for n, s in zip("fq fk fv ff fg mq mk mv mg sq sk sv sg wq wk wv wg".split(),
                    (256, 256, 256, 4, 256, 256, 256, 256, 256, 256, 256, 256, 256, 256, 128, 128, 256)):
        at[n] = w[:, off:off + s]
        off += s
    at["ff"] = np.concatenate([at["ff"], np.zeros((1024, 124), np.float32)], 1)
    a = {n: tiles(v) for n, v in at.items()}
    out += a["ff"]
    for g in "fm":
        for p in range(2):
            out += [a[g + "q"][p], a[g + "k"][p], a[g + "v"][p], a[g + "g"][p]]
    for p in range(2):
        out += [a["sq"][p], a["sk"][p], a["sv"][p], a["sg"][p]]
    out += [a["wv"][0]]
    for p in range(2):
        kp = at["wk"][:, 64 * p:64 * p + 64]
        out += [a["wq"][p], tiles(np.concatenate([kp, kp], 1))[0], a["wg"][p]]
    out += tiles(A("w_out_3"))
    return out


N1 = 3 + 24 + 8 + 24 + 24 + 8 + 32 + 32
N2 = 1 + 16 + 12 + 16 + 48 + 8 + 64 + 32


class Kern:

    def __init__(self, nc, P, ring, psum, arena, cst, par):
        self.nc, self.P, self.ring, self.ps, self.ar = nc, P, ring, psum, arena
        self.c, self.p = cst, par
        self.top = 0
        self.woff = 0

    def sb(self, n):
        a = self.ar[:, self.top:self.top + n]
        self.top += n
        assert self.top <= self.ar.shape[1], (self.top, self.ar.shape)
        return a

    def bank(self, b, n=1):
        return self.ps[:, 512 * b:512 * (b + n)]

    def tt(self, out, a, b, op, *w, eng="dve"):
        e = self.nc.vector if eng == "dve" else self.nc.gpsimd
        return self.P.op(eng, lambda: e.tensor_tensor(out, a, b, op), *w)

    def ts(self, out, a, s1, s2, op0, op1, *w, eng="dve"):
        e = self.nc.vector if eng == "dve" else self.nc.gpsimd
        if op1 is None:
            return self.P.op(eng, lambda: e.tensor_scalar(out, a, s1, None, op0), *w)
        return self.P.op(eng, lambda: e.tensor_scalar(out, a, s1, s2, op0, op1), *w)

    def stt(self, out, a, s, b, op0, op1, *w):
        return self.P.op("dve", lambda: self.nc.vector.scalar_tensor_tensor(out=out, in0=a, scalar=s, in1=b, op0=op0, op1=op1), *w)

    def cp(self, out, a, *w, eng="dve"):
        if eng == "act":
            return self.act(out, a, ACT.Copy, *w)
        e = self.nc.vector if eng == "dve" else self.nc.gpsimd
        return self.P.op(eng, lambda: e.tensor_copy(out, a), *w)

    def ms(self, out, v, *w, eng="dve"):
        e = self.nc.vector if eng == "dve" else self.nc.gpsimd
        return self.P.op(eng, lambda: e.memset(out, v), *w)

    def rec(self, out, a, *w):
        return self.P.op("dve", lambda: self.nc.vector.reciprocal(out, a), *w)

    def red(self, out, a, op, *w, neg=False):
        return self.P.op("dve", lambda: self.nc.vector.tensor_reduce(out, a, AXX, op, negate=neg), *w)

    def scan(self, out, d0, d1, *w):
        return self.P.op("dve", lambda: self.nc.vector.tensor_tensor_scan(out, d0, d1, 0.0, MUL, ADD), *w)

    def cpred(self, out, mask, data, *w):
        return self.P.op("dve", lambda: self.nc.vector.copy_predicated(out, mask, data), *w)

    def act(self, out, a, f, *w, bias=0.0, scale=1.0, accum=None):
        return self.P.op("act", lambda: self.nc.scalar.activation(out, a, f, bias=bias, scale=scale, accum_out=accum), *w)

    def mm(self, out, l, r, start, stop, *w, skip=False):
        return self.P.op("pe", lambda: self.nc.tensor.matmul(out, l, r, start=start, stop=stop, skip_group_check=skip), *w)

    def tr(self, out, a, *w):
        n = a.shape[0]
        return self.P.op("pe", lambda: self.nc.tensor.transpose(out, a, self.c["ident"][0:n, 0:n]), *w)

    def slab(self, n=1024, off=None):
        s = Slab(n, self.woff if off is None else off, len(self.P.slabs))
        if off is None:
            self.woff += n
        self.P.slabs.append(s)
        s.ap = self.ring[:, (s.i % RING) * SLAB:(s.i % RING) * SLAB + n].rearrange("p (k c) -> p k c", c=128)
        return s

    def lin(self, x, T, nk=8, m=128, x0=0, w=()):
        s = self.slab(nk * 128)
        return self.lin_slab(s, x, T, 0, nk, m, x0, w, True)

    def lin_slab(self, s, x, T, k0, nk, m=128, x0=0, w=(), done=False):
        n = 2 if T > 512 else 1
        b, fr = self.P.banks(n)
        hw = T // n
        first = [s.tok, fr, *w]
        for k in range(nk):
            for j in range(n):
                t = self.mm(self.ps[0:m, 512 * (b + j):512 * (b + j) + hw], s.ap[:, k0 + k, 0:m],
                            x[:, (x0 + k) * T + j * hw:(x0 + k) * T + (j + 1) * hw], k == 0, k == nk - 1, *first)
                first = []
        if done:
            s.done = t
        return b, n, t

    def alias(self, buf, width):
        c0, n = (buf.offset, buf.shape[1]) if isinstance(buf, bass.AP) else (0, buf.shape[1])
        name = buf.tensor.name if isinstance(buf, bass.AP) else buf.name
        for c in range(c0, c0 + n, width):
            if not any(x[0:3] == (name, c, width) for x in self.short):
                h = self.nc.alloc_sbuf_tensor_at(f"{name}_{c}_{width}", [128, width], F32R, offset=self.at[name] + 4 * c)
                self.short.append((name, c, width, h))
            else:
                i = [x[0:3] for x in self.short].index((name, c, width))
                self.short.append(self.short.pop(i))

    def r(self, ap):
        n = 1
        for st, k in list(ap.ap)[1:]:
            n += st * (k - 1)
        for name, c, width, h in reversed(self.short):
            if name == ap.tensor.name and c <= ap.offset and ap.offset + n <= c + width:
                return bass.AP(tensor=h, offset=ap.offset - c, ap=[[width, ap.shape[0]]] + [list(x) for x in list(ap.ap)[1:]])
        assert False, (ap.offset, n)

    def split(self, x, hi, *w, eng="dve", hi_eng="dve"):
        t = self.cp(self.r(hi), x, *w, eng=hi_eng)
        return [t, self.tt(self.r(x), x, self.r(hi), SUB, t, *w, eng=eng)]

    def split_tiles(self, x, hi, T, n, *w):
        return [self.split(x[:, k * T:k * T + T], hi[:, k * T:k * T + T], *w, eng="pool") for k in range(n)]

    def mm3(self, out, wh, wl, xs, T, k0, first, last, *w):
        n = 2 if T > 512 else 1
        hw = T // n
        for i, (a, x) in enumerate(((wh, xs[0]), (wh, xs[1]), (wl, xs[0]))):
            for j in range(n):
                t = self.mm(out(j), self.r(a), self.r(x[:, k0 * T + j * hw:k0 * T + (j + 1) * hw]),
                            first and i == 0, last and i == 2, *w)
                w = ()
        return t

    def lin3(self, ws, xs, T, nk=8, x0=0, w=()):
        n = 2 if T > 512 else 1
        s = ws.take()
        b, fr = self.P.banks(n)
        out = lambda j: self.ps[:, 512 * (b + j):512 * (b + j) + T // n]
        for k in range(nk):
            t = self.mm3(out, s.hi[:, k, :], s.ap[:, k, :], xs, T, x0 + k, k == 0, k == nk - 1, s.ready, fr, w[x0 + k] if w else None)
        s.done = t
        return b, n, t

    def view(self, b, n, T, m0=0, m1=128):
        if n == 1:
            return self.ps[m0:m1, 512 * b:512 * b + T]
        return self.ps[m0:m1, 512 * b:512 * (b + 2)].rearrange("p (a c) -> p a c", a=2)[:, :, 0:T // 2]

    def like(self, ap, n):
        return ap if n == 1 else ap.rearrange("p (a c) -> p a c", a=2)

    def colsum(self, ones, srcs, T, *w, m=128, per=None):
        n = 2 if T > 512 else 1
        b, fr = self.P.banks(n)
        first = [fr, *w]
        hw = T // n
        for k, s in enumerate(srcs):
            for j in range(n):
                t = self.mm(self.ps[0:m, 512 * (b + j):512 * (b + j) + hw], ones, s[:, j * hw:(j + 1) * hw],
                            k == 0, k == len(srcs) - 1, *first, per[k] if per else None)
                first = []
        return b, n, t

    def rstd(self, out, b, n, T, scale, eps, tok):
        t = self.act(self.like(out, n), self.view(b, n, T), ACT.Sqrt, tok, scale=scale, bias=eps)
        self.P.free(b, n, t)
        return self.rec(out, out, t)

    def rms(self, x, wcol, out, T, eps, sq, rs, *w, per=None, hi=None, o0=0):
        ts = [self.act(sq[:, k * T:(k + 1) * T], x[:, k * T:(k + 1) * T], ACT.Square, *w, per[k] if per else None)
              for k in range(8)]
        b, n, t = self.colsum(self.c["ones"], [sq[:, k * T:(k + 1) * T] for k in range(8)], T, per=ts)
        self.rstd(rs, b, n, T, 1.0 / 1024, eps, t)
        got = []
        for k in range(8):
            S = slice(k * T, (k + 1) * T)
            t = self.stt(out[:, k * (T - o0):(k + 1) * (T - o0)], x[:, k * T + o0:(k + 1) * T], wcol[:, k:k + 1], rs[:, o0:T], MUL, MUL)
            if hi is not None:
                got.append(self.split(out[:, S], hi[:, S], t, eng="pool"))
        return t if hi is None else got

    def lnorm(self, x, g, b_, out, T, eps, sq, rs, *w, per=None):
        b, n, t = self.colsum(self.c["ones"], [x[:, k * T:(k + 1) * T] for k in range(8)], T, *w, per=per)
        ts = []
        for k in range(8):
            xs = x[:, k * T:(k + 1) * T]
            t = self.stt(xs, self.view(b, n, T), -1.0 / 1024, xs, MUL, ADD, t)
            ts.append(self.act(sq[:, k * T:(k + 1) * T], xs, ACT.Square, t))
        self.P.free(b, n, t)
        b, n, t = self.colsum(self.c["ones"], [sq[:, k * T:(k + 1) * T] for k in range(8)], T, per=ts)
        self.rstd(rs, b, n, T, 1.0 / 1024, eps, t)
        for k in range(8):
            xs = x[:, k * T:(k + 1) * T]
            self.stt(xs, xs, g[:, k:k + 1], rs, MUL, MUL)
            t = self.ts(out[:, k * T:(k + 1) * T], xs, b_[:, k:k + 1], None, ADD, None)
        return t

    def phase(self, top):
        self.P.gate(self.P.marks())
        self.top = top


class Weights:

    def __init__(self, K, offs, hi, tok=None):
        self.K, self.offs, self.hi, self.slabs, self.i, self.tok = K, offs, hi, [], 0, tok
        for q in hi:
            K.alias(q, SLAB)
        self.ahead()

    def ahead(self):
        K, NH = self.K, len(self.hi)
        while len(self.slabs) < min(self.i + NH, len(self.offs)):
            n = len(self.slabs)
            off, size = self.offs[n]
            s = K.slab(size, off)
            hi = self.hi[n % NH][:, 0:size]
            free = self.slabs[n - NH].done if n >= NH else self.tok
            raw = s.ap.rearrange("p k c -> p (k c)")
            s.ready = K.split(raw, hi, s.tok, free, hi_eng="act")
            s.hi = hi.rearrange("p (k c) -> p k c", c=128)
            self.slabs.append(s)

    def take(self):
        self.ahead()
        self.i += 1
        return self.slabs[self.i - 1]


class Slab:
    def __init__(self, n, off, i):
        self.n, self.off, self.i = n, off, i
        self.tok, self.done = Tok("slab"), None


def block1(K, xT, x_tok=None):
    P, c, p, T = K.P, K.c, K.p, T1
    base = K.top
    oy = K.sb(8 * T)
    h = K.sb(8 * T)
    out = oy[:, 0:4096]
    mark = K.top
    hres = K.sb(8 * T)
    sq = K.sb(8 * T)
    rs = K.sb(T)
    ld = P.dma(hres, xT)
    th = K.rms(hres, p["nmix"], h, T, c["eps5"], sq, rs, ld, x_tok)
    K.phase(mark)

    omka = K.sb(8)
    K.ts(omka, p["k_a"], -1.0, 1.0, MUL, ADD)
    lora = [K.sb(T) for _ in range(3)]
    sh = [K.sb(T + 4) for _ in range(3)]
    dd = [K.sb(T) for _ in range(3)]
    for s in sh:
        tz = K.ms(s[:, 0:1], 0.0)
    dsh = dict((n, K.sb(T)) for n in ("k", "cum", "pm", "e", "a", "kt"))
    pads = [K.sb(T + 8) for _ in range(2)]
    dsh["at"], dsh["bt"] = pads[0][:, 0:T], pads[1][:, 0:T]
    for q in pads:
        K.ms(q[:, T:T + 8], 0.0)
    sets = [dict(dsh, r=K.sb(T), v=K.sb(T), rt=K.sb(T), pc=K.sb(8)) for _ in range(2)]
    fin = [K.sb(T) for _ in range(2)]
    toks = dict((n, K.sb(NCH * 128)) for n in ("V", "B", "Kh", "At"))
    unit = [dict((n, K.sb(w)) for n, w in (
        ("Mb", T), ("Ak", T), ("Mk", T), ("XT", T), ("ATo", 56 * NCH), ("ATp", 32 * NCH), ("Xp", 32 * NCH), ("XTp", 32 * NCH),
        ("M0", 32 * NCH), ("M1", 32 * NCH), ("Yp", 32 * NCH))) for _ in range(2)]
    for u in unit:
        K.ms(u["XT"], 0.0)
        u["AV"], u["U0"] = K.sb(NCH * 64), K.sb(NCH * 64)
    WT = K.sb(T)
    St = [K.sb(64) for _ in range(2)]
    tsh = [None] * 3

    def shifted(i, b, n, tok, mu, out, rows=128):
        s = sh[i]
        t = K.act(K.like(s[0:rows, 1:T + 1], n), K.view(b, n, T, 0, rows), ACT.Copy, tok, tz, tsh[i])
        P.free(b, n, t)
        K.tt(dd[i][0:rows], s[0:rows, 0:T], s[0:rows, 1:T + 1], SUB, t)
        tsh[i] = K.stt(out[0:rows], dd[i][0:rows], mu[0:rows], s[0:rows, 1:T + 1], MUL, ADD)
        return tsh[i]

    for i, (mu, rows) in enumerate(((p["muwa"][:, 0:1], 128), (p["mug"][:, 0:1], 128), (p["mug"][:, 1:2], 32))):
        b, n, t = K.lin(h, T, m=rows, w=[th])
        t = shifted(i, b, n, t, mu, lora[i], rows)
        if i == 0:
            tl = K.act(lora[0][0:64], lora[0][0:64], ACT.Tanh, t)
        else:
            tl = K.act(lora[i][0:rows], lora[i][0:rows], ACT.Sigmoid, t)

    BLK = ((0, 32), (32, 32), (64, CH - 64))

    def p3(ap):
        return ap[0:CH, 0:32 * NCH].rearrange("p (c t) -> p c t", c=NCH)

    def pk(n):
        return c[n][0:CH].unsqueeze(1).to_broadcast([CH, NCH, 32])

    def blocks(l, r, *w):
        b, fr = P.banks(1)
        for ci in range(NCH):
            for k, n in BLK:
                t = K.mm(K.ps[k:k + n, 512 * b + 32 * ci:512 * b + 32 * ci + 32], l[k:k + n, 32 * ci:32 * ci + n],
                         r[k:k + n, 32 * ci:32 * ci + 32], True, True, fr, *w)
        return b, t

    up = c["sup"][0:CH, 0:CH].unsqueeze(1).to_broadcast([CH, NCH, CH])
    upi = c["triu"][0:CH, 0:CH].unsqueeze(1).to_broadcast([CH, NCH, CH])
    lo = c["slo"][0:CH, 0:CH].unsqueeze(1).to_broadcast([CH, NCH, CH])
    EH = math.exp(-0.5)

    def bc(ap):
        return ap.unsqueeze(1).to_broadcast([CH, NCH, CH])

    def u3(ap):
        return ap[0:CH, 0:T].rearrange("p (c t) -> p c t", c=NCH)

    def ps4(b):
        return K.ps[0:CH, 512 * b:512 * (b + 2)].rearrange("p (a c) -> p a c", a=2)[:, :, 0:264]

    def blk(b, ci, rows=slice(0, CH), w=CH):
        o = 512 * (b + ci // 3) + (ci % 3) * w
        return K.ps[rows, o:o + w]

    def h2(ap):
        return ap.rearrange("p (a t) -> p a t", a=2)

    def glin(x, w=()):
        s = K.slab()
        b, fr = P.banks(2)
        P.held |= {b, b + 1}
        first = [s.tok, fr, *w]
        for k in range(8):
            for j in range(2):
                t = K.mm(K.ps[:, 512 * (b + j):512 * (b + j) + 264], s.ap[:, k, :],
                         x[:, k * T + j * 264:k * T + (j + 1) * 264], k == 0, k == 7, *first)
                first = []
            if k % 2 and k < 7:
                yield
        s.done = t
        P.held -= {b, b + 1}
        return b, 2, t

    def prep(hp, m2):
        d = sets[hp % 2]
        col = slice(hp, hp + 1)
        P.gate(m2, ("act", "dve"))
        for i, nme in enumerate("rkv"):
            b, n, t = yield from glin(h)
            shifted(i, b, n, t, p["mu"][:, 8 * i + hp:8 * i + hp + 1], d[nme])
            if nme == "k":
                K.ts(dd[0], d["k"], p["k_k"][:, col], None, MUL, None)
                tkk = K.tt(dd[1], dd[0], dd[0], MUL)
            yield
            if nme == "k":
                b, n, t = K.colsum(c["oblk"], [dd[1]], T, tkk)
                t = K.act(h2(fin2), K.view(b, n, T), ACT.Sqrt, t)
                P.free(b, n, t)
                K.ts(fin2, fin2, 1e-12, None, MAX, None, t)
                K.rec(fin2, fin2)
                K.tt(dd[0], dd[0], fin2, MUL)
        b, fr = P.banks(2)
        for j in range(2):
            t = K.mm(K.ps[:, 512 * (b + j):512 * (b + j) + 264], p["w2a2"][0:64, 128 * hp:128 * hp + 128],
                     lora[0][0:64, 264 * j:264 * j + 264], True, True, fr, tl)
        t = K.act(h2(d["e"]), K.view(b, 2, T), ACT.Sigmoid, t, bias=p["w0"][:, col])
        P.free(b, 2, t)
        b, fr = P.banks(2)
        for j in range(2):
            t2 = K.mm(K.ps[:, 512 * (b + j):512 * (b + j) + 264], p["w2a2"][64:128, 128 * hp:128 * hp + 128],
                      lora[0][64:128, 264 * j:264 * j + 264], True, True, fr)
        ta = K.act(h2(d["a"]), K.view(b, 2, T), ACT.Sigmoid, t2, bias=p["a0"][:, col])
        P.free(b, 2, ta)
        K.scan(d["cum"], c["rst88"], d["e"], t)
        t1 = K.tt(d["pm"], d["cum"], d["e"], SUB)
        tpm = K.act(d["pm"], d["pm"], ACT.Exp, t1, scale=-EH)
        K.act(d["e"], d["cum"], ACT.Exp, scale=EH)
        tcum = K.act(d["cum"], d["cum"], ACT.Exp, scale=-EH)
        yield
        K.ts(dd[1], d["a"], p["k_a"][:, col], omka[:, col], MUL, ADD, ta)
        K.tt(d["k"], d["k"], dd[1], MUL)
        K.tt(dd[1], dd[0], d["a"], MUL)
        K.stt(d["at"], dd[0], -1.0, d["pm"], MUL, MUL, tpm)
        yield
        K.tt(d["bt"], dd[1], d["e"], MUL, tcum)
        K.tt(d["kt"], d["k"], d["e"], MUL)
        K.tt(d["rt"], d["r"], d["cum"], MUL)
        yield
        K.cp(d["pc"][:, 0:NCH].unsqueeze(2), d["cum"].rearrange("p (c t) -> p c t", c=NCH)[:, :, CH - 1:CH])
        K.stt(d["r"], d["r"], p["r_k"][:, col], d["k"], MUL, MUL)
        pcb = d["pc"][:, 0:NCH].unsqueeze(2).to_broadcast([128, NCH, CH])
        v3 = lambda x: x.rearrange("p (c t) -> p c t", c=NCH)
        K.tt(v3(d["e"]), v3(d["bt"]), pcb, MUL)
        d["tq"] = K.tt(v3(d["pm"]), v3(d["kt"]), pcb, MUL)

    def finish(hp, by, ty, tprev):
        d = sets[hp % 2]
        col = slice(hp, hp + 1)
        y, s1 = fin
        t = K.act(h2(y), K.view(by, 2, T), ACT.Copy, ty, tprev)
        P.free(by, 2, t)
        yield
        b, n, tr2 = K.colsum(c["oblk"], [d["r"]], T)
        b2, n, t = K.colsum(c["oblk"], [y], T, t)
        t = K.stt(h2(y), K.view(b2, n, T), -1.0 / 64, h2(y), MUL, ADD, t)
        P.free(b2, n, t)
        t = K.act(s1, y, ACT.Square, t)
        tv = K.tt(h2(d["v"]), h2(d["v"]), K.view(b, n, T), MUL, tr2)
        P.free(b, n, tv)
        yield
        yield
        b, n, t = K.colsum(c["oblk"], [s1], T, t)
        K.rstd(s1, b, n, T, 1.0 / 64, c["epsgn"], t)
        K.tt(y, y, s1, MUL)
        K.ts(y, y, p["ln_w"][:, col], p["ln_b"][:, col], MUL, ADD)
        K.tt(y, y, d["v"], ADD)
        yield
        yield
        b, fr = P.banks(2)
        for j in range(2):
            o = K.ps[:, 512 * (b + j):512 * (b + j) + 264]
            J = slice(264 * j, 264 * j + 264)
            K.mm(o, p["g2a"][:, 128 * hp:128 * hp + 128], lora[1][:, J], True, False, fr)
            t = K.mm(o, p["g2b"][0:32, 128 * hp:128 * hp + 128], lora[2][0:32, J], False, True)
        d["toy"] = K.tt(h2(oy[:, T * hp:T * hp + T]), h2(y), K.view(b, 2, T), MUL, t)
        P.free(b, 2, d["toy"])

    work = []

    def step():
        while work:
            try:
                next(work[0])
                return
            except StopIteration:
                work.pop(0)

    def drain():
        while work:
            step()

    fin2 = dd[2]
    work.append(prep(0, P.marks()))
    drain()
    mscan = None
    for hp in range(8):
        d = sets[hp % 2]
        pc, tq = d["pc"], d["tq"]
        if mscan:
            P.gate(mscan, ("act", "dve"))
        tt_ = {}
        for nme, src in (("V", d["v"]), ("At", d["at"]), ("B", d["e"]), ("Kh", d["pm"])):
            b, fr = P.banks(2)
            for ci in range(NCH):
                o = 512 * (b + ci // 3) + (ci % 3) * 128
                t = K.tr(K.ps[0:CH, o:o + 128], src[:, CH * ci:CH * ci + CH], fr, tq)
            pv = K.ps[0:CH, 512 * b:512 * (b + 2)].rearrange("p (a c) -> p a c", a=2)[:, :, 0:384]
            tt_[nme] = K.act(h2(toks[nme][0:CH]), pv, ACT.Copy, t)
            P.free(b, 2, tt_[nme])
            step()
        ttok = tt_["Kh"]
        tu = {}
        for hh in range(2):
            u = unit[hh]
            R = slice(64 * hh, 64 * hh + 64)
            for nme, l, r in (("ATp", "bt", "at"), ("Xp", "at", "bt")):
                b, fr = P.banks(1)
                for ci in range(NCH):
                    for k, w in BLK:
                        o = CH * ci + k
                        t = K.mm(K.ps[k:k + w, 512 * b + 32 * ci:512 * b + 32 * ci + 32], d[l][R, o:o + w],
                                 pads[r == "bt"][R, o:o + 32], True, True, fr, tq)
                if nme == "ATp":
                    tu[nme] = K.act(u[nme][0:CH], K.ps[0:CH, 512 * b:512 * b + 192], ACT.Copy, t)
                else:
                    tu[nme] = K.tt(p3(u[nme]), p3(K.bank(b)), pk("ql1"), MUL, t)
                P.free(b, 1, tu[nme])
            b, fr = P.banks(1)
            for ci in range(NCH):
                t = K.mm(K.ps[0:64, 512 * b + 56 * ci:512 * b + 56 * ci + 56], d["bt"][R, CH * ci:CH * ci + 64],
                         d["at"][R, CH * ci + 32:CH * ci + CH], True, True, fr)
            tu["ATo"] = K.act(u["ATo"][0:64], K.ps[0:64, 512 * b:512 * b + 336], ACT.Copy, t)
            P.free(b, 1, tu["ATo"])
            step()
            for nme, l, r, msk in (("Ak", "kt", "at", "sup"), ("Mb", "bt", "rt", "triu"), ("Mk", "kt", "rt", "triu")):
                b, fr = P.banks(2)
                for ci in range(NCH):
                    S = slice(CH * ci, CH * ci + CH)
                    t = K.mm(blk(b, ci), d[l][R, S], d[r][R, S], True, True, fr, tq)
                pin = ps4(b)
                mk = c[msk][0:CH, 0:CH].unsqueeze(1).to_broadcast([CH, 3, CH])
                for a in range(2):
                    t2 = K.tt(u[nme][0:CH, 264 * a:264 * a + 264].rearrange("p (c t) -> p c t", c=3),
                              pin[:, a].rearrange("p (c t) -> p c t", c=3), mk, MUL, t)
                P.free(b, 2, t2)
                tu[nme] = t2
                step()
            b, fr = P.banks(1)
            for ci in range(NCH):
                t = K.mm(K.ps[0:CH, 512 * b + 64 * ci:512 * b + 64 * ci + 64], u["Ak"][0:CH, CH * ci:CH * ci + CH],
                         toks["V"][0:CH, 128 * ci + 64 * hh:128 * ci + 64 * hh + 64], True, True, fr, tu["Ak"], tt_["V"])
            tav = K.cp(u["AV"][0:CH], K.ps[0:CH, 512 * b:512 * b + 384], t, eng="act")
            P.free(b, 1, tav)
            u["tav"] = tav
            K.tt(p3(u["Xp"]), p3(u["Xp"]), pk("qid"), ADD)
            K.tt(p3(u["XTp"]), p3(u["ATp"]), pk("qu1"), MUL, tu["ATp"])
            K.tt(p3(u["XTp"]), p3(u["XTp"]), pk("qid"), ADD)
            u["tx"] = u["tm"] = K.tt(p3(u["M0"]), p3(u["ATp"]), pk("qu2"), MUL)
        drain()
        if hp < 7:
            work.append(prep(hp + 1, P.marks()))
        for l in (2, 4, 8, 16):
            for hh in range(2):
                u = unit[hh]
                MT = u["M0"] if l in (2, 8) else u["M1"]
                b, t = blocks(MT, u["Xp"], u["tm"], u["tx"])
                u["ty"] = K.act(u["Yp"][0:CH], K.ps[0:CH, 512 * b:512 * b + 192], ACT.Copy, t)
                P.free(b, 1, u["ty"])
                if l < 16:
                    MN = u["M1"] if l in (2, 8) else u["M0"]
                    u["tm"] = K.tt(p3(MN), p3(u["ATp"]), pk(f"qu{2 * l}"), MUL)
            step()
            for hh in range(2):
                u = unit[hh]
                bz, tz_ = blocks(u["XTp"], u["Yp"], u["ty"])
                b, t = blocks(u["Yp"], u["XTp"])
                x = K.tt(p3(u["Xp"]), p3(u["Xp"]), p3(K.bank(bz)), ADD, tz_)
                P.free(bz, 1, x)
                u["tx"] = K.tt(p3(u["XTp"]), p3(u["XTp"]), p3(K.bank(b)), ADD, t)
                P.free(b, 1, u["tx"])
            step()
        def pw(b, rows, width):
            return K.ps[rows, 512 * b:512 * b + NCH * width].rearrange("p (c t) -> p c t", c=NCH)

        A_, B_, C_ = slice(0, 32), slice(32, 64), slice(64, CH)
        for hh in range(2):
            u = unit[hh]
            b, fr = P.banks(1)
            for ci in range(NCH):
                I = slice(32 * ci, 32 * ci + 32)
                t = K.mm(K.ps[B_, 512 * b + 32 * ci:512 * b + 32 * ci + 32], u["ATo"][A_, 56 * ci:56 * ci + 32],
                         u["Xp"][A_, I], True, True, fr, u["tx"], tu["ATo"])
            u["ty"] = K.act(u["Yp"][B_], K.ps[B_, 512 * b:512 * b + 192], ACT.Copy, t)
            P.free(b, 1, u["ty"])
            K.act(u["M0"][A_], u["Xp"][A_], ACT.Copy)
            for k, w in BLK:
                u["te"] = K.act(u3(u["XT"])[k:k + w, :, k:k + w], p3(u["XTp"])[k:k + w, :, 0:w], ACT.Copy)
        step()
        for hh in range(2):
            u = unit[hh]
            bz, fr = P.banks(1)
            b, fr2 = P.banks(1)
            for ci in range(NCH):
                I = slice(32 * ci, 32 * ci + 32)
                tz_ = K.mm(K.ps[B_, 512 * bz + 32 * ci:512 * bz + 32 * ci + 32], u["XTp"][B_, I], u["Yp"][B_, I], True, True, fr, u["ty"])
            for ci in range(NCH):
                I = slice(32 * ci, 32 * ci + 32)
                t = K.mm(K.ps[A_, 512 * b + 32 * ci:512 * b + 32 * ci + 32], u["Yp"][B_, I], u["XTp"][B_, I], True, True, fr2)
            u["tm"] = K.act(u["M0"][B_], K.ps[B_, 512 * bz:512 * bz + 192], ACT.Copy, tz_)
            P.free(bz, 1, u["tm"])
            x = K.cp(u3(u["XT"])[A_, :, 32:64], pw(b, A_, 32), t)
            P.free(b, 1, x)
        step()
        for hh in range(2):
            u = unit[hh]
            b, fr = P.banks(1)
            for ci in range(NCH):
                I = slice(32 * ci, 32 * ci + 32)
                o = 512 * b + 64 * ci
                K.mm(K.ps[C_, o:o + 32], u["ATo"][0:64, 56 * ci + 32:56 * ci + 56], u["M0"][0:64, I], True, True, fr, u["tm"])
                t = K.mm(K.ps[C_, o + 32:o + 64], u["ATo"][B_, 56 * ci + 32:56 * ci + 56], u["Xp"][B_, I], True, True)
            u["ty"] = K.act(u["Ak"][C_, 0:384], K.ps[C_, 512 * b:512 * b + 384], ACT.Copy, t)
            P.free(b, 1, u["ty"])
        step()
        for hh in range(2):
            u = unit[hh]
            b, fr = P.banks(1)
            for ci in range(NCH):
                t = K.mm(K.ps[0:64, 512 * b + 24 * ci:512 * b + 24 * ci + 24], u["Ak"][C_, 64 * ci:64 * ci + 64],
                         u["XTp"][C_, 32 * ci:32 * ci + 24], True, True, fr, u["ty"])
            u["tx"] = K.cp(u3(u["XT"])[0:64, :, 64:CH], pw(b, slice(0, 64), 24), t)
            P.free(b, 1, u["tx"])
            u["tx"] = [u["tx"], u["te"]]
        step()
        b, fr = P.banks(2)
        for hh in range(2):
            u = unit[hh]
            for ci in range(NCH):
                S = slice(CH * ci, CH * ci + CH)
                t = K.mm(blk(b, ci, slice(64 * hh, 64 * hh + 64)), toks["At"][0:CH, 128 * ci + 64 * hh:128 * ci + 64 * hh + 64],
                         u["XT"][0:CH, S], True, True, fr, u["tx"], ttok)
        tw = K.act(h2(WT), K.view(b, 2, T), ACT.Copy, t)
        P.free(b, 2, tw)
        for hh in range(2):
            u = unit[hh]
            b, fr = P.banks(1)
            for ci in range(NCH):
                t = K.mm(K.ps[0:CH, 512 * b + 64 * ci:512 * b + 64 * ci + 64], u["XT"][0:CH, CH * ci:CH * ci + CH],
                         u["AV"][0:CH, 64 * ci:64 * ci + 64], True, True, fr, u["tx"])
            u["tu"] = K.cp(u["U0"][0:CH], K.ps[0:CH, 512 * b:512 * b + 384], t)
            P.free(b, 1, u["tu"])
        by, fry = P.banks(2)
        P.held |= {by, by + 1}
        tS = None
        for ci in range(NCH):
            S = slice(CH * ci, CH * ci + CH)
            so = St[ci % 2]
            sn = St[(ci + 1) % 2]
            tuu = []
            for hh in range(2):
                u = unit[hh]
                R = slice(64 * hh, 64 * hh + 64)
                if ci:
                    b, fr = P.banks(1)
                    t = K.mm(K.ps[0:CH, 512 * b:512 * b + 64], WT[R, S], so[R, :], True, True, fr, tS, tw)
                    us = u["U0"][0:CH, 64 * ci:64 * ci + 64]
                    t = K.tt(us, us, K.ps[0:CH, 512 * b:512 * b + 64], ADD, t)
                    P.free(b, 1, t)
                    tuu.append(t)
                else:
                    tuu.append(u["tu"])
            step()
            if ci < NCH - 1:
                b, fr = P.banks(1)
                for hh in range(2):
                    u = unit[hh]
                    R = slice(64 * hh, 64 * hh + 64)
                    C = slice(128 * ci + 64 * hh, 128 * ci + 64 * hh + 64)
                    o = K.ps[R, 512 * b:512 * b + 64]
                    K.mm(o, toks["Kh"][0:CH, C], toks["V"][0:CH, C], True, False, fr, ttok)
                    t = K.mm(o, toks["B"][0:CH, C], u["U0"][0:CH, 64 * ci:64 * ci + 64], False, True, tuu[hh])
                o = K.ps[:, 512 * b:512 * b + 64]
                if ci:
                    tSn = K.stt(sn, so, pc[:, ci:ci + 1], o, MUL, ADD, t, ty2)
                else:
                    tSn = K.cp(sn, o, t)
                P.free(b, 1, tSn)
                step()
            for hh in range(2):
                u = unit[hh]
                R = slice(64 * hh, 64 * hh + 64)
                o = blk(by, ci, R)
                C = slice(128 * ci + 64 * hh, 128 * ci + 64 * hh + 64)
                K.mm(o, toks["V"][0:CH, C], u["Mk"][0:CH, S], True, False, fry, tu["Mk"])
                t = K.mm(o, u["U0"][0:CH, 64 * ci:64 * ci + 64], u["Mb"][0:CH, S], False, ci == 0, tuu[hh])
                if ci:
                    t = K.mm(o, so[R, :], d["rt"][R, S], False, True)
            ty2 = t
            tS = tSn
            step()
        drain()
        P.held -= {by, by + 1}
        f = finish(hp, by, ty2, sets[(hp + 1) % 2].get("toy"))
        next(f)
        mscan = P.marks()
        work.append(f)
    drain()
    K.phase(mark)

    def run_of(n, size=1024):
        K.woff += n * size
        return [(K.woff - (n - i) * size, size) for i in range(n)]

    orw = K.sb(8 * T)
    od = K.sb(8 * T)
    wh = [K.sb(1024) for _ in range(3)]
    for q in (oy, od):
        K.alias(q, T)
    ws = Weights(K, run_of(8), wh)
    tsp = [K.split(oy[:, k * T:k * T + T], od[:, k * T:k * T + T], eng="pool" if k % 3 == 2 else "dve") for k in range(8)]
    for k in range(8):
        b, n, t = K.lin3(ws, (od, oy), T, w=tsp)
        t = K.act(h2(orw[:, k * T:k * T + T]), K.view(b, n, T), ACT.Copy, t)
        P.free(b, n, t)
    torw = t
    lam = K.sb(8)
    lt = K.sb(64)
    K.tt(lt, p["lq1"], p["lk1"], MUL)
    K.red(lam[:, 0:1], lt, ADD)
    K.tt(lt, p["lq2"], p["lk2"], MUL)
    t = K.red(lam[:, 1:2], lt, ADD)
    t = K.act(lam[:, 2:4], lam[:, 0:2], ACT.Exp, t)
    K.stt(lam[:, 4:5], lam[:, 2:3], -1.0, lam[:, 3:4], MUL, ADD, t)
    K.ts(lam[:, 4:5], lam[:, 4:5], -0.2, None, ADD, None)
    K.ts(lam[:, 5:6], p["subln"], 0.8, None, MUL, None)
    bufs = [dict((n, K.sb(w)) for n, w in (
        ("q", T), ("k", T), ("t1", T), ("t2", T), ("V", 5 * 128), ("P0", T), ("P1", T), ("P2", T), ("P3", T),
        ("aw0", 512), ("aw1", 512), ("am", 256), ("O", T), ("sc", 64))) for _ in range(2)]
    TK = [(0, 16)] + [(16 + 128 * j, 128) for j in range(4)]
    old = [None, None]
    tqv = {}

    wd = Weights(K, run_of(24), wh, ws.slabs[-1].done)
    hh = oy
    for q in (h, hh):
        K.alias(q, T)
    thh = [K.split(h[:, k * T:k * T + T], hh[:, k * T:k * T + T], ws.slabs[-1].done, eng="pool" if k % 3 == 2 else "dve")
           for k in range(8)]

    def glin3():
        s = wd.take()
        b, fr = P.banks(2)
        P.held |= {b, b + 1}
        out = lambda j: K.ps[:, 512 * (b + j):512 * (b + j) + 264]
        for k in range(8):
            t = K.mm3(out, s.hi[:, k, :], s.ap[:, k, :], (hh, h), T, k, k == 0, k == 7, s.ready, fr, thh[k])
            if k % 2 and k < 7:
                yield
        s.done = t
        P.held -= {b, b + 1}
        return b, 2, t

    def project(hd):
        d = bufs[hd % 2]
        if old[hd % 2]:
            P.gate(old[hd % 2], ("act", "dve"))
        for nme in "qk":
            b, n, t = yield from glin3()
            t = K.act(h2(d[nme]), K.view(b, n, T), ACT.Copy, t, scale=0.125 if nme == "q" else 1.0)
            P.free(b, n, t)
            K.tt(d["t1"], d[nme], c["cos"], MUL, t)
            yield
            b, n, t2 = K.colsum(c["rot"], [d[nme]], T, t)
            t3 = K.tt(h2(d["t2"]), K.view(b, n, T), h2(c["sin"]), MUL, t2)
            P.free(b, n, t3)
            tqk = K.tt(d[nme], d["t1"], d["t2"], ADD)
        b, n, t = yield from glin3()
        t = K.act(h2(d["O"]), K.view(b, n, T), ACT.Copy, t)
        P.free(b, n, t)
        yield
        b, fr = P.banks(2)
        for j, (t0, tw_) in enumerate(TK):
            o = 512 * b + 512 * (j > 0) + 128 * max(j - 1, 0)
            t2 = K.tr(K.ps[0:tw_, o:o + 128], d["O"][:, t0:t0 + tw_], fr, t)
        K.act(d["V"][0:16, 0:128], K.ps[0:16, 512 * b:512 * b + 128], ACT.Copy, t2)
        tV = K.act(d["V"][:, 128:640], K.ps[:, 512 * b + 512:512 * b + 1024], ACT.Copy)
        P.free(b, 2, tV)
        tqv[hd] = (tqk, tV)

    def scores(hd, i):
        d = bufs[hd % 2]
        q0, qw = TK[i]
        W = q0 + qw
        nb = 2 if W > 512 else 1
        pr = []
        for sub in range(2):
            R = slice(64 * sub, 64 * sub + 64)
            b, fr = P.banks(nb)
            m0 = 512 * b + (496 if nb == 2 else 0)
            sm = K.ps[0:qw, m0:m0 + 16]
            sn = K.ps[0:qw, m0 + 16:m0 + max(W, 17)]
            if nb == 2 or i == 0:
                K.mm(sm, d["q"][R, q0:q0 + qw], d["k"][R, 0:16], True, i > 0, fr, tqv[hd])
                if i == 0:
                    t = K.mm(sm, c["ident"][0:16, 0:16], c["negm"][0:16, 0:16], False, True)
                else:
                    K.mm(sn[:, 0:W - 144], d["q"][R, q0:q0 + qw], d["k"][R, 16:W - 128], True, True)
            else:
                K.mm(K.ps[0:qw, m0:m0 + W - 128], d["q"][R, q0:q0 + qw], d["k"][R, 0:W - 128], True, True, fr, tqv[hd])
            if i:
                K.mm(sn[:, W - 144:W - 16], d["q"][R, q0:q0 + qw], d["k"][R, W - 128:W], True, False)
                t = K.mm(sn[:, W - 144:W - 16], c["ident"], c["negm"], False, True)
            s_ = K.ps[0:qw, m0:m0 + W]
            sc = d["sc"][0:qw, 6 * i + 3 * sub:6 * i + 3 * sub + 3]
            Pt = d[f"P{2 * (i % 2) + sub}"][0:qw, 0:W]
            t = K.red(sc[:, 0:1], s_, MAX, t, neg=True)
            t = K.act(Pt, s_, ACT.Exp, t, bias=sc[:, 0:1], accum=sc[:, 1:2])
            P.free(b, nb, t)
            pr.append((Pt, sc, t))
        K.rec(pr[0][1][:, 2:3], pr[0][1][:, 1:2], pr[0][2])
        K.rec(pr[1][1][:, 2:3], pr[1][1][:, 1:2], t)
        K.tt(pr[1][1][:, 2:3], pr[1][1][:, 2:3], lam[0:qw, 4:5], MUL)
        K.ts(pr[1][0], pr[1][0], pr[1][1][:, 2:3], None, MUL, None)
        return pr[0][0], K.stt(pr[0][0], pr[0][0], pr[0][1][:, 2:3], pr[1][0], MUL, ADD)

    def values(hd, i, aw, t):
        d = bufs[hd % 2]
        q0, qw = TK[i]
        nb = 2 if i == 4 else 1
        b, fr = P.banks(nb)
        m0 = 512 * b if i == 4 else 512 * b + 128 * i
        n0 = 512 * (b + 1) if i == 4 else 512 * b
        t2 = K.tr(K.ps[0:16, m0:m0 + qw], aw[:, 0:16], fr, t)
        for j in range(1, i + 1):
            t2 = K.tr(K.ps[:, n0 + 128 * (j - 1):n0 + 128 * j], aw[:, TK[j][0]:TK[j][0] + 128])
        a = d[f"aw{i % 2}"]
        am = d["am"][0:16, 128 * (i % 2):128 * (i % 2) + qw]
        t3 = K.act(am, K.ps[0:16, m0:m0 + qw], ACT.Copy, t2)
        if i:
            t3 = K.act(a[:, 0:128 * i], K.ps[:, n0:n0 + 128 * i], ACT.Copy)
        P.free(b, nb, t3)
        step()
        bo, fro = d["bo"]
        o = K.ps[:, 512 * bo + 496 + q0:512 * bo + 496 + q0 + qw]
        tO = K.mm(o, d["V"][0:16, 0:128], am, True, i == 0, fro, t3)
        for j in range(1, i + 1):
            tO = K.mm(o, d["V"][:, 128 * j:128 * j + 128], a[:, 128 * (j - 1):128 * j], False, j == i)
        if i < 4:
            return None
        t = K.act(d["O"], K.ps[:, 512 * bo + 496:512 * bo + 1024], ACT.Copy, tO)
        P.free(bo, 2, t)
        P.held -= {bo, bo + 1}
        t = K.act(d["t2"], d["O"], ACT.Square)
        step()
        b, n, t = K.colsum(c["ones"], [d["t2"]], T, t)
        K.rstd(d["t1"], b, n, T, 1.0 / 128, c["eps5"], t)
        tod = K.stt(od[:, hd * T:hd * T + T], d["O"], lam[:, 5:6], d["t1"], MUL, MUL)
        old[hd % 2] = P.marks()
        if hd < 6:
            work.append(project(hd + 2))
        return tod

    work.append(project(0))
    drain()
    work.append(project(1))
    behind = None
    for hd in range(8):
        while hd not in tqv:
            step()
        for i in range(5):
            cur = (hd, i, *scores(hd, i))
            step()
            if behind:
                tod = values(*behind)
            if i == 0:
                bufs[hd % 2]["bo"] = P.banks(2)
                P.held |= {bufs[hd % 2]["bo"][0], bufs[hd % 2]["bo"][0] + 1}
            step()
            behind = cur
    tod = values(*behind)
    drain()
    K.P.gate(P.marks())
    K.top = mark + 16 * T
    sg = [K.sb(T) for _ in range(2)]
    mg, odh, mgh = K.sb(8 * T), K.sb(8 * T), K.sb(8 * T)
    wh = [K.sb(1024) for _ in range(3)]
    for q in (od, odh, mg, mgh):
        K.alias(q, T)
    ws = Weights(K, run_of(32), wh)
    tsp = [thh]
    tmg, thr = [], []
    for k in range(8):
        b, n, t = K.lin3(ws, (hh, h), T, w=tsp[0])
        t0 = K.act(h2(sg[0]), K.view(b, n, T), ACT.Sigmoid, t, P.last["dve"])
        P.free(b, n, t0)
        if k == 0:
            tsp.append(K.split_tiles(od, odh, T, 8))
        b, n, t = K.lin3(ws, (hh, h), T)
        t1 = K.act(h2(sg[1]), K.view(b, n, T), ACT.Sigmoid, t)
        P.free(b, n, t1)
        b, n, t = K.lin3(ws, (odh, od), T, w=tsp[1])
        K.tt(sg[0], sg[0], orw[:, k * T:k * T + T], MUL, t0)
        t = K.tt(h2(sg[1]), h2(sg[1]), K.view(b, n, T), MUL, t, t1)
        P.free(b, n, t)
        tm = K.tt(mg[:, k * T:k * T + T], sg[0], sg[1], ADD)
        tmg.append(K.split(mg[:, k * T:k * T + T], mgh[:, k * T:k * T + T], tm, eng="pool"))
    hres = orw
    ld = P.dma(hres, xT, tm)
    for k in range(8):
        b, n, t = K.lin3(ws, (mgh, mg), T, w=tmg)
        t = K.tt(h2(hres[:, k * T:k * T + T]), h2(hres[:, k * T:k * T + T]), K.view(b, n, T), ADD, t, ld)
        P.free(b, n, t)
        thr.append(t)
    tr_ = t
    tlast = ws.slabs[-1].done
    K.top = mark + 8 * T
    rs = K.sb(T)
    rl = [K.sb(T) for _ in range(2)]
    Hh, Hl = K.sb(16 * T), K.sb(16 * T)
    wh = [K.sb(1024) for _ in range(3)]
    for q in (h, oy, Hh, Hl):
        K.alias(q, T)
    up, down = run_of(32), run_of(32)
    ws = Weights(K, [x for half in range(2) for x in up[16 * half:16 * half + 16] +
                     [down[4 * k + 2 * half + g] for k in range(8) for g in range(2)]], wh, tlast)
    th = K.rms(hres, p["nmlp"], h, T, c["eps5"], Hh, rs, per=thr, hi=oy)
    tsq = [tr_, tr_]
    tdown = None
    for half in range(2):
        for k in range(16):
            b, n, t = K.lin3(ws, (oy, h), T, w=th)
            t = K.act(h2(rl[k % 2]), K.view(b, n, T), ACT.Relu, t, tsq[k % 2])
            P.free(b, n, t)
            S = slice(k * T, k * T + T)
            tsq[k % 2] = K.tt(Hl[:, S], rl[k % 2], rl[k % 2], MUL, t, tdown)
            tH = K.split(Hl[:, S], Hh[:, S])
        thr = []
        for k in range(8):
            b, fr = P.banks(2)
            out2 = lambda j: K.ps[:, 512 * (b + j):512 * (b + j) + 264]
            for g in range(2):
                s = ws.take()
                for kk in range(8):
                    kx = 8 * g + kk
                    t = K.mm3(out2, s.hi[:, kk, :], s.ap[:, kk, :], (Hh, Hl), T, kx, kx == 0, kx == 15, s.ready, fr, tH)
                s.done = tdown = t
            t = K.tt(h2(hres[:, k * T:k * T + T]), h2(hres[:, k * T:k * T + T]), K.view(b, 2, T), ADD, t)
            P.free(b, 2, t)
            thr.append(t)
    t = K.rms(hres, p["fin"], out, T, c["eps5"], oy, rs, per=thr, o0=16)
    K.phase(base + 8 * 512)
    return out, t


def block2(K, x, x_tok):
    P, c, p, T = K.P, K.c, K.p, T2
    h = K.sb(8 * T)
    O = K.sb(12 * T)
    rs = K.sb(T)
    th = K.lnorm(x, p["ln0_g"], p["ln0_b"], h, T, c["eps5"], O, rs, x_tok)
    mark = K.top

    def bc4(ap):
        return ap.unsqueeze(1).to_broadcast([128, 4, 128])

    def v4(ap):
        return ap.rearrange("p (j t) -> p j t", j=4)

    def evac(out, b, t, f=ACT.Copy, *w, **kw):
        t = K.act(out, K.bank(b), f, t, *w, **kw)
        P.free(b, 1, t)
        return t

    now = [None]

    def slab_of():
        s = K.slab(off=now[0][1])
        now[0][1] += 1024
        return s

    def glin(w=()):
        s = slab_of()
        b, fr = P.banks(1)
        P.held.add(b)
        for k in range(8):
            t = K.mm(K.bank(b), s.ap[:, k, :], h[:, k * T:k * T + T], k == 0, k == 7, fr, s.tok, *w)
            if k in (2, 5):
                yield
        s.done = t
        P.held.discard(b)
        return b, 1, t

    def v_tile(out):
        s = slab_of()
        b, fr = P.banks(1)
        P.held.add(b)
        for j in range(4):
            for k in range(8):
                t = K.mm(K.bank(b)[:, 128 * j:128 * j + 128], h[:, k * T + 128 * j:k * T + 128 * j + 128], s.ap[:, k, :],
                         k == 0, k == 7, fr, s.tok)
            if j < 3:
                yield
        s.done = t
        P.held.discard(b)
        return evac(out, b, t)

    def gated(bo, tO, ncol, gate, out, o, q, r):
        t = evac(o, bo, tO)
        P.held.discard(bo)
        t = K.act(q, o, ACT.Square)
        yield
        b, n, t = K.colsum(c["ones"], [q], T, t)
        K.rstd(r, b, n, T, 1.0 / 128, c["eps6"], t)
        K.stt(o, o, ncol, r, MUL, MUL)
        return K.tt(out, o, gate, MUL)

    s = K.slab()
    LR = K.sb(T)
    b, n, t = K.lin_slab(s, h, T, 0, 8, 16, w=[th])
    tlr = K.act(LR[0:16], K.ps[0:16, 512 * b:512 * b + T], ACT.Copy, t)
    P.free(b, 1, tlr)
    b, fr = P.banks(1)
    for j in range(4):
        for k in range(8):
            t = K.mm(K.bank(b)[:, 8 * j:8 * j + 8], h[:, k * T + 128 * j:k * T + 128 * j + 128], s.ap[:, k, 16:24], k == 0, k == 7, fr)
    s.done = t
    sm = K.bank(b)[:, 0:32].rearrange("p (j e) -> p j e", e=8)
    G = {n: K.sb(16) for n in ("be", "nbe", "v", "sp", "g", "cu", "to", "ec", "el", "eks", "bec", "ea", "s", "s2")}
    g4 = lambda n: G[n].rearrange("p (j e) -> p j e", e=4)
    t = K.act(g4("be"), sm[:, :, 0:4], ACT.Sigmoid, t)
    tdt = K.tt(g4("v"), sm[:, :, 4:8], p["dtb"].unsqueeze(1).to_broadcast([128, 4, 4]), ADD, t)
    P.free(b, 1, tdt)
    CT = K.sb(128)

    def rates():
        K.act(G["sp"], G["v"], ACT.Abs, tdt)
        K.act(G["sp"], G["sp"], ACT.Exp, scale=-1.0)
        t = K.act(G["ea"][:, 0:4], p["alog"], ACT.Exp)
        K.ts(G["s"], G["sp"], 2.0, None, ADD, None, t)
        K.rec(G["s"], G["s"])
        K.tt(G["s"], G["s"], G["sp"], MUL)
        K.tt(G["s2"], G["s"], G["s"], MUL)
        K.ts(G["sp"], G["s2"], 1.0 / 17, None, MUL, None)
        for k in (15, 13, 11, 9, 7, 5, 3):
            K.stt(G["sp"], G["sp"], 1.0 / k, G["s2"], ADD, MUL)
        K.stt(G["sp"], G["sp"], 1.0, G["s"], ADD, MUL)
        K.ts(G["s2"], G["v"], 0.0, None, MAX, None)
        K.stt(G["sp"], G["sp"], 2.0, G["s2"], MUL, ADD)
        t = K.stt(g4("g"), g4("sp"), -1.0, G["ea"][:, 0:4].unsqueeze(1).to_broadcast([128, 4, 4]), MUL, MUL)
        yield
        b, fr = P.banks(1)
        K.mm(K.bank(b)[:, 0:16], c["triu"], G["g"], True, True, fr, t)
        t = K.mm(K.bank(b)[:, 16:32], c["ones"], G["g"], True, True)
        K.cp(G["cu"], K.bank(b)[:, 0:16], t)
        t = K.cp(G["to"], K.bank(b)[:, 16:32])
        P.free(b, 1, t)
        K.tt(G["eks"], G["to"], G["cu"], SUB)
        t = K.ts(G["nbe"], G["be"], -1.0, None, MUL, None)
        K.act(G["ec"], G["cu"], ACT.Exp, t)
        K.act(G["el"], G["to"], ACT.Exp)
        t = K.act(G["eks"], G["eks"], ACT.Exp)
        K.tt(G["bec"], G["be"], G["ec"], MUL, t)
        t = P.last["dve"]
        yield
        b, fr = P.banks(1)
        t = K.tr(K.bank(b)[0:16, 0:128], G["cu"], fr, t)
        tct = K.cp(CT[0:16], K.bank(b)[0:16, 0:128], t)
        P.free(b, 1, tct)
        return tct

    s16 = c["sel16"].rearrange("p (e j) -> p e j", e=16)
    keep = K.top

    pad = [K.sb(516) for _ in range(2)]
    for q in pad:
        tz = K.ms(q[:, 0:3], 0.0)
    U = {n: K.sb(T) for n in ("q", "k", "v", "g", "er", "D", "DT", "A", "AT", "XT", "M", "VB", "KB", "KS", "qi", "u", "wT",
                              "n0", "n1")}
    St = [K.sb(128) for _ in range(2)]
    U.update((n, K.sb(128)) for n in ("ATp", "Xp", "XTp", "M0", "M1", "Yp"))
    U["Y"] = K.sb(256)
    K.ms(U["XT"], 0.0)

    def w4(ap):
        return ap[:, 0:128].rearrange("p (j t) -> p j t", j=4)

    def pk(n):
        return c[n].unsqueeze(1).to_broadcast([128, 4, 32])

    def delta():
        tct = yield from rates()
        old = None
        for hd in range(4):
            if old:
                P.gate(old, ("act", "dve"))
            tp = {}
            tcv = [None, None]
            for i, nme in enumerate("qkv"):
                b, n, t = yield from glin([th])
                pp = pad[i % 2]
                t = K.act(pp[:, 3:515], K.bank(b), ACT.Copy, t, tz, tcv[i % 2])
                P.free(b, 1, t)
                w = p["conv"][:, 16 * i + 4 * hd:16 * i + 4 * hd + 4]
                K.ts(U[nme], pp[:, 0:512], w[:, 0:1], None, MUL, None, t)
                for k in range(1, 4):
                    t = K.stt(U[nme], pp[:, k:k + 512], w[:, k:k + 1], U[nme], MUL, ADD)
                tcv[i % 2] = t
                tp[nme] = K.act(U[nme], U[nme], ACT.Silu, t)
                if nme != "v":
                    sq_, r_ = ("n0", "n1") if nme == "q" else ("u", "wT")
                    t = K.act(U[sq_], U[nme], ACT.Square)
                    yield
                    b, n, t = K.colsum(c["ones"], [U[sq_]], T, t)
                    K.rstd(U[r_], b, n, T, 1.0, c["eps6"], t)
                    tp[nme] = K.stt(U[nme], U[nme], 128.0 ** -0.5 if nme == "q" else 1.0, U[r_], MUL, MUL)
            b, n, t = yield from glin()
            tg = evac(U["g"], b, t, ACT.Silu)
            yield
            b, fr = P.banks(1)
            for j in range(4):
                t = K.mm(K.bank(b)[:, 128 * j:128 * j + 128], s16[0:16, 4 * j + hd, :], CT[0:16], True, True, fr, tct)
            ter = K.act(U["er"], K.bank(b), ACT.Exp, t)
            def col(n):
                return G[n].rearrange("p (j e) -> p j e", e=4)[:, :, hd:hd + 1].to_broadcast([128, 4, 128])

            t = K.tt(v4(U["D"]), v4(K.bank(b)), col("cu"), SUB, ter)
            P.free(b, 1, t)
            K.act(U["DT"], U["D"], ACT.Relu, t, scale=-1.0)
            K.act(U["D"], U["D"], ACT.Relu)
            K.act(U["D"], U["D"], ACT.Exp, scale=-1.0)
            t = K.act(U["DT"], U["DT"], ACT.Exp, scale=-1.0)
            K.tt(v4(U["D"]), v4(U["D"]), bc4(c["slo"]), MUL, t)
            K.tt(v4(U["DT"]), v4(U["DT"]), bc4(c["triu"]), MUL)
            t = K.tt(U["qi"], U["q"], U["er"], MUL)
            yield
            b, fr = P.banks(1)
            for j in range(4):
                J = slice(128 * j, 128 * j + 128)
                t = K.mm(K.bank(b)[:, J], U["k"][:, J], U["k"][:, J], True, True, fr, tp["k"], t)
            for j in range(4):
                J = slice(128 * j, 128 * j + 128)
                ta = K.stt(U["A"][:, J], K.bank(b)[:, J], G["nbe"][:, 4 * j + hd:4 * j + hd + 1], U["D"][:, J], MUL, MUL, t)
            P.free(b, 1, ta)
            b, fr = P.banks(1)
            for j in range(4):
                J = slice(128 * j, 128 * j + 128)
                t = K.mm(K.bank(b)[:, J], U["k"][:, J], U["q"][:, J], True, True, fr)
            tM = K.tt(U["M"], K.bank(b), U["DT"], MUL, t)
            P.free(b, 1, tM)
            for src in "vk":
                b, fr = P.banks(1)
                for j in range(4):
                    J = slice(128 * j, 128 * j + 128)
                    t = K.tr(K.bank(b)[:, J], U[src][:, J], fr, tp["v"])
                if src == "v":
                    t = K.tt(v4(U["VB"]), v4(K.bank(b)), col("be"), MUL, t)
                else:
                    K.tt(v4(U["KB"]), v4(K.bank(b)), col("bec"), MUL, t)
                    t = K.tt(v4(U["KS"]), v4(K.bank(b)), col("eks"), MUL)
                P.free(b, 1, t)
            tkb = t
            yield
            b, fr = P.banks(1)
            for j in range(4):
                J = slice(128 * j, 128 * j + 128)
                t = K.tr(K.bank(b)[:, J], U["A"][:, J], fr, ta)
            for q in range(4):
                Q = slice(32 * q, 32 * q + 32)
                tat = K.act(w4(U["ATp"])[Q], v4(K.bank(b))[Q, :, Q], ACT.Copy, t)
            ta2 = K.act(U["AT"], K.bank(b), ACT.Copy)
            P.free(b, 1, ta2)

            def four(l, r, *w):
                b, fr = P.banks(1)
                for j in range(4):
                    J = slice(128 * j, 128 * j + 128)
                    t = K.mm(K.bank(b)[:, J], U[l][:, J], U[r][:, J], True, True, fr, *w)
                return b, t

            def blocks(l, r, *w):
                b, fr = P.banks(1)
                for j in range(4):
                    for q in range(4):
                        Q, I = slice(32 * q, 32 * q + 32), slice(32 * j, 32 * j + 32)
                        t = K.mm(K.bank(b)[Q, I], U[l][Q, I], U[r][Q, I], True, True, fr, *w)
                return b, t

            for q in range(4):
                Q = slice(32 * q, 32 * q + 32)
                K.tt(w4(U["Xp"])[Q], v4(U["A"])[Q, :, Q], pk("pl1")[Q], MUL)
            K.tt(w4(U["Xp"]), w4(U["Xp"]), pk("pid"), ADD)
            K.tt(w4(U["XTp"]), w4(U["ATp"]), pk("pu1"), MUL, tat)
            K.tt(w4(U["XTp"]), w4(U["XTp"]), pk("pid"), ADD)
            tx = tm = K.tt(w4(U["M0"]), w4(U["ATp"]), pk("pu2"), MUL)
            yield
            for i, l in enumerate((2, 4, 8, 16)):
                b, t = blocks(("M0", "M1")[i % 2], "Xp", tm, tx)
                ty = K.act(U["Yp"], K.bank(b)[:, 0:128], ACT.Copy, t)
                P.free(b, 1, ty)
                if l < 16:
                    tm = K.tt(w4(U[("M1", "M0")[i % 2]]), w4(U["ATp"]), pk(f"pu{2 * l}"), MUL)
                yield
                bz, tz2 = blocks("XTp", "Yp", ty)
                b, t2 = blocks("Yp", "XTp")
                t3 = K.tt(U["Xp"], U["Xp"], K.bank(bz)[:, 0:128], ADD, tz2)
                P.free(bz, 1, t3)
                tx = K.tt(U["XTp"], U["XTp"], K.bank(b)[:, 0:128], ADD, t2)
                P.free(b, 1, tx)
                yield
            b, fr = P.banks(1)
            for j in range(4):
                for o in (0, 64):
                    I = slice(32 * j, 32 * j + 32)
                    t = K.mm(K.bank(b)[o + 32:o + 64, I], U["AT"][o:o + 32, 128 * j + o + 32:128 * j + o + 64], U["Xp"][o:o + 32, I],
                             True, True, fr, tx, ta2)
            for o in (0, 64):
                ty = K.act(U["Yp"][o + 32:o + 64], K.bank(b)[o + 32:o + 64, 0:128], ACT.Copy, t)
            P.free(b, 1, ty)
            K.act(U["M0"][0:32], U["Xp"][0:32], ACT.Copy)
            for q in range(4):
                Q = slice(32 * q, 32 * q + 32)
                te = K.act(v4(U["XT"])[Q, :, Q], w4(U["XTp"])[Q], ACT.Copy)
            yield
            bz, fr = P.banks(1)
            b, fr2 = P.banks(1)
            for j in range(4):
                I = slice(32 * j, 32 * j + 32)
                tz2 = K.mm(K.bank(bz)[32:64, I], U["XTp"][32:64, I], U["Yp"][32:64, I], True, True, fr, ty)
            for j in range(4):
                for o in (0, 64):
                    I = slice(32 * j, 32 * j + 32)
                    t = K.mm(K.bank(b)[o:o + 32, I], U["Yp"][o + 32:o + 64, I], U["XTp"][o + 32:o + 64, I], True, True, fr2)
            tz2 = K.act(U["M0"][32:64], K.bank(bz)[32:64, 0:128], ACT.Copy, tz2)
            P.free(bz, 1, tz2)
            for o in (0, 64):
                tx = K.cp(v4(U["XT"])[o:o + 32, :, o + 32:o + 64], w4(K.bank(b))[o:o + 32], t)
            P.free(b, 1, tx)
            yield
            b, fr = P.banks(1)
            for j in range(4):
                I = slice(32 * j, 32 * j + 32)
                K.mm(K.bank(b)[64:128, 64 * j:64 * j + 32], U["AT"][0:64, 128 * j + 64:128 * j + 128], U["M0"][0:64, I],
                     True, True, fr, tz2)
                t = K.mm(K.bank(b)[64:128, 64 * j + 32:64 * j + 64], U["AT"][32:64, 128 * j + 64:128 * j + 128], U["Xp"][32:64, I],
                         True, True)
            ty = K.act(U["Y"][64:128], K.bank(b)[64:128, 0:256], ACT.Copy, t)
            P.free(b, 1, ty)
            yield
            b, fr = P.banks(1)
            for j in range(4):
                t = K.mm(K.ps[0:64, 512 * b + 64 * j:512 * b + 64 * j + 64], U["Y"][64:128, 64 * j:64 * j + 64],
                         U["XT"][64:128, 128 * j + 64:128 * j + 128], True, True, fr, ty, te, tx)
            tx = K.cp(v4(U["XT"])[0:64, :, 64:128],
                      K.ps[0:64, 512 * b:512 * b + 256].rearrange("p (j t) -> p j t", j=4), t)
            P.free(b, 1, tx)
            yield
            b, t = four("XT", "VB", tx, tkb)
            tu = K.cp(U["u"], K.bank(b), t)
            P.free(b, 1, tu)
            b, t = four("KB", "XT")
            tw = evac(U["wT"], b, t)
            bo, fro = P.banks(1)
            P.held.add(bo)
            yield
            tS = None
            tO = None
            for j in range(4):
                J = slice(128 * j, 128 * j + 128)
                so, sn = St[j % 2], St[(j + 1) % 2]
                tv = tu
                if j:
                    b, fr = P.banks(1)
                    t = K.mm(K.bank(b)[:, 0:128], U["wT"][:, J], so, True, True, fr, tS, tw)
                    tv = K.tt(U["u"][:, J], U["u"][:, J], K.bank(b)[:, 0:128], SUB, t)
                    P.free(b, 1, tv)
                yield
                if j < 3:
                    b, fr = P.banks(1)
                    t = K.mm(K.bank(b)[:, 0:128], U["KS"][:, J], U["u"][:, J], True, True, fr, tv)
                    if j:
                        tn = K.stt(sn, so, G["el"][:, 4 * j + hd:4 * j + hd + 1], K.bank(b)[:, 0:128], MUL, ADD, t, tO)
                    else:
                        tn = K.cp(sn, K.bank(b)[:, 0:128], t)
                    P.free(b, 1, tn)
                    yield
                o = K.bank(bo)[:, J]
                tO = K.mm(o, U["u"][:, J], U["M"][:, J], True, j == 0, fro, tv, tM)
                if j:
                    tO = K.mm(o, so, U["qi"][:, J], False, True)
                tS = tn
            yield from gated(bo, tO, p["gdnn"], U["g"], O[:, hd * T:hd * T + T], U["n0"], U["n1"], U["D"])
            old = P.marks()

    W = {n: x[:, i * T:i * T + T] for i, n in enumerate(("q", "k", "cum", "E", "Q", "Kz", "ks", "la"))}
    W.update((n, K.sb(T)) for n in ("t0", "t1", "n0", "n1", "n2"))
    V = [K.sb(T) for _ in range(2)]
    Gt = [K.sb(T) for _ in range(2)]
    acc = [K.sb(T) for _ in range(2)]
    Sg = [K.sb(128) for _ in range(2)]
    el = K.sb(8)
    u32 = mybir.dt.uint32

    oldg = []

    def decay_attention(heads, rows, tqk, tv, tg, ncol, out0):
        told = oldg[-1] if oldg else None
        for i in range(heads):
            tz0 = K.ms(acc[i], 0.0, told, eng="pool")
        def decays(n, l):
            nb = T // (2 * l)
            cu, E = (W[x].rearrange("p (b t) -> p b t", t=2 * l) for x in ("cum", "E"))
            ref = cu[:, :, l - 1:l].to_broadcast([128, nb, l])
            K.tt(E[:, :, l:2 * l], cu[:, :, l:2 * l], ref, SUB, tE[0])
            t = K.tt(E[:, :, 0:l], ref, cu[:, :, 0:l], SUB)
            te = K.act(W["E"], W["E"], ACT.Exp, t)
            qn, kn = (("Q", "Kz"), ("n0", "n1"))[n % 2]
            K.tt(W[qn], W["q"], W["E"], MUL, te, tmm[n % 2])
            tE[0] = K.tt(W[kn], W["k"], W["E"], MUL, te, tqk, tmm[n % 2], eng="pool")
            return kn, qn, [tE[0], P.last["dve"]]

        tmm, tE = [None, None], [None]
        lv = (0,) + LEVELS[::-1]
        nxt = ("k", "q", tqk)
        for n, l in enumerate(lv):
            a, bb, t = nxt
            got = []
            for i in range(heads):
                R = slice(rows * i, rows * i + rows)
                b, fr = P.banks(1)
                for j in range(4):
                    J = slice(128 * j, 128 * j + 128)
                    tl = K.mm(K.bank(b)[:, J], W[a][R, J], W[bb][R, J], True, True, fr, t)
                got.append((b, tl))
            if n:
                tmm[n % 2] = tl
            if n + 1 < len(lv):
                nxt = decays(n + 1, lv[n + 1])
            m = c[f"u{l}"] if l else c["ident"]
            for i, (b, tl) in enumerate(got):
                ta = K.cpred(v4(acc[i]), bc4(m.bitcast(u32)), v4(K.bank(b)), tl, tz0)
                P.free(b, 1, ta)
            yield
        cu = v4(W["cum"])
        t = K.tt(v4(W["E"]), cu[:, :, 127:128].to_broadcast([128, 4, 128]), cu, SUB, tE[0])
        K.act(W["E"], W["E"], ACT.Exp, t)
        K.act(el[:, 0:4].unsqueeze(2), cu[:, :, 127:128], ACT.Exp)
        t = K.act(W["cum"], W["cum"], ACT.Exp)
        K.tt(W["Kz"], W["k"], W["E"], MUL, t, tl)
        t = K.tt(W["Q"], W["q"], W["cum"], MUL)
        yield
        b, fr = P.banks(1)
        for j in range(4):
            J = slice(128 * j, 128 * j + 128)
            t2 = K.tr(K.bank(b)[:, J], W["Kz"][:, J], fr, t)
        tks = evac(W["ks"], b, t2)
        bo = []
        for i in range(heads):
            b, fro = P.banks(1)
            P.held.add(b)
            bo.append((b, fro))
        yield
        tS, tn, tO = None, None, None
        for j in range(4):
            J = slice(128 * j, 128 * j + 128)
            so, sn = Sg[j % 2], Sg[(j + 1) % 2]
            if j < 3:
                b, fr = P.banks(1)
                for i in range(heads):
                    R = slice(rows * i, rows * i + rows)
                    t = K.mm(K.ps[R, 512 * b:512 * b + 128], W["ks"][:, 128 * j + rows * i:128 * j + rows * i + rows], V[i][:, J],
                             True, True, fr, tks, tv)
                if j:
                    tn = K.stt(sn, so, el[:, j:j + 1], K.bank(b)[:, 0:128], MUL, ADD, t, tO)
                else:
                    tn = K.cp(sn, K.bank(b)[:, 0:128], t)
                P.free(b, 1, tn)
                yield
            for i in range(heads):
                R = slice(rows * i, rows * i + rows)
                o = K.bank(bo[i][0])[:, J]
                tO = K.mm(o, V[i][:, J], acc[i][:, J], True, j == 0, bo[i][1], ta, tv)
                if j:
                    tO = K.mm(o, so[R, :], W["Q"][R, J], False, True, tS)
            tS = tn
        for i in range(heads):
            yield from gated(bo[i][0], tO, ncol, Gt[i], O[:, (out0 + i) * T:(out0 + i) * T + T],
                  *((W["n0"], W["n1"], W["n2"]) if i == 0 else (W["la"], W["t0"], W["t1"])))
        oldg.append(P.marks())

    def linear():
        for pr in range(2):
            if oldg:
                P.gate(oldg[-1], ("act", "dve"))
            b, n, t = yield from glin()
            evac(W["q"], b, t, ACT.Copy, scale=0.125)
            b, n, t = yield from glin()
            tqk = evac(W["k"], b, t)
            for i in range(2):
                tv = yield from v_tile(V[i])
                b, n, t = yield from glin()
                tg = evac(Gt[i], b, t, ACT.Silu)
            b, fr = P.banks(1)
            t = K.mm(K.bank(b), p["glaw2"][0:16, 128 * pr:128 * pr + 128], LR[0:16], True, True, fr, tlr)
            logsig(K, W["la"], K.bank(b), p["glab2"][:, pr:pr + 1], (W["t0"], W["t1"], None), t, b)
            K.ts(W["la"], W["la"], 1.0 / 16, None, MUL, None)
            K.scan(W["cum"], c["rst128"], W["la"])
            yield
            yield from decay_attention(2, 64, tqk, tv, tg, p["glan"], 4 + 2 * pr)

        L = {n: K.sb(4) for n in ("m", "e", "r", "lb", "om", "llb", "l1")}
        K.tt(L["m"], p["lb"], p["lb"], MAX)
        t = K.tt(L["e"], p["lb"], L["m"], SUB)
        t = K.act(L["e"], L["e"], ACT.Exp, t)
        K.rec(L["r"], L["e"], t)
        K.tt(L["e"], L["e"], L["r"], MUL)
        K.tt(L["lb"], L["e"], L["e"], SUB)
        K.ts(L["lb"], L["lb"], 0.0, 1.0, MAX, MIN)
        K.ts(L["om"], L["lb"], -1.0, 1.0, MUL, ADD)
        t = K.ts(L["llb"], L["lb"], 1e-30, None, MAX, None)
        K.act(L["llb"], L["llb"], ACT.Sqrt, t)
        K.act(L["llb"], L["llb"], ACT.Ln)
        t = K.act(L["l1"], L["om"], ACT.Ln)
        K.ts(L["llb"], L["llb"], 2.0, None, MUL, None, t)
        for hd in range(4):
            H1 = slice(hd, hd + 1)
            P.gate(oldg[-1], ("act", "dve"))
            b, n, t = yield from glin()
            t = evac(W["q"], b, t, ACT.Silu)
            K.ts(W["q"], W["q"], 128.0 ** -0.5, None, MUL, None, t)
            b, n, t = yield from glin()
            K.act(W["k"], K.bank(b), ACT.Sigmoid, t, scale=-1.0)
            t = evac(W["t0"], b, t)
            tqk = K.ts(W["k"], W["k"], L["om"][:, H1], None, MUL, None, t)
            K.act(W["t1"], W["t0"], ACT.Abs)
            K.act(W["t1"], W["t1"], ACT.Exp, scale=-1.0)
            t = K.act(W["t1"], W["t1"], ACT.Ln, bias=c["one"])
            K.stt(W["t0"], W["t0"], 0.0, W["t1"], MIN, SUB, t)
            K.ts(W["t0"], W["t0"], L["l1"][:, H1], None, ADD, None)
            t = K.ts(W["t1"], W["t0"], L["llb"][:, H1], None, SUB, None)
            K.act(W["t1"], W["t1"], ACT.Abs, t)
            K.act(W["t1"], W["t1"], ACT.Exp, scale=-1.0)
            t = K.act(W["t1"], W["t1"], ACT.Ln, bias=c["one"])
            K.stt(W["la"], W["t0"], L["llb"][:, H1], W["t1"], MAX, ADD, t)
            K.scan(W["cum"], c["rst128"], W["la"])
            tv = yield from v_tile(V[0])
            b, n, t = yield from glin()
            tg = evac(Gt[0], b, t, ACT.Silu)
            yield
            yield from decay_attention(1, 128, tqk, tv, tg, p["hgrnn"], 8 + hd)

    runs = [[delta(), K.woff], [linear(), K.woff + 16 * 1024]]
    now[0] = runs[0]
    for _ in range(6):
        next(runs[0][0])
    while runs:
        for r in list(runs):
            now[0] = r
            try:
                next(r[0])
            except StopIteration:
                runs.remove(r)
    K.woff += 44 * 1024
    K.phase(mark)

    def run_of(n, size=1024):
        K.woff += n * size
        return [(K.woff - (n - i) * size, size) for i in range(n)]

    y = x
    sg = [K.sb(T) for _ in range(2)]
    hh, Oh = K.sb(8 * T), K.sb(12 * T)
    wh = [K.sb(1024) for _ in range(3)]
    for q in (h, hh, O, Oh, y):
        K.alias(q, T)
    offs = []
    for k in range(24):
        offs += run_of(1) + run_of(1, 512)
    ws = Weights(K, offs + run_of(8), wh)
    tsh = [K.split(h[:, k * T:k * T + T], hh[:, k * T:k * T + T], eng="pool" if k % 3 == 2 else "dve") for k in range(8)]
    tsO = []
    tsg = [None, None]
    i = 0
    ty, per = [], []
    for k in range(8):
        ys = y[:, k * T:k * T + T]
        for br in range(3):
            b, n, t = K.lin3(ws, (hh, h), T, w=tsh)
            t = K.act(sg[i % 2], K.bank(b), ACT.Sigmoid, t, tsg[i % 2])
            P.free(b, 1, t)
            if k == 0:
                tsO += [K.split(O[:, j * T:j * T + T], Oh[:, j * T:j * T + T], eng="pool") for j in range(4 * br, 4 * br + 4)]
            b, n, t2 = K.lin3(ws, (Oh, O), T, nk=4, x0=4 * br, w=tsO)
            if br == 0:
                tsg[i % 2] = K.tt(ys, sg[i % 2], K.bank(b), MUL, t, t2)
                P.free(b, 1, tsg[i % 2])
            else:
                t = K.tt(sg[i % 2], sg[i % 2], K.bank(b), MUL, t, t2)
                P.free(b, 1, t)
                tsg[i % 2] = t = K.tt(ys, ys, sg[i % 2], ADD)
            i += 1
    yh = Oh
    ty = [K.split(y[:, k * T:k * T + T], yh[:, k * T:k * T + T], t2, eng="pool" if k % 3 == 2 else "dve") for k in range(8)]
    for k in range(8):
        hs = h[:, k * T:k * T + T]
        t = K.tt(hs, K.r(hs), K.r(hh[:, k * T:k * T + T]), ADD)
        b, n, t = K.lin3(ws, (yh, y), T, w=ty)
        t = K.stt(hs, hs, ALPHA, K.bank(b), MUL, ADD, t)
        P.free(b, 1, t)
        per.append(t)
    th = K.lnorm(h, p["ln1_g"], p["ln1_b"], x, T, c["eps5"], O, rs, per=per)
    K.phase(mark)

    xh = O[:, 0:8 * T]
    sg = [O[:, (8 + i) * T:(9 + i) * T] for i in range(2)]
    Hh, Hl = K.sb(16 * T), K.sb(16 * T)
    wh = [K.sb(1024), K.sb(1024), O[:, 10 * T:12 * T]]
    for q in (x, xh, Hh, Hl):
        K.alias(q, T)
    up, down = run_of(64), run_of(32)
    ws = Weights(K, [q for half in range(2) for q in up[32 * half:32 * half + 32] +
                     [down[4 * k + 2 * half + g] for k in range(8) for g in range(2)]], wh)
    R = {n: K.sb(64) for n in ("sc", "sel", "gs", "tmp", "f", "kp", "w", "cnt")}
    e3 = lambda n: R[n].rearrange("p (a e) -> p a e", e=4)
    b, fr = P.banks(1)
    for j in range(4):
        for k in range(8):
            t = K.mm(K.bank(b)[:, 16 * j:16 * j + 16], x[:, k * T + 128 * j:k * T + 128 * j + 128], p["wr"][:, 16 * k:16 * k + 16],
                     k == 0, k == 7, fr, th)
    trt = t
    t = K.act(R["sc"], K.bank(b)[:, 0:64], ACT.Sigmoid, t)
    P.free(b, 1, t)
    tx = [K.split(x[:, k * T:k * T + T], xh[:, k * T:k * T + T], trt, eng="pool" if k % 3 == 2 else "dve") for k in range(8)]
    K.tt(R["sel"].rearrange("p (j e) -> p j e", e=16), R["sc"].rearrange("p (j e) -> p j e", e=16),
         p["rb"].unsqueeze(1).to_broadcast([128, 4, 16]), ADD, t)
    sel = [e3("sel")[:, :, e] for e in range(4)]
    gs, tmp = R["gs"][:, 0:16], R["tmp"][:, 0:16]
    first = True
    for a in range(4):
        for b_ in range(a + 1, 4):
            K.tt(gs if first else tmp, sel[a], sel[b_], ADD)
            if not first:
                K.tt(gs, gs, tmp, MAX)
            first = False
    gs3 = gs.rearrange("p (j g) -> p j g", g=4)
    K.red(R["tmp"][:, 16:20], gs3, MAX)
    f3 = R["f"][:, 0:16].rearrange("p (j g) -> p j g", g=4)
    K.tt(f3, gs3, R["tmp"][:, 16:20].unsqueeze(2).to_broadcast([128, 4, 4]), ALU.is_ge)
    left = R["tmp"][:, 20:24]
    K.ms(left, 1.0)
    for g in range(4):
        K.tt(f3[:, :, g], f3[:, :, g], left, MUL)
        K.tt(left, left, f3[:, :, g], SUB)
    for e in range(4):
        cnt = R["cnt"][:, 16 * e:16 * e + 16]
        n = 0
        for k in range(4):
            if k != e:
                K.tt(tmp if n else cnt, sel[k], sel[e], ALU.is_ge if k < e else ALU.is_gt)
                if n:
                    K.tt(cnt, cnt, tmp, ADD)
                n += 1
        K.stt(e3("kp")[:, :, e], cnt, 1.5, R["f"][:, 0:16], ALU.is_lt, MUL)
    K.tt(R["w"], R["kp"], R["sc"], MUL)
    w3 = R["w"].rearrange("p (j e) -> p j e", e=16)
    K.red(R["tmp"][:, 24:28], w3, ADD)
    K.rec(R["tmp"][:, 28:32], R["tmp"][:, 24:28])
    t = K.tt(w3, w3, R["tmp"][:, 28:32].unsqueeze(2).to_broadcast([128, 4, 16]), MUL)
    cT = K.sb(T)
    tw = t

    def shares():
        b, fr = P.banks(1)
        for j in range(4):
            t2 = K.tr(K.bank(b)[0:16, 128 * j:128 * j + 128], R["w"][:, 16 * j:16 * j + 16], fr, tw)
        tc = K.cp(cT[0:16], K.bank(b)[0:16, :], t2)
        P.free(b, 1, tc)
        return tc

    tsg = [None, None]
    tdown = None
    for half in range(2):
        for e in range(8 * half, 8 * half + 8):
            ts = []
            for f in range(2):
                b, n, t = K.lin3(ws, (xh, x), T, w=tx)
                t = K.act(sg[f], K.bank(b), ACT.Silu, t, tsg[f])
                P.free(b, 1, t)
                b, n, t2 = K.lin3(ws, (xh, x), T)
                ts.append(K.tt(sg[f], sg[f], K.bank(b), MUL, t, t2))
                P.free(b, 1, ts[f])
            if e == 0:
                tc = shares()
            bc_, fr = P.banks(1)
            tcb = K.mm(K.bank(bc_), s16[0:16, e, :], cT[0:16], True, True, fr, tc)
            for f in range(2):
                S = slice((2 * (e % 8) + f) * T, (2 * (e % 8) + f + 1) * T)
                tsg[f] = K.tt(Hl[:, S], sg[f], K.bank(bc_), MUL, tcb, tdown)
                tH = K.split(Hl[:, S], Hh[:, S])
            P.free(bc_, 1, tsg[1])
        per = []
        for k in range(8):
            b, fr = P.banks(1)
            hs, xs = h[:, k * T:k * T + T], x[:, k * T:k * T + T]
            out = lambda j: K.bank(b)
            for g in range(2):
                s = ws.take()
                for kk in range(8):
                    kx = 8 * g + kk
                    t = K.mm3(out, s.hi[:, kk, :], s.ap[:, kk, :], (Hh, Hl), T, kx, kx == 0, kx == 15, s.ready, fr, tH)
                s.done = tdown = t
            if half == 0:
                t = K.cp(hs, K.bank(b), t, eng="act")
            else:
                t = K.tt(hs, hs, K.bank(b), ADD, t)
                K.tt(xs, K.r(xs), K.r(xh[:, k * T:k * T + T]), ADD)
                t = K.stt(hs, xs, ALPHA, hs, MUL, ADD)
                per.append(t)
            P.free(b, 1, t)
    t = K.lnorm(h, p["ln2_g"], p["ln2_b"], x, T, c["eps5"], O, rs, per=per)
    K.phase(mark - 21 * T)
    return x, t


def block3(K, x, x_tok):
    P, c, p, T = K.P, K.c, K.p, T2
    nc = K.nc
    h = K.sb(8 * T)
    y = K.sb(8 * T)
    sq = y
    rs = K.sb(T)
    th = K.rms(x, p["ng3"], h, T, c["eps6"], sq, rs, x_tok)
    small = K.sb(32)
    g8 = {}
    for i, n in enumerate(("foxg", "mobag", "swag")):
        K.ts(small[:, i:i + 1], p[n][:, 0:1], 0.125, None, MUL, None)
        g8[n] = (small[:, i:i + 1], p[n][:, 1:2])

    C4, Cn, Z4 = K.sb(T), K.sb(T), [K.sb(T) for _ in range(3)]
    one4 = K.sb(T)
    K.ms(one4[0:4], 1.0)
    b, n, t = K.lin(h, T, m=4, w=[th])
    logsig(K, C4[0:4], K.ps[0:4, 512 * b:512 * b + T], p["bf"][0:4, 0:1], [z[0:4] for z in Z4], t, b)
    tc = K.scan(Cn[0:4], one4[0:4], C4[0:4])

    vec = [K.sb(640) for _ in range(2)]
    rb = K.sb(128)
    table = [K.sb(512 if i < 4 else 256) for i in range(8)]
    ttab = []
    ttab_pe = []

    def tables():
        for i in range(8):
            v = vec[i % 2]
            moba = i < 4
            trb_ = ttab_pe[-1] if ttab_pe else None
            trb = K.ts(rb[0:32], c["ones"][0:32], p["relb"][0:32, i:i + 1], None, MUL, None, trb_)
            b, fr = P.banks(1)
            t = K.mm(K.bank(b), rb[0:32, 0:128], c["oh"][0:32], True, True, fr, trb)
            ttab_pe.append(t)
            wr = [ttab[-2]] if i >= 2 else []
            if moba:
                K.ms(v[:, 512:640], -1e30, wr)
                t = K.cp(v[:, 0:512], K.bank(b), t)
                W = 640
            else:
                K.ms(v[:, 0:384], -1e30, wr)
                t = K.cp(v[:, 128:256], K.bank(b)[:, 384:512], t)
                W = 384
            P.free(b, 1, t)
            dr = nc.dram_tensor(f"skew{i}", [128 * 640], F32, kind="Internal").ap()
            t = P.dma(dr[0:128 * W].rearrange("(p w) -> p w", w=W), v[:, 0:W], t, eng="pool")
            n = 512 if moba else 256
            rd = dr[127:127 + 128 * (W - 1)].rearrange("(p w) -> p w", w=W - 1)[:, 0:n]
            ttab.append(P.dma(table[i][:, 0:n], rd, t, eng="pool"))
            yield

    bufs = [dict((n, K.sb(w)) for n, w in (
        ("q", T), ("k", T), ("V", T), ("g", T), ("s0", T), ("s1", T), ("P0", T), ("P1", T), ("t0", T), ("t1", T),
        ("sc", 64))) for _ in range(2)]
    vt = K.sb(T)
    old = [None, None]

    now = [None]

    def slab_of():
        s = K.slab(off=now[0][1])
        now[0][1] += 1024
        return s

    def glin():
        s = slab_of()
        b, fr = P.banks(1)
        P.held.add(b)
        for k in range(8):
            t = K.mm(K.bank(b), s.ap[:, k, :], h[:, k * T:k * T + T], k == 0, k == 7, fr, s.tok)
            if k in (1, 3, 5):
                yield
        s.done = t
        P.held.discard(b)
        return b, t

    def qk_tile(d, nme, gain):
        b, t = yield from glin()
        if gain is None:
            t = K.act(d[nme], K.bank(b), ACT.Copy, t, scale=0.125 if nme == "q" else 1.0)
            P.free(b, 1, t)
            return t
        t = K.act(d[nme], K.bank(b), ACT.Copy, t)
        P.free(b, 1, t)
        s0, s1 = (d["s0"], d["s1"]) if nme == "q" else (d["P0"], d["P1"])
        t = K.act(s0, d[nme], ACT.Square)
        yield
        b, n, t = K.colsum(c["oblk"], [s0], T, t)
        K.rstd(s1, b, n, T, 1.0 / 64, c["eps6"], t)
        return K.stt(d[nme], d[nme], gain, s1, MUL, MUL)

    def v_tile(out, fr_tok=None):
        s = slab_of()
        b, fr = P.banks(1)
        P.held.add(b)
        for j in range(4):
            for k in range(8):
                t = K.mm(K.bank(b)[:, 128 * j:128 * j + 128], h[:, k * T + 128 * j:k * T + 128 * j + 128], s.ap[:, k, :],
                         k == 0, k == 7, fr, s.tok)
            if j < 3:
                yield
        s.done = t
        P.held.discard(b)
        t = K.act(out, K.bank(b), ACT.Copy, t, fr_tok)
        P.free(b, 1, t)
        return t

    def gate_tile(d):
        b, t = yield from glin()
        t = K.act(d["g"], K.bank(b), ACT.Silu, t)
        P.free(b, 1, t)
        return t

    def scores(d, kind, r, i, hd, tqk):
        R = slice(64 * r, 64 * r + 64)
        q = d["q"][R, 128 * i:128 * i + 128]
        k0 = max(0, i - 1) if kind == "swa" else 0
        W = 128 * (i + 1 - k0)
        b, fr = P.banks(1)
        s_ = K.bank(b)[:, 0:W]
        t = K.mm(s_, q, d["k"][R, 128 * k0:128 * (i + 1)], True, False, fr, tqk)
        if kind == "fox":
            K.mm(s_, Cn[0:4, 128 * i:128 * i + 128], s16[0:4, hd, 0:1].to_broadcast([4, W]), False, False, tc, tsel)
            K.mm(s_, seln[0:4, 128 * hd:128 * hd + 128], Cn[0:4, 0:W], False, True)
            t = K.mm(s_[:, W - 128:W], c["ident"], c["negm"], False, True, skip=True)
        elif kind == "moba":
            t = K.mm(s_, c["ident"], table[hd][:, 512 - W:512], False, True, ttab[hd])
        else:
            t = K.mm(s_, c["ident"], table[4 + hd][:, 256 - W:256], False, True, ttab[4 + hd])
        sc = d["sc"][:, 32 * r + 8 * i:32 * r + 8 * i + 8]
        Pt = d[f"P{i % 2}"][:, 0:W]
        if kind == "swa":
            K.red(sc[:, 3:4], s_, MAX, t)
            t = K.ts(sc[:, 0:1], sc[:, 3:4], p["sinks"][:, hd:hd + 1], -1.0, MAX, MUL)
        else:
            t = K.red(sc[:, 0:1], s_, MAX, t, neg=True)
        t = K.act(Pt, s_, ACT.Exp, t, bias=sc[:, 0:1], accum=sc[:, 1:2])
        P.free(b, 1, t)
        if kind == "swa":
            t = K.act(sc[:, 4:5], p["sinks"][:, hd:hd + 1], ACT.Exp, bias=sc[:, 0:1])
            K.tt(sc[:, 1:2], sc[:, 1:2], sc[:, 4:5], ADD, t)
        K.rec(sc[:, 2:3], sc[:, 1:2], t)
        return r, i, k0, W, Pt, K.ts(Pt, Pt, sc[:, 2:3], None, MUL, None)

    def values(d, V, vcol, bo, fro, tv, r, i, k0, W, Pt, t):
        b, fr = P.banks(1)
        nb = W // 128
        for j in range(nb):
            t2 = K.tr(K.bank(b)[:, 128 * j:128 * j + 128], Pt[:, 128 * j:128 * j + 128], fr, t)
        a = d[f"t{i % 2}"]
        t3 = K.cp(a[:, 0:W], K.bank(b)[:, 0:W], t2, eng="act")
        P.free(b, 1, t3)
        yield
        for j in range(nb):
            tO = K.mm(K.ps[64 * r:64 * r + 64, 512 * bo + 128 * i:512 * bo + 128 * i + 128],
                      V[:, 128 * (k0 + j) + vcol[r]:128 * (k0 + j) + vcol[r] + 64], a[:, 128 * j:128 * j + 128],
                      j == 0, j == nb - 1, t3, tv, fro)
        return tO

    def softmax_pair(d, kind, V, vcol, hd, tqk, tv, bo, fro):
        behind = None
        for r in range(2):
            for i in range(4):
                cur = scores(d, kind, r, i, hd + r, tqk)
                yield
                if behind:
                    yield from values(d, V, vcol, bo, fro, tv, *behind)
                behind = cur
        return (yield from values(d, V, vcol, bo, fro, tv, *behind))

    seln = K.sb(4 * 128)
    s16 = c["sel16"].rearrange("p (e j) -> p e j", e=16)
    for e in range(4):
        tsel = K.ts(seln[0:4, 128 * e:128 * e + 128], s16[0:4, e, :], -1.0, None, MUL, None)

    def start(i):
        if old[i]:
            P.gate(old[i], ("act", "dve"))
        return bufs[i]

    def out_bank():
        bo, fro = P.banks(1)
        P.held.add(bo)
        return bo, fro

    def finish(i, d, bo, tO, tile, tg):
        t = K.tt(y[:, T * tile:T * tile + T], d["g"], K.bank(bo), MUL, tO, tg)
        P.free(bo, 1, t)
        P.held.discard(bo)
        old[i] = P.marks()
        return t

    def dense():
        for gi, kind in enumerate(("fox", "moba")):
            for pr in range(2):
                d = start(0)
                gq, gk = g8[kind + "g"]
                yield from qk_tile(d, "q", gq)
                yield
                tqk = yield from qk_tile(d, "k", gk)
                yield
                tv = yield from v_tile(d["V"])
                tg = yield from gate_tile(d)
                yield
                bo, fro = out_bank()
                tO = yield from softmax_pair(d, kind, d["V"], (0, 64), 2 * pr, tqk, tv, bo, fro)
                finish(0, d, bo, tO, 2 * gi + pr, tg)

    Lk = [K.sb(T) for _ in range(4)]
    Zk = Z4 + [C4]

    def sticks(pr):
        d = start(1)
        yield from qk_tile(d, "q", None)
        tqk = yield from qk_tile(d, "k", None)
        tv = yield from v_tile(d["V"])
        tg = yield from gate_tile(d)
        yield
        bo, fro = out_bank()
        tdv, tpe = tc, None
        for r in range(2):
            R = slice(64 * r, 64 * r + 64)
            for j in range(4):
                W = 512 - 128 * j
                b, fr = P.banks(1)
                t = K.mm(K.bank(b)[:, 0:W], d["k"][R, 128 * j:128 * j + 128], d["q"][R, 128 * j:512], True, True, fr, tqk)
                z, lk = Zk[j][:, 0:W], Lk[j][:, 0:W]
                s0, s1 = (d["s0"], d["s1"]) if j % 2 == 0 else (d["P0"], d["P1"])
                s0, s1 = s0[:, 0:W], s1[:, 0:W]
                t = K.act(z, K.bank(b)[:, 0:W], ACT.Copy, t, tdv)
                P.free(b, 1, t)
                K.act(s0, z, ACT.Abs, tpe)
                K.act(s0, s0, ACT.Exp, scale=-1.0)
                t = K.act(s0, s0, ACT.Ln, bias=c["one"])
                K.stt(s1, z, 0.0, s0, MAX, ADD, t)
                K.tt(z, z, s1, SUB)
                K.ts(lk, s1, -1.0, None, MUL, None, tpe)
                tl = K.tt(lk[:, 0:128], lk[:, 0:128], c["sup"], MUL)
                if j:
                    tdv = tlast
                tlast = tl
                yield
            for j in range(4):
                W = 512 - 128 * j
                b, fr = P.banks(1)
                t = K.mm(K.bank(b)[:, 0:W], c["slo"], Lk[j][:, 0:W], True, True, fr, tl)
                for j2 in range(j + 1, 4):
                    o = 128 * (j2 - j)
                    t = K.mm(K.bank(b)[:, o:W], c["ones"], Lk[j2][:, 0:W - o], False, True, skip=True)
                a = d[f"P{j % 2}"][:, 0:W]
                t = K.tt(a, Zk[j][:, 0:W], K.bank(b)[:, 0:W], ADD, t)
                P.free(b, 1, t)
                t = K.act(d[f"t{j % 2}"][:, 0:W], a, ACT.Exp, t)
                w0 = d[f"t{j % 2}"]
                t = tdv = K.tt(w0[:, 0:128], w0[:, 0:128], c["sup"], MUL, t)
                yield
                tO = tpe = K.mm(K.ps[R, 512 * bo + 128 * j:512 * bo + 512], d["V"][:, 128 * j + 64 * r:128 * j + 64 * r + 64],
                                w0[:, 0:W], j == 0, True, t, tv, fro, skip=j > 0)
        finish(1, d, bo, tO, 4 + pr, tg)

    def local():
        for pr in range(2):
            yield from sticks(pr)
        tv = yield from v_tile(vt)
        for pr in range(2):
            d = start(1)
            gq, gk = g8["swag"]
            yield from qk_tile(d, "q", gq)
            yield
            tqk = yield from qk_tile(d, "k", gk)
            yield
            tg = yield from gate_tile(d)
            yield
            bo, fro = out_bank()
            tO = yield from softmax_pair(d, "swa", vt, (64 * pr, 64 * pr), 2 * pr, tqk, tv, bo, fro)
            finish(1, d, bo, tO, 6 + pr, tg)

    runs = [[dense(), K.woff], [local(), K.woff + 16 * 1024], [tables(), 0]]
    while runs:
        for r in list(runs):
            now[0] = r
            try:
                next(r[0])
            except StopIteration:
                runs.remove(r)
    K.woff += 31 * 1024
    ty = P.last["dve"]
    for k in range(8):
        b, n, t = K.lin(y, T, w=[ty])
        xs = x[:, k * T:k * T + T]
        t = K.tt(xs, xs, K.bank(b), ADD, t)
        P.free(b, 1, t)
    return x, t


def logsig(K, out, src, bias, tmp, tok, b):
    v, a, e = tmp
    n = v.shape[0]
    t = K.act(v, src, ACT.Identity, tok, bias=bias)
    if b is not None:
        K.P.free(b, 1, t)
    K.act(a, v, ACT.Abs)
    K.act(a, a, ACT.Exp, scale=-1.0)
    t = K.act(a, a, ACT.Ln, bias=K.c["one"][0:n])
    return K.stt(out, v, 0.0, a, MIN, SUB, t)


def layout(inputs):
    I = {k: np.asarray(v) for k, v in inputs.items()}
    x = np.concatenate([I["meta_tokens"], I["x"][0]], 0)
    xT = x.T.reshape(8, 128, T1).transpose(1, 0, 2).reshape(128, 8 * T1)
    con = constants()
    par = pack_params(I)
    return xT, con, par, pack_weights(I)


def program(nc, xT, out, con, par, wall, at, blocks=(1, 2, 3)):
    P = Prog(nc)
    at0 = (nc.sbuf_base + 31) // 32 * 32
    ring = nc.alloc_sbuf_tensor("ring", [128, RING * SLAB], F32)
    assert nc.sbuf_base == at0 + 4 * RING * SLAB
    at1 = nc.sbuf_base
    nfree = (nc.sbuf_bytes_remaining - 64) // 4 // 8 * 8
    arena = nc.alloc_sbuf_tensor("arena", [128, nfree], F32)
    psum = nc.alloc_psum_tensor("psum", [128, 4096], F32)
    c, p = {}, {}
    K = Kern(nc, P, ring, psum, arena, c, p)
    K.at, K.short = {"ring": at0, "arena": at1}, []
    K.alias(ring, SLAB)
    cb, pb = K.sb(at["ncon"]), K.sb(at["npar"])
    loads = [P.dma(cb, con), P.dma(pb, par)]
    for k, (o, n) in at["con"].items():
        c[k] = cb[:, o:o + n]
    for k, (o, n) in at["par"].items():
        p[k] = pb[:, o:o + n]
    eps = K.sb(8)
    for i, (k, v) in enumerate((("eps5", 1e-5), ("eps6", 1e-6), ("epsgn", 64e-5), ("one", 1.0))):
        c[k] = eps[:, i:i + 1]
        K.ms(c[k], v)
    P.gate(P.marks() + loads)
    base = K.top
    x, t = None, None
    if 1 in blocks:
        x, t = block1(K, xT)
    else:
        x = K.sb(4096)
        t = P.dma(x, xT)
    if 2 in blocks:
        x, t = block2(K, x, t)
    if 3 in blocks:
        x, t = block3(K, x, t)
    P.dma(out, x, t)
    with nc.Block() as block:
        P.emit(wall, ring, block)


def offsets(d):
    off, at = 0, {}
    for k, v in d.items():
        at[k] = (off, v.shape[1])
        off += v.shape[1]
    return at, off


def kernel(**inputs):
    import concourse.bacc as bacc
    from concourse.bass_utils import run_bass_kernel_spmd as run

    xT, con, par, w = layout(inputs)
    at = {}
    at["con"], at["ncon"] = offsets(con)
    at["par"], at["npar"] = offsets(par)
    arrays = {
        "in_x": np.ascontiguousarray(xT, np.float32),
        "in_con": np.ascontiguousarray(np.concatenate(list(con.values()), 1)),
        "in_par": np.ascontiguousarray(np.concatenate(list(par.values()), 1)),
        "in_w": np.concatenate(w, 1),
    }
    nc = bacc.Bacc("TRN2", target_bir_lowering=False, num_devices=1)
    d = {k: nc.dram_tensor(k, list(v.shape), F32, kind="ExternalInput").ap() for k, v in arrays.items()}
    out = nc.dram_tensor("out_0", [128, 8 * 512], F32, kind="ExternalOutput").ap()
    program(nc, d["in_x"], out, d["in_con"], d["in_par"], d["in_w"], at)
    r = run(nc, [arrays], core_ids=[0])
    o = np.asarray(r.results[0]["out_0"]).reshape(128, 8, 512).transpose(1, 0, 2).reshape(1024, 512)
    return np.ascontiguousarray(o.T).reshape(1, 512, 1024)
```
